# Optimizing a Trainium2 kernel written in Bass

```python
import math
import jax
import jax.numpy as jnp
from jax import lax
import numpy as np

D_MODEL = 1024
BATCH = 1
SEQ = 512
DEPTH = 2

GRID_W = 64
CTX_LEN = 256
N_EVEN = (DEPTH + 1) // 2
N_ODD = DEPTH // 2
MIX_WIDTH = D_MODEL
HGRN_WIDTH = MIX_WIDTH // 2
HGRN_HEAD_DIM = 128
HGRN_HEADS = HGRN_WIDTH // HGRN_HEAD_DIM
CHUNK = 64
DIFF_WIDTH = MIX_WIDTH - HGRN_WIDTH
DIFF_HEAD_DIM = 64
DIFF_HEADS = DIFF_WIDTH // (2 * DIFF_HEAD_DIM)
Q_BLOCK = 128
ROPE_THETA = 10000.0
EVEN_IN = 5 * HGRN_WIDTH + 3 * DIFF_WIDTH
CONV_WIDTH = 3
N_EXPERTS = 16
EXPERT_FF = 1024
EC_CAPACITY = 2
MOD_CHUNKS = 6
EPS = 1e-6

kernel_name = "hybrid_hgrn2_diffattn_shortconv_ecmoe_dit"

def rmsnorm(x, g):
    xf = x.astype(jnp.float32)
    y = xf * lax.rsqrt(jnp.mean(xf * xf, axis=-1, keepdims=True) + EPS)
    return y.astype(x.dtype) * g

def modulate(h, shift, scale):
    return h * (1 + scale) + shift

def lambda_init(layer):
    return 0.8 - 0.6 * math.exp(-0.3 * layer)

def _heads(a, n_heads):
    B, T, W = a.shape
    return a.reshape(B, T, n_heads, W // n_heads).transpose(0, 2, 1, 3)

def _rope_axis(x, pos):
    n = x.shape[-1]
    inv = 1.0 / (ROPE_THETA ** (jnp.arange(0, n, 2, dtype=jnp.float32) / n))
    ang = pos.astype(jnp.float32)[:, None] * inv[None, :]
    cos, sin = jnp.cos(ang).astype(x.dtype), jnp.sin(ang).astype(x.dtype)
    x1, x2 = x[..., : n // 2], x[..., n // 2:]
    return jnp.concatenate([x1 * cos - x2 * sin, x2 * cos + x1 * sin], axis=-1)

def rope_2d(x):
    T = x.shape[-2]
    n_rows = T // GRID_W
    rows = jnp.repeat(jnp.arange(n_rows), GRID_W)
    cols = jnp.tile(jnp.arange(GRID_W), n_rows)
    half = x.shape[-1] // 2
    return jnp.concatenate([_rope_axis(x[..., :half], rows), _rope_axis(x[..., half:], cols)], axis=-1)

def gla_chunk_scan(q, k, v, log_f, s0, with_output=True):
    B, H, T, dk = q.shape
    dv = v.shape[-1]
    n_chunks = T // CHUNK

    def to_chunks(a):
        return jnp.moveaxis(a.reshape(B, H, n_chunks, CHUNK, a.shape[-1]), 2, 0)

    lower = jnp.tril(jnp.ones((CHUNK, CHUNK), dtype=bool))[:, :, None]

    def step(s, inp):
        qi, ki, vi, gi = inp
        b = jnp.cumsum(gi, axis=2)
        b_last = b[:, :, -1:, :]
        s_new = (jnp.exp(b_last)[:, :, 0, :, None] * s
                 + jnp.einsum('bhsd,bhse->bhde', ki * jnp.exp(b_last - b), vi))
        if not with_output:
            return s_new, None
        rel = b[:, :, :, None, :] - b[:, :, None, :, :]
        decay = jnp.where(lower, jnp.exp(jnp.where(lower, rel, 0.0)), 0.0)
        scores = jnp.einsum('bhtd,bhtsd,bhsd->bhts', qi, decay, ki)
        o = (jnp.einsum('bhld,bhde->bhle', qi * jnp.exp(b), s)
             + jnp.einsum('bhts,bhse->bhte', scores, vi))
        return s_new, o

    s_final, oc = lax.scan(step, s0, tuple(to_chunks(a) for a in (q, k, v, log_f)))
    if not with_output:
        return None, s_final
    return jnp.moveaxis(oc, 0, 2).reshape(B, H, T, dv), s_final

def hgrn2_direction(q, z, v, lb, qc, zc, vc, reverse, ctx_out):
    def prep(qq, zz, vv):
        zf = zz.astype(jnp.float32)
        log_f = jnp.log(lb + (1 - lb) * jax.nn.sigmoid(zf))
        key = (1 - lb) * jax.nn.sigmoid(-zf)
        arrs = [_heads(a, HGRN_HEADS) for a in (qq.astype(jnp.float32), key, vv.astype(jnp.float32), log_f)]
        return [jnp.flip(a, axis=2) for a in arrs] if reverse else arrs

    B = q.shape[0]
    s0 = jnp.zeros((B, HGRN_HEADS, HGRN_HEAD_DIM, HGRN_HEAD_DIM), jnp.float32)
    oc, s_ctx = gla_chunk_scan(*prep(qc, zc, vc), s0, with_output=ctx_out)
    o, _ = gla_chunk_scan(*prep(q, z, v), s_ctx)
    if reverse:
        o = jnp.flip(o, axis=2)
        oc = jnp.flip(oc, axis=2) if ctx_out else None
    return o, oc

def hgrn2_readout(o, gate, g):
    B, H, T, dv = o.shape
    o = rmsnorm(o, g[:, None, :]).transpose(0, 2, 1, 3).reshape(B, T, H * dv)
    return o.astype(gate.dtype) * jax.nn.silu(gate)

def qk_heads(a, g, rotary):
    B, T, _ = a.shape
    a = rmsnorm(a.reshape(B, T, DIFF_HEADS, 2, DIFF_HEAD_DIM).transpose(0, 2, 3, 1, 4), g)
    return rope_2d(a) if rotary else a

def diff_attend(q, k, v, lam):
    s = jnp.einsum('bhmqd,bhmkd->bhmqk', q, k).astype(jnp.float32)
    p = jax.nn.softmax(s, axis=-1)
    w = p[:, :, 0] - lam * p[:, :, 1]
    return jnp.einsum('bhqk,bhke->bhqe', w.astype(v.dtype), v)

def blocked_diff_attention(q, k_all, v_all, lam):
    B, H, _, T, dh = q.shape
    nb = T // Q_BLOCK
    qb = jnp.moveaxis(q.reshape(B, H, 2, nb, Q_BLOCK, dh), 3, 0)
    ob = lax.map(lambda qi: diff_attend(qi, k_all, v_all, lam), qb)
    return jnp.moveaxis(ob, 0, 2).reshape(B, H, T, 2 * DIFF_HEAD_DIM)

def diff_readout(o, g, lam_init):
    B, H, T, e = o.shape
    o = rmsnorm(o, g) * (1 - lam_init)
    return o.transpose(0, 2, 1, 3).reshape(B, T, H * e)

def even_mixer(h, hc, w_in, w_out, lb, hgrn_g, qn_g, kn_g, lam_vec, subln_g, lam_init, ctx_out):
    cuts = [HGRN_WIDTH * i for i in range(1, 6)] + [5 * HGRN_WIDTH + DIFF_WIDTH * i for i in range(1, 3)]
    hq, hzf, hzb, hv, hgate, dq, dk, dv = jnp.split(h @ w_in, cuts, axis=-1)
    cq, czf, czb, cv, cgate, cdq, cdk, cdv = jnp.split(hc @ w_in, cuts, axis=-1)
    o_f, oc_f = hgrn2_direction(hq, hzf, hv, lb[0], cq, czf, cv, False, ctx_out)
    o_b, oc_b = hgrn2_direction(hq, hzb, hv, lb[1], cq, czb, cv, True, ctx_out)
    y_h = hgrn2_readout(o_f + o_b, hgate, hgrn_g)
    lv = lam_vec.astype(jnp.float32)
    lam = jnp.exp(jnp.sum(lv[0] * lv[1])) - jnp.exp(jnp.sum(lv[2] * lv[3])) + lam_init
    scale = DIFF_HEAD_DIM ** -0.5
    q = qk_heads(dq, qn_g, True) * scale
    k = qk_heads(dk, kn_g, True)
    kc = qk_heads(cdk, kn_g, False)
    v, vc = _heads(dv, DIFF_HEADS), _heads(cdv, DIFF_HEADS)
    k_all = jnp.concatenate([k, kc], axis=3)
    v_all = jnp.concatenate([v, vc], axis=2)
    y_d = diff_readout(blocked_diff_attention(q, k_all, v_all, lam), subln_g, lam_init)
    y = jnp.concatenate([y_h, y_d], axis=-1) @ w_out
    if not ctx_out:
        return y, None
    yc_h = hgrn2_readout(oc_f + oc_b, cgate, hgrn_g)
    qc = qk_heads(cdq, qn_g, False) * scale
    yc_d = diff_readout(diff_attend(qc, kc, vc, lam), subln_g, lam_init)
    yc = jnp.concatenate([yc_h, yc_d], axis=-1) @ w_out
    return y, yc

def short_conv_mixer(h, w_in, conv_w, w_out):
    b_gate, c_gate, v = jnp.split(h @ w_in, 3, axis=-1)
    u = c_gate * v
    y = lax.conv_general_dilated(u, conv_w[:, None, :].astype(u.dtype), window_strides=(1,),
                                 padding=((CONV_WIDTH // 2, CONV_WIDTH // 2),),
                                 dimension_numbers=('NWC', 'WIO', 'NWC'),
                                 feature_group_count=u.shape[-1])
    return (b_gate * y) @ w_out

def expert_choice_ffn(h, router_w, w_gate, w_up, w_down):
    B, N, D = h.shape
    cap = EC_CAPACITY * N // N_EXPERTS
    affinity = jax.nn.softmax((h @ router_w).astype(jnp.float32), axis=-1)
    gate, idx = lax.top_k(jnp.swapaxes(affinity, 1, 2), cap)
    idx_flat = idx.reshape(B, N_EXPERTS * cap)
    xe = jax.vmap(lambda hb, ib: hb[ib])(h, idx_flat).reshape(B, N_EXPERTS, cap, D)
    a = jnp.einsum('becd,edf->becf', xe, w_gate)
    u = jnp.einsum('becd,edf->becf', xe, w_up)
    ye = jnp.einsum('becf,efd->becd', jax.nn.silu(a) * u, w_down) * gate[..., None].astype(h.dtype)
    return jax.vmap(lambda yb, ib: jnp.zeros((N, D), h.dtype).at[ib].add(yb))(
        ye.reshape(B, N_EXPERTS * cap, D), idx_flat)

def setup_inputs(seed: int = 0) -> dict:
    key = jax.random.key(seed)
    ks = jax.random.split(key, 24)
    D = D_MODEL

    def nrm(k, shape, scale):
        return jax.random.normal(k, shape, jnp.float32) * scale

    return {
        "x": nrm(ks[0], (BATCH, SEQ, D), 1.0),
        "c": nrm(ks[1], (BATCH, D), 1.0),
        "ctx": nrm(ks[2], (BATCH, CTX_LEN, D), 1.0),
        "c_ctx": nrm(ks[3], (D,), 1.0),
        "mod_w": nrm(ks[4], (DEPTH, D, MOD_CHUNKS * D), 0.3 * D ** -0.5),
        "mod_b": nrm(ks[5], (DEPTH, MOD_CHUNKS * D), 0.02),
        "norm1_g": 1.0 + nrm(ks[6], (DEPTH, D), 0.02),
        "norm2_g": 1.0 + nrm(ks[7], (DEPTH, D), 0.02),
        "even_w_in": nrm(ks[8], (N_EVEN, D, EVEN_IN), D ** -0.5),
        "even_w_out": nrm(ks[9], (N_EVEN, MIX_WIDTH, D), MIX_WIDTH ** -0.5),
        "hgrn_lb_logits": nrm(ks[10], (N_EVEN, 2, HGRN_WIDTH), 1.0),
        "hgrn_norm_g": 1.0 + nrm(ks[11], (N_EVEN, HGRN_HEADS, HGRN_HEAD_DIM), 0.02),
        "diff_qnorm_g": 1.0 + nrm(ks[12], (N_EVEN, DIFF_HEAD_DIM), 0.02),
        "diff_knorm_g": 1.0 + nrm(ks[13], (N_EVEN, DIFF_HEAD_DIM), 0.02),
        "diff_lambda": nrm(ks[14], (N_EVEN, 4, DIFF_HEAD_DIM), 0.1),
        "diff_subln_g": 1.0 + nrm(ks[15], (N_EVEN, 2 * DIFF_HEAD_DIM), 0.02),
        "conv_w_in": nrm(ks[16], (N_ODD, D, 3 * D), D ** -0.5),
        "conv_w": nrm(ks[17], (N_ODD, CONV_WIDTH, D), CONV_WIDTH ** -0.5),
        "conv_w_out": nrm(ks[18], (N_ODD, D, D), D ** -0.5),
        "router_w": nrm(ks[19], (DEPTH, D, N_EXPERTS), D ** -0.5),
        "exp_w_gate": nrm(ks[20], (DEPTH, N_EXPERTS, D, EXPERT_FF), D ** -0.5),
        "exp_w_up": nrm(ks[21], (DEPTH, N_EXPERTS, D, EXPERT_FF), D ** -0.5),
        "exp_w_down": nrm(ks[22], (DEPTH, N_EXPERTS, EXPERT_FF, D), EXPERT_FF ** -0.5),
    }

def reference(x, c, ctx, c_ctx, mod_w, mod_b, norm1_g, norm2_g, even_w_in, even_w_out,
              hgrn_lb_logits, hgrn_norm_g, diff_qnorm_g, diff_knorm_g, diff_lambda, diff_subln_g,
              conv_w_in, conv_w, conv_w_out, router_w, exp_w_gate, exp_w_up, exp_w_down):
    lb_soft = jax.nn.softmax(hgrn_lb_logits.astype(jnp.float32), axis=0)
    lower_bounds = jnp.cumsum(lb_soft, axis=0) - lb_soft[:1]
    last_ctx_layer = 2 * ((DEPTH - 1) // 2)
    silu_c = jax.nn.silu(c)
    silu_cc = jax.nn.silu(c_ctx)
    xc = ctx
    for l in range(DEPTH):
        read_ctx = l <= last_ctx_layer
        ctx_out = l < last_ctx_layer
        sh1, sc1, g1, sh2, sc2, g2 = jnp.split((silu_c @ mod_w[l] + mod_b[l])[:, None, :], MOD_CHUNKS, axis=-1)
        h = modulate(rmsnorm(x, norm1_g[l]), sh1, sc1)
        if read_ctx:
            csh1, csc1, cg1, csh2, csc2, cg2 = jnp.split(silu_cc @ mod_w[l] + mod_b[l], MOD_CHUNKS, axis=-1)
            hc = modulate(rmsnorm(xc, norm1_g[l]), csh1, csc1)
        if l % 2 == 0:
            e = l // 2
            y, yc = even_mixer(h, hc, even_w_in[e], even_w_out[e], lower_bounds[e], hgrn_norm_g[e],
                               diff_qnorm_g[e], diff_knorm_g[e], diff_lambda[e], diff_subln_g[e],
                               lambda_init(l), ctx_out)
        else:
            j = l // 2
            y = short_conv_mixer(h, conv_w_in[j], conv_w[j], conv_w_out[j])
            yc = short_conv_mixer(hc, conv_w_in[j], conv_w[j], conv_w_out[j]) if ctx_out else None
        x = x + g1 * y
        x = x + g2 * expert_choice_ffn(modulate(rmsnorm(x, norm2_g[l]), sh2, sc2),
                                       router_w[l], exp_w_gate[l], exp_w_up[l], exp_w_down[l])
        if ctx_out:
            xc = xc + cg1 * yc
            xc = xc + cg2 * expert_choice_ffn(modulate(rmsnorm(xc, norm2_g[l]), csh2, csc2),
                                              router_w[l], exp_w_gate[l], exp_w_up[l], exp_w_down[l])
    return x


_drawn_inputs = setup_inputs


def setup_inputs(seed=0):
    import zlib

    import numpy as np

    out = dict(_drawn_inputs(seed))
    spreads = {}
    factors = {'norm1_g': 6.795,
     'norm2_g': 8.0,
     'hgrn_norm_g': 8.0,
     'diff_qnorm_g': 8.0,
     'diff_knorm_g': 8.0,
     'diff_lambda': 6.274,
     'diff_subln_g': 31.417}
    for name, (base, spread) in spreads.items():
        noise = np.random.default_rng([zlib.crc32(name.encode()), seed]).standard_normal(out[name].shape)
        drawn = base * np.exp(spread * noise) if base else spread * noise
        out[name] = jnp.asarray(drawn.astype(out[name].dtype))
    for name, factor in factors.items():
        out[name] = (out[name] * factor).astype(out[name].dtype)
    return out
```

```python
from contextlib import ExitStack
import math

import numpy as np

import concourse.bass as bass
from concourse import mybir

P = 128
D = 1024
T = 512
TC = 256
KT = D // P
TT = T // P
CT = TC // P
GRID_W = 64
HH = 4
HD = 128
AH = 4
AD = 64
CH = 128
NC = T // CH
LEVELS = 7
E = 16
CAP = 2 * T // E
EPS = 1e-6
LAM_INIT = 0.8 - 0.6 * math.exp(0.0)
ROPE_THETA = 10000.0
SLOTS = 3

F32 = mybir.dt.float32
U8 = mybir.dt.uint8
ALU = mybir.AluOpType
ACT = mybir.ActivationFunctionType
AX = mybir.AxisListType.X

KB = 256


class Job:

    def __init__(self, lead, banks, count, owners):
        self.lead, self.banks, self.count, self.owners = lead, banks, count, owners


class BankPlan:

    def __init__(self):
        self.used = [0] * 8
        self.owner = [None] * 8

    def job(self, *banks):
        lead = banks[0]
        self.used[lead] += 1
        owners = []
        for b in banks:
            if self.owner[b] is not None and self.owner[b] not in owners:
                owners.append(self.owner[b])
        j = Job(lead, banks, self.used[lead], owners)
        for b in banks:
            self.owner[b] = j
        return j

    def loop(self, per, leads, times):
        base = list(self.used)
        for b in range(8):
            self.used[b] += per[b] * times
        for b in range(8):
            self.owner[b] = Job(leads[b], (b,), self.used[leads[b]], [])
        return base


class Chain:

    def __init__(self, eng, sem):
        self.eng, self.sem, self.n, self.base, self.turn, self.per = eng, sem, 0, 0, None, 0

    def __call__(self, ins):
        self.n += 1
        ins.then_inc(self.sem, 1)
        if self.turn is None:
            self.eng.wait_ge(self.sem, self.n)
        else:
            self.eng.wait_ge(self.sem, self.turn * self.per + self.n)

    def enter(self, turn, per):
        self.base, self.turn, self.per = self.n, turn, per

    def leave(self, times):
        assert self.n - self.base == self.per, (self.n - self.base, self.per)
        self.n = self.base + self.per * times
        self.turn = None


def build(nc, a, out, stop=None, tap=None):
    bp = BankPlan()
    J = {}
    J["colsA"] = bp.job(0)
    J["colsB"] = bp.job(1)
    mods0 = [(0, 0), (0, 1)]
    mods1 = [(0, j) for j in range(2, 6)] + [(1, j) for j in range(6)]
    def mod_jobs(m, half, b):
        J["modr", m, half] = bp.job(b)
        J["modc", m, half] = bp.job(b)

    for m in mods0:
        for half in range(2):
            mod_jobs(m, half, 2 + half)
    for kt in range(KT):
        J["hT", kt] = bp.job([4, 5, 6, 7][kt % 4])
    for kt in range(KT):
        J["hcT", kt] = bp.job([4, 5, 6, 7][kt % 4])
    n = 0
    for t in range(TT + CT):
        J["dk", t] = bp.job(n % 4); n += 1
    for t in range(TT + CT):
        J["dv", t] = bp.job(n % 4); n += 1
    for h in range(HH):
        J["gate", h] = bp.job(n % 4); n += 1
    for t in range(TT):
        J["dq", t] = bp.job(n % 4); n += 1
    for h in range(AH):
        J["qT", h] = bp.job(6)
        J["kT", h] = bp.job(4, 5)
    att = [(h, t) for h in range(AH) for t in range(TT)]
    def score_jobs(h, t):
        J["s0", h, t] = bp.job(0, 1)
        J["s1", h, t] = bp.job(2, 3)

    score_jobs(0, 0)
    for n, (h, t) in enumerate(att):
        if n + 1 < len(att):
            score_jobs(*att[n + 1])
        J["wT", h, t] = bp.job(4, 5)
        J["o", h, t] = bp.job(6)
    for h in range(AH):
        J["oT", h] = bp.job(h)
    n = 0
    for t in range(TT + CT):
        J["hv", t] = bp.job(n % 4); n += 1
    for d in (1, 0):
        for h in range(HH):
            J["zc", d, h] = bp.job(n % 4); n += 1
        for h in range(HH):
            J["z", d, h] = bp.job(n % 4); n += 1
        if d == 0:
            for h in range(HH):
                J["hq", h] = bp.job(n % 4); n += 1
    halves = [(m, half) for m in mods1 for half in range(2)]
    fills = {}
    for n in range(2 * HH):
        for L in (0, 3, 6)[:3 - n % 2]:
            fills[n, L] = halves.pop(0)
    assert not halves
    for n, (d, h) in enumerate([(d, h) for d in (1, 0) for h in range(HH)]):
            J["kcT", d, h] = bp.job(4)
            J["s0c", d, h] = bp.job(5)
            for L in range(LEVELS + 1):
                if (n, L) in fills:
                    mod_jobs(*fills[n, L], 7)
                J["sc", d, h, L] = bp.job(L % 4)
            J["kdT", d, h] = bp.job(4)
            J["ho", d, h] = bp.job(6)
            for c in range(NC - 1):
                J["kv", d, h, c] = bp.job(5)
    for h in range(HH):
        J["ssq", h] = bp.job(h)

    def out_jobs(l):
        J["grow", l] = bp.job(4, 5)
        for t in range(TT):
            for half in range(2):
                J["y", l, t, half] = bp.job((2 * t + half) % 4)

    LOOP_PER = [2, 0, 1, 0, 2, 2, 5, 4]
    LOOP_LEAD = [0, 0, 2, 2, 4, 5, 6, 7]
    loop_base = {}

    def moe_jobs(l):
        for kt in range(KT):
            J["h2T", l, kt] = bp.job(kt)
        J["logit", l] = bp.job(0)
        J["affT", l] = bp.job(1)
        J["slotT", l] = bp.job(2)
        J["grow2", l] = bp.job(6, 7)
        loop_base[l] = bp.loop(LOOP_PER, LOOP_LEAD, E // 2)

    out_jobs(0)
    moe_jobs(0)
    for kt in range(KT):
        J["h3T", kt] = bp.job(kt)
    n = 0
    for part in "bcv":
        for f in range(KT):
            J["conv", part, f] = bp.job(n % 8); n += 1
    out_jobs(1)
    moe_jobs(1)

    def w_in(j):
        return a["even_w_in"][0][:, j * D:(j + 1) * D]

    chunks = {}
    stream = []
    slot_last = {}
    slot_used = [0] * SLOTS

    def chunk(name, slot, src, last_job):
        slot_used[slot] += 1
        chunks[name] = (slot, slot_used[slot])
        stream.append((slot, src, slot_last.get(slot), name))
        slot_last[slot] = last_job

    n = 0
    for m in mods0:
        chunk(("mod", m), (n + 1) % 2, a["mod_w"][m[0]][:, m[1] * D:(m[1] + 1) * D], J["modr", m, 1]); n += 1
    chunk("w3", (n + 1) % 2, w_in(3), J["dv", TT + CT - 1]); n += 1
    chunk("w2", (n + 1) % 2, w_in(2), J["dq", TT - 1]); n += 1
    chunk("w1", (n + 1) % 2, w_in(1), J["z", 1, HH - 1]); n += 1
    chunk("w0", (n + 1) % 2, w_in(0), J["hq", HH - 1]); n += 1
    for m in mods1:
        chunk(("mod", m), (n + 1) % 2, a["mod_w"][m[0]][:, m[1] * D:(m[1] + 1) * D], J["modr", m, 1]); n += 1
    chunk("wo", (n + 1) % 2, a["even_w_out"][0], J["y", 0, TT - 1, 1]); n += 1
    assert chunks["wo"][0] == 1
    head0 = list(stream)
    stream.clear()
    exp_base = {}

    def experts(l):
        exp_base[l] = list(slot_used)
        first = [slot_last.get(s) for s in range(3)]
        b = loop_base[l]
        for s in range(3):
            slot_used[s] += E
        slot_last[0] = Job(2, (2,), b[2] + LOOP_PER[2] * E // 2, [])
        slot_last[1] = slot_last[2] = Job(0, (0,), b[0] + LOOP_PER[0] * E // 2, [])
        return first

    first0 = experts(0)
    chunk("cb", 1, a["conv_w_in"][0][:, 0:D], J["conv", "b", KT - 1])
    chunk("cc", 2, a["conv_w_in"][0][:, D:2 * D], J["conv", "c", KT - 1])
    chunk("cv", 0, a["conv_w_in"][0][:, 2 * D:3 * D], J["conv", "v", KT - 1])
    chunk("co", 1, a["conv_w_out"][0], J["y", 1, TT - 1, 1])
    head1 = list(stream)
    first1 = experts(1)

    with ExitStack() as ctx:
        def sb(name, shape, dt=F32):
            return ctx.enter_context(nc.sbuf_tensor(name, shape, dt))

        def sem(name):
            return ctx.enter_context(nc.semaphore(name))

        ring = sb("ring", [P, SLOTS, KT, D])
        annex = ring[:, 2, :, :].rearrange("p k n -> p (k n)")
        room = sb("room", [P, 92 * KB])
        ident = sb("ident", [P, P])
        rope_cos = sb("rope_cos", [P, TT, AD])
        rope_sin = sb("rope_sin", [P, TT, AD])
        iota = sb("iota", [P, CAP])
        masks = sb("masks", [P, 2, LEVELS + 1, CH], U8)
        ones = sb("ones", [P, TC])
        reset = sb("reset", [P, 2, T])
        rowsA = room[:, 60 * KB:60 * KB + P]
        rowsB = room[:, 61 * KB:61 * KB + P]
        colsA = sb("colsA", [P, P])
        colsB = sb("colsB", [P, 96])
        silc = sb("silc", [P, KT, 2])
        modc = sb("modc", [P, 2, 6, KT])
        modx = sb("modx", [P, 2, KT])
        scaleA = sb("scaleA", [P, 5, KT])
        grow = sb("grow", [P, D])
        small = sb("small", [P, 256])
        gains = sb("gains", [P, AD + AD + 2 * AD])
        lamv = sb("lamv", [P, 4 * AD])
        slotc = sb("slotc", [P, TT, E])
        aff = sb("aff", [P, TT, E])
        router = room[:, 75 * KB:75 * KB + KT * E].rearrange("p (k e) -> p k e", k=KT)

        def view(at_kb, *shape, base=None):
            base = room if base is None else base
            size = 1
            for s in shape:
                size *= s
            v = base[:, int(at_kb * KB):int(at_kb * KB) + size]
            if len(shape) == 1:
                return v
            names = "abcd"[:len(shape)]
            spec = "p (" + " ".join(names) + ") -> p " + " ".join(names)
            return v.rearrange(spec, **{k: s for k, s in zip(names[:-1], shape[:-1])})

        xs = view(0, TT, D)
        xn = view(16, TT, D)
        x6 = view(16, TT + CT, D)
        hT = view(76, KT, T)
        hcT = view(68, KT, TC)
        yT = view(52, KT, T)
        qtok = view(0, TT, T)
        ktok = view(8, TT + CT, T)
        vtok = view(20, TT + CT, T)
        qT = view(32, AH, T)
        kT = view(40, AH, T + TC)
        prob = view(0, 2, 2, T + TC)
        wgt = view(12, T + TC)
        wT = view(15, CT + TT, P)
        oall = view(16, TT, T, base=annex)
        junk = view(0, D, base=annex)
        tsq = view(4, 2, T, base=annex)
        trot = view(8, 2, T, base=annex)
        ta = view(12, T, base=annex)
        hv = view(0, TT + CT, T)
        hq = view(12, HH, T)
        hb = [view(20, HH, T), view(36, HH, T)]
        hk = [view(28, HH, T), view(44, HH, T)]
        ho = view(0, HH, T, base=annex)
        cb = [view(8, HH, TC, base=annex), view(16, HH, TC, base=annex)]
        ck = [view(12, HH, TC, base=annex), view(20, HH, TC, base=annex)]
        spl = view(24, 2, T, base=annex)
        lvE = view(68, 2, T)
        lvQ = view(72, 2, T)
        lvK = view(76, 2, T)
        qdec = view(80, T)
        kdec = view(82, T)
        kdtok = view(84, NC, P)
        sc = view(86, T)
        state = view(88, 2, P)
        masks_in = view(16, 2 * (LEVELS + 1) * CH, base=annex)
        modrow = view(28, D, base=annex)[0:2]
        kcdec = view(24, TC, base=annex)
        kcdtok = view(25, CT, P, base=annex)
        sq = view(36, HH, T)
        root_h = view(44, HH, T)
        h2T = view(76, KT, T)
        sel = view(41, 4, T)
        onehot = view(49, TT, 2, CAP)
        gated = view(51, TT, 2, CAP)
        spread = view(53, T)
        xe = view(55, KT, P)
        sil = view(59, D)
        actb = view(32, D)
        actT = view(63, KT, P)
        ye = view(67, D)
        junk_moe = view(36, D)
        xtmp = view(70, 2, T)
        bT = view(16, KT, T)
        cT = view(32, KT, T)
        uT = view(48, T + 2)
        vT = view(51, T)
        ycT = view(54, KT, T)

        ps = ctx.enter_context(nc.psum_tensor("ps", [P, 8, 512], F32))
        psf = ps[:, :, :].rearrange("p b n -> p (b n)")

        def bank(b, n=512):
            return ps[:, b, 0:n]

        full = [sem(f"bank_full{b}") for b in range(8)]
        free = [sem(f"bank_free{b}") for b in range(8)]
        ring_full = [sem(f"ring_full{s}") for s in range(SLOTS)]
        consts_in = sem("consts_in")
        rows_in = sem("rows_in")
        x_in = sem("x_in")
        x_again = sem("x_again")
        router_in = [sem("router_in0"), sem("router_in1")]
        cols_ready = sem("cols_ready")
        silc_ready = sem("silc_ready")
        squares_ready = sem("squares_ready")
        means_ready = sem("means_ready")
        roots_ready = sem("roots_ready")
        xn_ready = sem("xn_ready")
        scale_ready = sem("scale_ready")
        act_step = sem("act_step")
        dve_step = sem("dve_step")
        lam_dots = sem("lam_dots")
        lam_exps = sem("lam_exps")
        qk_squares = sem("qk_squares")
        qk_means = sem("qk_means")
        qk_roots = sem("qk_roots")
        qk_normed = sem("qk_normed")
        max_ready = sem("max_ready")
        wgt_ready = sem("wgt_ready")
        o_squares = sem("o_squares")
        o_means = sem("o_means")
        o_roots = sem("o_roots")
        o_normed = sem("o_normed")
        log_ready = sem("log_ready")
        hk_ready = sem("hk_ready")
        b_ready = sem("b_ready")
        cdec_ready = sem("cdec_ready")
        kcd_ready = sem("kcd_ready")
        diff_ready = sem("diff_ready")
        decay_ready = sem("decay_ready")
        lv_ready = sem("lv_ready")
        ends_ready = sem("ends_ready")
        qdec_ready = sem("qdec_ready")
        sq_ready = sem("sq_ready")
        y_hgrn = sem("y_hgrn")
        hroot_out = sem("hroot_out")
        x_ready = sem("x_ready")
        logit_exp = sem("logit_exp")
        aff_ready = sem("aff_ready")
        slot_ready = sem("slot_ready")
        onehot_ready = sem("onehot_ready")
        gated_ready = sem("gated_ready")
        gate0_used = sem("gate0_used")
        up0_used = sem("up0_used")
        down0_used = sem("down0_used")
        ycT_ready = sem("ycT_ready")
        out_done = sem("out_done")

        stops = ["A", "B", "C", "D", "M0", "X"]
        upto = stops.index(stop) if stop else 99

        locals_of_build = locals()
        block = ctx.enter_context(nc.Block())

        @block.sync
        def _(sp):
            def load_chunk(slot, src, owner):
                if owner is not None:
                    sp.wait_ge(full[owner.lead], owner.count)
                sp.dma_start(ring[:, slot], src.rearrange("(k p) n -> p k n", p=P)).then_inc(ring_full[slot], 16)

            for dst, src in ((ident, "c_ident"), (rope_cos, "c_cos"), (rope_sin, "c_sin"),
                             (iota, "c_iota"), (masks_in, "c_masks")):
                sp.dma_start(dst if dst is masks_in else dst[:], a[src]).then_inc(consts_in, 16)
            rows = [(0, a["c"].rearrange("b (k p) -> (b k) p", p=P)),
                    (8, a["c_ctx"].rearrange("(k p) -> k p", p=P)),
                    (16, a["norm1_g"].rearrange("l (k p) -> (l k) p", p=P)),
                    (32, a["norm2_g"].rearrange("l (k p) -> (l k) p", p=P)),
                    (48, a["hgrn_norm_g"][0]),
                    (52, a["conv_w"][0].rearrange("w (k p) -> (w k) p", p=P))]
            for at, src in rows:
                sp.dma_start(rowsA[at:at + src.shape[0], :], src).then_inc(rows_in, 16)
            sp.dma_start(rowsB[0:96, :], a["mod_b"].rearrange("l (k p) -> (l k) p", p=P)).then_inc(rows_in, 16)
            for t in range(CT):
                sp.dma_start(x6[:, TT + t], a["ctx"][0, t * P:(t + 1) * P, :]).then_inc(x_in, 16)
            for t in range(TT):
                sp.dma_start(x6[:, t], a["x"][0, t * P:(t + 1) * P, :]).then_inc(x_in, 16)
            for at, n, src in ((0, AD, a["diff_qnorm_g"]), (AD, AD, a["diff_knorm_g"]), (2 * AD, 2 * AD, a["diff_subln_g"])):
                sp.dma_start(gains[:, at:at + n], src.broadcast_to((P, n))).then_inc(rows_in, 16)
            sp.dma_start(lamv[:, :], a["diff_lambda"].rearrange("a r n -> a (r n)").broadcast_to((P, 4 * AD))).then_inc(rows_in, 16)
            for slot, src, owner, name in head0:
                if (upto < 1 and name == "w3") or (upto < 3 and name == "w0"):
                    break
                load_chunk(slot, src, owner)
            if upto >= 5:
                load_chunk(0, a["exp_w_gate"][0][0], first0[0])
            if upto >= 4:
                sp.wait_ge(y_hgrn, HH)
                sp.dma_start(xs, a["x"][0].rearrange("(t p) d -> p t d", p=P)).then_inc(x_again, 16)

            def load_experts(l, first):
                tables = (a["exp_w_gate"][l], a["exp_w_up"][l], a["exp_w_down"][l])
                sp.dma_start(router, a["router_w"][l].rearrange("(k p) e -> p k e", p=P)).then_inc(router_in[l], 16)
                gate, up, down = tables
                if l:
                    load_chunk(0, gate[0], first[0])
                load_chunk(1, up[0], first[1])
                load_chunk(2, gate[1], first[2])
                base = loop_base[l]

                def load(slot, table, e):
                    src = table[bass.ds(e, 1)].rearrange("e (k p) n -> p (e k) n", p=P)
                    sp.dma_start(ring[:, slot], src).then_inc(ring_full[slot], 16)

                def rest_of_pair(i):
                    sp.wait_ge(gate0_used, i + (l * 8 + 1))
                    load(0, up, i * 2 + 1)
                    sp.wait_ge(up0_used, i + (l * 8 + 1))
                    load(1, down, i * 2)
                    sp.wait_ge(full[0], i * 2 + (base[0] + 1))
                    load(2, down, i * 2 + 1)

                with sp.Fori(0, E // 2 - 1) as i:
                    rest_of_pair(i)
                    sp.wait_ge(full[2], i + (base[2] + 1))
                    load(0, gate, i * 2 + 2)
                    sp.wait_ge(down0_used, i + (l * 8 + 1))
                    load(1, up, i * 2 + 2)
                    sp.wait_ge(full[0], i * 2 + (base[0] + 2))
                    load(2, gate, i * 2 + 3)
                rest_of_pair(E // 2 - 1)

            if upto >= 5:
                load_experts(0, first0)
                for slot, src, owner, name in head1:
                    load_chunk(slot, src, owner)
                sp.wait_ge(full[0], J["logit", 0].count)
                load_experts(1, first1)
                for b in (6, 7):
                    sp.wait_ge(free[b], loop_base[1][b] + LOOP_PER[b] * E // 2)
                sp.dma_start(out[0].rearrange("(t p) d -> p t d", p=P), xs).then_inc(out_done, 16)
                sp.wait_ge(out_done, 16)
            if tap is not None:
                tap(sp, dict(locals_of_build))

        @block.tensor
        def _(pe):
            def open_(j):
                for o in j.owners:
                    pe.wait_ge(free[o.lead], o.count)
                return j

            def taken(j):
                pe.wait_ge(free[j.lead], j.count)

            def arrived(name):
                slot, n = chunks[name]
                pe.wait_ge(ring_full[slot], 16 * n)
                return ring[:, slot]

            def mod(m, half):
                j = open_(J["modr", m, half])
                w = arrived(("mod", m))
                for k in range(KT):
                    mm = nc.tensor.matmul(ps[0:2, j.lead, :], silc[:, k, :], w[:, k, half * 512:(half + 1) * 512],
                                          start=(k == 0), stop=(k == KT - 1))
                mm.then_inc(full[j.lead], 1)

            def mod_turn(m, half):
                taken(J["modr", m, half])
                turn(J["modc", m, half], [modrow[:, (4 * half + q) * P:(4 * half + q + 1) * P] for q in range(4)])

            def tok_product(j, h, tile, w, n0):
                open_(j)
                for k in range(KT):
                    mm = nc.tensor.matmul(bank(j.lead), h[:, k, tile * P:(tile + 1) * P], w[:, k, n0:n0 + 512],
                                          start=(k == 0), stop=(k == KT - 1))
                mm.then_inc(full[j.lead], 1)

            def feat_product(j, h, n, w, n0):
                open_(j)
                for k in range(KT):
                    mm = nc.tensor.matmul(bank(j.lead, n), w[:, k, n0:n0 + P], h[:, k, 0:n],
                                          start=(k == 0), stop=(k == KT - 1))
                mm.then_inc(full[j.lead], 1)

            def turn(j, pieces):
                open_(j)
                at = 512 * j.lead
                for piece in pieces:
                    rows = piece.shape[0]
                    cols = piece.shape[1]
                    mm = nc.tensor.transpose(psf[0:cols, at:at + rows], piece, ident[0:rows, 0:rows])
                    at += rows
                mm.then_inc(full[j.lead], 1)

            pe.wait_ge(consts_in, 16 * 5)
            pe.wait_ge(rows_in, 16 * 11)
            turn(J["colsA"], [rowsA[0:76, :]])
            turn(J["colsB"], [rowsB[0:96, :]])
            pe.wait_ge(silc_ready, 1)
            for m in mods0:
                for half in range(2):
                    mod(m, half)
                    mod_turn(m, half)
            pe.wait_ge(xn_ready, TT + CT)
            for k in range(KT):
                turn(J["hT", k], [x6[:, t, k * P:(k + 1) * P] for t in range(TT)])
            for k in range(KT):
                turn(J["hcT", k], [x6[:, TT + t, k * P:(k + 1) * P] for t in range(CT)])
            if upto < 1:
                return
            for k in range(KT):
                taken(J["hT", k])
                taken(J["hcT", k])
            w = arrived("w3")
            for name, n0 in (("dk", 0), ("dv", 512)):
                for t in range(TT):
                    tok_product(J[name, t], hT, t, w, n0)
                for t in range(CT):
                    tok_product(J[name, TT + t], hcT, t, w, n0)
            w = arrived("w2")
            for h in range(HH):
                feat_product(J["gate", h], hT, T, w, h * P)
            for t in range(TT):
                tok_product(J["dq", t], hT, t, w, 512)
            pe.wait_ge(qk_normed, 2 * TT + CT)
            for h in range(AH):
                turn(J["qT", h], [qtok[:, t, h * P:(h + 1) * P] for t in range(TT)])
                turn(J["kT", h], [ktok[:, t, h * P:(h + 1) * P] for t in range(TT + CT)])
            for h in range(AH):
                taken(J["qT", h])
                taken(J["kT", h])
            for t in range(TT + CT):
                taken(J["dv", t])

            def scores(h, t):
                for m in range(2):
                    j = open_(J[f"s{m}", h, t])
                    f = slice(m * AD, (m + 1) * AD)
                    for k0, kn in ((0, T), (T, TC)):
                        mm = nc.tensor.matmul(psf[:, 512 * j.lead + k0:512 * j.lead + k0 + kn],
                                              qT[f, h, t * P:(t + 1) * P], kT[f, h, k0:k0 + kn],
                                              start=True, stop=True)
                    mm.then_inc(full[j.lead], 1)

            scores(0, 0)
            for n, (h, t) in enumerate(att):
                if n + 1 < len(att):
                    scores(*att[n + 1])
                pe.wait_ge(wgt_ready, n + 1)
                turn(J["wT", h, t], [wgt[:, k * P:(k + 1) * P] for k in range(TT + CT)])
                taken(J["wT", h, t])
                j = open_(J["o", h, t])
                for k in range(TT + CT):
                    mm = nc.tensor.matmul(bank(j.lead, P), wT[:, k, :], vtok[:, k, h * P:(h + 1) * P],
                                          start=(k == 0), stop=(k == TT + CT - 1))
                mm.then_inc(full[j.lead], 1)
            pe.wait_ge(o_normed, TT)
            for h in range(AH):
                turn(J["oT", h], [oall[:, t, h * P:(h + 1) * P] for t in range(TT)])
            if upto < 3:
                return
            w = arrived("w1")
            for t in range(TT):
                tok_product(J["hv", t], hT, t, w, 512)
            for t in range(CT):
                tok_product(J["hv", TT + t], hcT, t, w, 512)
            for d, name, n0 in ((1, "w1", 0), (0, "w0", 512)):
                w = arrived(name)
                for h in range(HH):
                    feat_product(J["zc", d, h], hcT, TC, w, n0 + h * P)
                for h in range(HH):
                    feat_product(J["z", d, h], hT, T, w, n0 + h * P)
            for h in range(HH):
                feat_product(J["hq", h], hT, T, w, h * P)
            for t in range(TT + CT):
                taken(J["hv", t])
            for h in range(HH):
                taken(J["hq", h])
            pe.wait_ge(hk_ready, 4 * HH)
            n = 0
            for d in (1, 0):
                for h in range(HH):
                    pe.wait_ge(kcd_ready, n + 1)
                    turn(J["kcT", d, h], [kcdec[:, t * P:(t + 1) * P] for t in range(CT)])
                    taken(J["kcT", d, h])
                    j = open_(J["s0c", d, h])
                    for t in range(CT):
                        mm = nc.tensor.matmul(bank(j.lead, P), kcdtok[:, t, :], hv[:, TT + t, h * P:(h + 1) * P],
                                              start=(t == 0), stop=(t == CT - 1))
                    mm.then_inc(full[j.lead], 1)
                    for L in range(LEVELS + 1):
                        if (n, L) in fills:
                            mod(*fills[n, L])
                            mod_turn(*fills[n, L])
                        if L < LEVELS:
                            m = n * LEVELS + L
                            pe.wait_ge(lv_ready, m + 1)
                            kk, qq = lvK[:, m % 2], lvQ[:, m % 2]
                        else:
                            kk, qq = hk[d][:, h], hq[:, h]
                        j = open_(J["sc", d, h, L])
                        for c in range(NC):
                            cc = slice(c * CH, (c + 1) * CH)
                            mm = nc.tensor.matmul(bank(j.lead)[:, cc], kk[:, cc], qq[:, cc], start=True, stop=True)
                        mm.then_inc(full[j.lead], 1)
                    pe.wait_ge(qdec_ready, n + 1)
                    turn(J["kdT", d, h], [kdec[:, c * CH:(c + 1) * CH] for c in range(NC)])
                    taken(J["kdT", d, h])
                    taken(J["sc", d, h, LEVELS])
                    jo = open_(J["ho", d, h])
                    order = range(NC) if d == 0 else range(NC - 1, -1, -1)
                    for s, c in enumerate(order):
                        cc = slice(c * CH, (c + 1) * CH)
                        if s < NC - 1:
                            j = open_(J["kv", d, h, s])
                            nc.tensor.matmul(bank(j.lead, P), kdtok[:, c, :], hv[:, c, h * P:(h + 1) * P],
                                             start=True, stop=True).then_inc(full[j.lead], 1)
                        nc.tensor.matmul(bank(jo.lead)[:, cc], hv[:, c, h * P:(h + 1) * P], sc[:, cc],
                                         start=True, stop=False)
                        taken(J["kv", d, h, s - 1] if s else J["s0c", d, h])
                        mm = nc.tensor.matmul(bank(jo.lead)[:, cc], state[:, s % 2], qdec[:, cc],
                                              start=False, stop=True)
                    mm.then_inc(full[jo.lead], 1)
                    n += 1
            for h in range(HH):
                pe.wait_ge(sq_ready, h + 1)
                j = open_(J["ssq", h])
                nc.tensor.matmul(bank(j.lead), ones[:, 0:P], sq[:, h], start=True, stop=True).then_inc(full[j.lead], 1)

            def grow_row(j, l, which):
                open_(j)
                for k in range(KT):
                    mm = nc.tensor.matmul(psf[:, 512 * j.lead + k * P:512 * j.lead + (k + 1) * P],
                                          modc[:, l, which, k:k + 1].broadcast_to((P, P)), ident[:, :],
                                          start=True, stop=True)
                mm.then_inc(full[j.lead], 1)

            def project_out(l, y, w):
                grow_row(J["grow", l], l, 2)
                w = arrived(w)
                for t in range(TT):
                    for half in range(2):
                        tok_product(J["y", l, t, half], y, t, w, 512 * half)

            pe.wait_ge(y_hgrn, HH)
            for h in range(AH):
                taken(J["oT", h])
            project_out(0, yT, "wo")
            if upto < 5:
                return

            def moe(l):
                pe.wait_ge(xn_ready, TT + CT + TT * (1 + 2 * l))
                for k in range(KT):
                    turn(J["h2T", l, k], [xn[:, t, k * P:(k + 1) * P] for t in range(TT)])
                pe.wait_ge(router_in[l], 16)
                for k in range(KT):
                    taken(J["h2T", l, k])
                j = open_(J["logit", l])
                for t in range(TT):
                    for k in range(KT):
                        mm = nc.tensor.matmul(bank(j.lead)[:, t * E:(t + 1) * E], h2T[:, k, t * P:(t + 1) * P],
                                              router[:, k, :], start=(k == 0), stop=(k == KT - 1))
                mm.then_inc(full[j.lead], 1)
                pe.wait_ge(aff_ready, l + 1)
                turn(J["affT", l], [aff[:, t, :] for t in range(TT)])
                pe.wait_ge(slot_ready, l + 1)
                turn(J["slotT", l], [sel[0:E, 3, t * P:(t + 1) * P] for t in range(TT)])
                pe.wait_ge(x_ready, 8 * (l + 1))
                grow_row(J["grow2", l], l, 5)
                taken(J["grow2", l])
                for b in range(8):
                    pe.wait_ge(free[b], loop_base[l][b])
                base = loop_base[l]
                with pe.Fori(0, E // 2) as i:
                    def use(b, nth):
                        pe.wait_ge(free[b], i * LOOP_PER[b] + (base[b] + nth))

                    def made(b, nth):
                        pe.wait_ge(free[b], i * LOOP_PER[b] + (base[b] + nth + 1))

                    def product(b, e, slot, nth, left):
                        pe.wait_ge(ring_full[slot], i * 32 + 16 * (exp_base[l][slot] + nth + 1))
                        for half in range(2):
                            for k in range(KT):
                                mm = nc.tensor.matmul(ps[e * CAP:(e + 1) * CAP, b + half, :],
                                                      left[:, k, e * CAP:(e + 1) * CAP],
                                                      ring[:, slot, k, half * 512:(half + 1) * 512],
                                                      start=(k == 0), stop=(k == KT - 1))
                        return mm

                    pe.wait_ge(onehot_ready, i + (l * 8 + 1))
                    for half in range(2):
                        use(4 + half, 0)
                        for q in range(4):
                            k = 4 * half + q
                            for t in range(TT):
                                mm = nc.tensor.matmul(bank(4 + half)[:, q * P:(q + 1) * P], xn[:, t, k * P:(k + 1) * P],
                                                      onehot[:, t].rearrange("p e s -> p (e s)"),
                                                      start=(t == 0), stop=(t == TT - 1))
                        mm.then_inc(full[4 + half], 1)
                    use(6, 0)
                    pe.wait_ge(gated_ready, i + (l * 8 + 1))
                    for t in range(TT):
                        mm = nc.tensor.transpose(bank(6)[:, t * P:(t + 1) * P],
                                                 gated[:, t].rearrange("p e s -> p (e s)"), ident[:, :])
                    mm.then_inc(full[6], 1)
                    made(4, 0)
                    made(5, 0)
                    use(0, 0)
                    product(0, 0, 0, 0, xe).then_inc(gate0_used, 1)
                    use(2, 0)
                    product(2, 0, 1, 0, xe).then_inc(up0_used, 1)
                    product(0, 1, 2, 0, xe).then_inc(full[0], 1)
                    product(2, 1, 0, 1, xe).then_inc(full[2], 1)
                    made(2, 0)
                    for half in range(2):
                        use(4 + half, 1)
                        for q in range(4):
                            mm = nc.tensor.transpose(bank(4 + half)[:, q * P:(q + 1) * P],
                                                     actb[:, (4 * half + q) * P:(4 * half + q + 1) * P], ident[:, :])
                        mm.then_inc(full[4 + half], 1)
                    use(0, 1)
                    made(4, 1)
                    made(5, 1)
                    product(0, 0, 1, 1, actT).then_inc(down0_used, 1)
                    product(0, 1, 2, 1, actT).then_inc(full[0], 1)
                    made(6, 0)
                    made(0, 1)
                    for t in range(TT):
                        for half in range(2):
                            b = 6 + half
                            use(b, t + 1 - half)
                            nc.tensor.matmul(bank(b), spread[:, t * P:(t + 1) * P], ye[:, half * 512:(half + 1) * 512],
                                             start=True, stop=True).then_inc(full[b], 1)

            moe(0)
            pe.wait_ge(xn_ready, TT + CT + 2 * TT)
            for k in range(KT):
                turn(J["h3T", k], [xn[:, t, k * P:(k + 1) * P] for t in range(TT)])
            for k in range(KT):
                taken(J["h3T", k])
            for part, name in (("b", "cb"), ("c", "cc"), ("v", "cv")):
                w = arrived(name)
                for f in range(KT):
                    feat_product(J["conv", part, f], hT, T, w, f * P)
            pe.wait_ge(ycT_ready, KT)
            project_out(1, ycT, "co")
            moe(1)

        @block.vector
        def _(dve):
            step = Chain(dve, dve_step)
            V = nc.vector

            def wait_full(j):
                dve.wait_ge(full[j.lead], j.count)

            step(V.memset(ones[:, :], 1.0))
            step(V.memset(reset[:, :, :], 1.0))
            step(V.memset(reset[:, 0, 0:T:CH], 0.0))
            step(V.memset(reset[:, 1, CH - 1:T:CH], 0.0))
            dve.wait_ge(consts_in, 16 * 5)
            step(V.tensor_copy(masks[:, :, :, :].rearrange("p d l n -> p (d l n)"), masks_in))
            wait_full(J["colsA"])
            V.tensor_copy(colsA[:, 0:76], bank(0, 76)).then_inc(free[0], 1)
            dve.wait_ge(free[0], 1)
            V.tensor_copy(silc[:, :, :].rearrange("p k w -> p w k"), colsA[:, 0:16].rearrange("p (w k) -> p w k", w=2)).then_inc(cols_ready, 1)
            wait_full(J["colsB"])
            V.tensor_copy(colsB[:, :], bank(1, 96)).then_inc(free[1], 1)
            dve.wait_ge(free[1], 1)
            dve.wait_ge(rows_in, 16 * 11)
            lv = lamv[:, :].rearrange("p (r n) -> p r n", r=4)
            step(V.tensor_tensor(ta[:, 0:2 * AD].rearrange("p (r n) -> p r n", r=2), lv[:, 0::2], lv[:, 1::2], ALU.mult))
            V.tensor_reduce(small[:, 0:2], ta[:, 0:2 * AD].rearrange("p (r n) -> p r n", r=2), AX, ALU.add).then_inc(lam_dots, 1)
            dve.wait_ge(lam_exps, 1)
            step(V.tensor_tensor(small[:, 4:5], small[:, 2:3], small[:, 3:4], ALU.subtract))
            step(V.tensor_scalar(small[:, 5:6], small[:, 4:5], LAM_INIT, -1.0, ALU.add, ALU.mult))
            step(V.tensor_scalar(gains[:, 2 * AD:4 * AD], gains[:, 2 * AD:4 * AD], 1.0 - LAM_INIT, None, ALU.mult))

            def root(src, dst, n, scale, which):
                sem_in, sem_out, count = which
                V.tensor_scalar(dst, src, scale, EPS, ALU.mult, ALU.add).then_inc(sem_in, 1)
                dve.wait_ge(sem_out, count)
                step(V.reciprocal(dst, dst))

            dve.wait_ge(squares_ready, TT + CT)
            rstd = small[:, 16:16 + TT + CT]
            root(small[:, 8:8 + TT + CT], rstd, TT + CT, 1.0 / D, (means_ready, roots_ready, 1))
            for t in range(TT + CT):
                V.tensor_scalar(x6[:, t], x6[:, t], rstd[:, t:t + 1], None, ALU.mult).then_inc(xn_ready, 1)

            def take_mod(m, half):
                l, jj = m
                j = J["modc", m, half]
                wait_full(j)
                pv = bank(j.lead, KT).rearrange("p (k w) -> p k w", w=2)
                kk = slice(4 * half, 4 * half + 4)
                b0 = (6 * l + jj) * KT + 4 * half
                if l == 0 and jj < 2:
                    step(V.tensor_tensor(modx[:, jj, kk], pv[:, :, 1], colsB[:, b0:b0 + 4], ALU.add))
                V.tensor_tensor(modc[:, l, jj, kk], pv[:, :, 0], colsB[:, b0:b0 + 4], ALU.add).then_inc(free[j.lead], 1)
                dve.wait_ge(free[j.lead], j.count)
                if jj in (1, 4):
                    n = (0 if jj == 1 else 2) + l
                    g0 = (16 if jj == 1 else 32) + l * KT + 4 * half
                    V.scalar_tensor_tensor(scaleA[:, n, kk], modc[:, l, jj, kk], 1.0, colsA[:, g0:g0 + 4],
                                           ALU.add, ALU.mult).then_inc(scale_ready, 1)
                    if m == (0, 1):
                        V.scalar_tensor_tensor(scaleA[:, 4, kk], modx[:, 1, kk], 1.0, colsA[:, g0:g0 + 4],
                                               ALU.add, ALU.mult).then_inc(scale_ready, 1)

            for m in mods0:
                for half in range(2):
                    take_mod(m, half)
            dve.wait_ge(scale_ready, 4)

            def modulate(j, dst, k, gain, shift, n):
                wait_full(j)
                V.tensor_scalar(dst[:, k], bank(j.lead, n), gain[:, k:k + 1], shift[:, k:k + 1],
                                ALU.mult, ALU.add).then_inc(free[j.lead], 1)

            for k in range(1, KT, 2):
                modulate(J["hT", k], hT, k, scaleA[:, 0], modc[:, 0, 0], T)
            for k in range(1, KT, 2):
                modulate(J["hcT", k], hcT, k, scaleA[:, 4], modx[:, 0], TC)
            if upto < 1:
                return
            for n, (arr, t, g0, rot) in enumerate([(ktok, t, AD, t < TT) for t in range(TT + CT)]
                                                  + [(qtok, t, 0, True) for t in range(TT)]):
                x8 = arr[:, t].rearrange("p (g n) -> p g n", n=AD)
                r8 = small[:, 32 + 8 * (n % 2):40 + 8 * (n % 2)]
                dve.wait_ge(qk_squares, n + 1)
                step(V.tensor_reduce(r8, tsq[:, n % 2].rearrange("p (g n) -> p g n", n=AD), AX, ALU.add))
                root(r8, r8, 8, 1.0 / AD, (qk_means, qk_roots, n + 1))
                step(V.tensor_tensor(x8, x8, r8[:, :, None].broadcast_to((P, 8, AD)), ALU.mult))
                gain = gains[:, g0:g0 + AD][:, None, :].broadcast_to((P, 8, AD))
                last = V.tensor_tensor(x8, x8, gain, ALU.mult)
                if rot:
                    step(last)
                    cos8 = rope_cos[:, t][:, None, :].broadcast_to((P, 8, AD))
                    halves = arr[:, t].rearrange("p (g a w n) -> p (g a) w n", a=2, w=2, n=AD // 4)
                    sw = trot[:, 1].rearrange("p (g a w n) -> p (g a) w n", a=2, w=2, n=AD // 4)
                    step(V.tensor_tensor(trot[:, 0].rearrange("p (g n) -> p g n", n=AD), x8, cos8, ALU.mult))
                    for w in range(2):
                        sin8 = rope_sin[:, t].rearrange("p (a w n) -> p a w n", a=2, w=2)[:, :, w]
                        sin8 = sin8[:, None].broadcast_to((P, 8, 2, AD // 4))
                        o4 = sw[:, :, w].rearrange("p (g a) n -> p g a n", a=2)
                        i4 = halves[:, :, 1 - w].rearrange("p (g a) n -> p g a n", a=2)
                        step(V.tensor_tensor(o4, i4, sin8, ALU.mult))
                    last = V.tensor_tensor(arr[:, t], trot[:, 0], trot[:, 1], ALU.add)
                last.then_inc(qk_normed, 1)
            for h in range(AH):
                j = J["qT", h]
                wait_full(j)
                V.tensor_copy(qT[:, h], bank(j.lead)).then_inc(free[j.lead], 1)

            def maxima(n):
                h, t = att[n]
                for m in range(2):
                    j = J[f"s{m}", h, t]
                    wait_full(j)
                    if n >= 2:
                        j2 = J[f"s{m}", *att[n - 2]]
                        dve.wait_ge(free[j2.lead], j2.count)
                    mx = small[:, 64 + 2 * (n % 2) + m:65 + 2 * (n % 2) + m]
                    step(V.tensor_reduce(mx, psf[:, 512 * j.lead:512 * j.lead + T + TC], AX, ALU.max))
                    V.tensor_scalar(mx, mx, -AD ** -0.5, None, ALU.mult).then_inc(max_ready, 1)

            maxima(0)
            for n, (h, t) in enumerate(att):
                if n + 1 < len(att):
                    maxima(n + 1)
                j = J["s1", h, t]
                dve.wait_ge(free[j.lead], j.count)
                j = J["s0", h, t]
                dve.wait_ge(free[j.lead], j.count)
                sums = small[:, 68 + 2 * (n % 2):70 + 2 * (n % 2)]
                step(V.reciprocal(sums, sums))
                step(V.tensor_scalar(sums[:, 1:2], sums[:, 1:2], small[:, 5:6], None, ALU.mult))
                pr = prob[:, n % 2]
                step(V.tensor_scalar(pr[:, 1], pr[:, 1], sums[:, 1:2], None, ALU.mult))
                if n:
                    jw = J["wT", *att[n - 1]]
                    dve.wait_ge(full[jw.lead], jw.count)
                V.scalar_tensor_tensor(wgt, pr[:, 0], sums[:, 0:1], pr[:, 1], ALU.mult, ALU.add).then_inc(wgt_ready, 1)
            dve.wait_ge(o_squares, len(att))
            root(small[:, 80:96], small[:, 80:96], 16, 1.0 / (2 * AD), (o_means, o_roots, 1))
            for t in range(TT):
                o4 = oall[:, t].rearrange("p (h n) -> p h n", h=AH)
                step(V.tensor_tensor(o4, o4, small[:, 80 + 4 * t:84 + 4 * t][:, :, None].broadcast_to((P, AH, P)), ALU.mult))
                V.tensor_tensor(o4, o4, gains[:, 2 * AD:4 * AD][:, None, :].broadcast_to((P, AH, P)),
                                ALU.mult).then_inc(o_normed, 1)
            if upto < 3:
                return
            n = 0
            for d in (1, 0):
                for c, B, K, N in (("zc", cb[d], ck[d], TC), ("z", hb[d], hk[d], T)):
                    for h in range(HH):
                        j = J[c, d, h]
                        dve.wait_ge(log_ready, n + 1)
                        l1 = spl[:, n % 2, 0:N]
                        step(V.scalar_tensor_tensor(B[:, h], bank(j.lead, N), 0.0, l1, ALU.min, ALU.subtract))
                        V.scalar_tensor_tensor(K[:, h], bank(j.lead, N), 0.0, l1, ALU.max, ALU.add).then_inc(free[j.lead], 1)
                        rev = slice(None, None, -1) if d else slice(None)
                        keep = ones[:, 0:N] if c == "zc" else reset[:, d]
                        V.tensor_tensor_scan(B[:, h][:, rev], keep[:, rev], B[:, h][:, rev], 0.0,
                                             ALU.mult, ALU.add).then_inc(b_ready, 1)
                        n += 1
            dve.wait_ge(hk_ready, 4 * HH)
            for h in range(HH):
                j = J["hq", h]
                dve.wait_ge(free[j.lead], j.count)
            n = 0
            for d in (1, 0):
                for h in range(HH):
                    dve.wait_ge(cdec_ready, n + 1)
                    V.tensor_tensor(kcdec, kcdec, ck[d][:, h], ALU.mult).then_inc(kcd_ready, 1)
                    if h == 0:
                        if n:
                            j = J["ho", 1, HH - 1]
                            dve.wait_ge(full[j.lead], j.count)
                        step(V.memset(sc, 0.0))

                    def take_level(L):
                        j = J["sc", d, h, L]
                        wait_full(j)
                        mk = masks[:, d, L][:, None, :].broadcast_to((P, NC, CH))
                        V.copy_predicated(sc.rearrange("p (c n) -> p c n", c=NC), mk,
                                          bank(j.lead).rearrange("p (c n) -> p c n", c=NC)).then_inc(free[j.lead], 1)
                        dve.wait_ge(free[j.lead], j.count)

                    if n:
                        j = J["ho", (1, 0)[(n - 1) // HH], (n - 1) % HH]
                        dve.wait_ge(full[j.lead], j.count)
                    for L in range(LEVELS):
                        m = n * LEVELS + L
                        if (n, L) in fills:
                            take_mod(*fills[n, L])
                        dve.wait_ge(decay_ready, m + 1)
                        if L >= 2:
                            take_level(L - 2)
                        step(V.tensor_tensor(lvQ[:, m % 2], lvE[:, m % 2], hq[:, h], ALU.mult))
                        V.tensor_tensor(lvK[:, m % 2], lvE[:, m % 2], hk[d][:, h], ALU.mult).then_inc(lv_ready, 1)
                    dve.wait_ge(ends_ready, n + 1)
                    end = 0 if d else CH - 1
                    step(V.tensor_copy(small[:, 100:100 + NC], qdec[:, end::CH]))
                    step(V.tensor_tensor(qdec, qdec, hq[:, h], ALU.mult))
                    V.tensor_tensor(kdec, kdec, hk[d][:, h], ALU.mult).then_inc(qdec_ready, 1)
                    for L in (LEVELS - 2, LEVELS - 1, LEVELS):
                        take_level(L)
                    order = range(NC) if d == 0 else range(NC - 1, -1, -1)
                    j = J["s0c", d, h]
                    dve.wait_ge(free[j.lead], j.count)
                    for s, c in enumerate(order):
                        if s < NC - 1:
                            j = J["kv", d, h, s]
                            wait_full(j)
                            V.scalar_tensor_tensor(state[:, (s + 1) % 2], state[:, s % 2], small[:, 100 + c:101 + c],
                                                   bank(j.lead, P), ALU.mult, ALU.add).then_inc(free[j.lead], 1)
                            dve.wait_ge(free[j.lead], j.count)
                    if d == 0:
                        j = J["ho", 0, h]
                        wait_full(j)
                        V.tensor_tensor(ho[:, h], bank(j.lead), ho[:, h], ALU.add).then_inc(free[j.lead], 1)
                    n += 1
            for h in range(HH):
                j = J["ssq", h]
                wait_full(j)
                V.tensor_scalar(root_h[:, h], bank(j.lead), 1.0 / HD, EPS, ALU.mult, ALU.add).then_inc(free[j.lead], 1)
            for h in range(HH):
                dve.wait_ge(hroot_out, h + 1)
                step(V.reciprocal(root_h[:, h], root_h[:, h]))
                step(V.tensor_tensor(root_h[:, h], root_h[:, h], ho[:, h], ALU.mult))
                V.scalar_tensor_tensor(yT[:, h], root_h[:, h], colsA[:, 48 + h:49 + h], yT[:, h],
                                       ALU.mult, ALU.mult).then_inc(y_hgrn, 1)

            def add_out(l):
                j = J["grow", l]
                dve.wait_ge(free[j.lead], j.count)
                if l == 0:
                    dve.wait_ge(x_again, 16)
                for t in range(TT):
                    for half in range(2):
                        hs = slice(512 * half, 512 * half + 512)
                        j = J["y", l, t, half]
                        wait_full(j)
                        V.tensor_tensor(xtmp[:, half], bank(j.lead), grow[:, hs], ALU.mult).then_inc(free[j.lead], 1)
                        dve.wait_ge(free[j.lead], j.count)
                        V.tensor_tensor(xs[:, t, hs], xs[:, t, hs], xtmp[:, half], ALU.add).then_inc(x_ready, 1)

            def norm(nth):
                dve.wait_ge(squares_ready, TT + CT + TT * nth)
                root(small[:, 8:8 + TT], rstd[:, 0:TT], TT, 1.0 / D, (means_ready, roots_ready, nth + 1))
                for t in range(TT):
                    V.tensor_scalar(xn[:, t], xs[:, t], rstd[:, t:t + 1], None, ALU.mult).then_inc(xn_ready, 1)

            def moe(l):
                norm(1 + 2 * l)
                for k in range(1, KT, 2):
                    modulate(J["h2T", l, k], h2T, k, scaleA[:, 2 + l], modc[:, l, 3], T)
                j = J["logit", l]
                wait_full(j)
                lg = bank(j.lead, TT * E).rearrange("p (t e) -> p t e", e=E)
                m4 = small[:, 120:124]
                step(V.tensor_reduce(m4, lg, AX, ALU.max))
                V.tensor_tensor(aff[:, :, :], lg, m4[:, :, None].broadcast_to((P, TT, E)), ALU.subtract).then_inc(free[j.lead], 1)
                dve.wait_ge(logit_exp, l + 1)
                step(V.tensor_reduce(m4, aff[:, :, :], AX, ALU.add))
                step(V.reciprocal(m4, m4))
                V.tensor_tensor(aff[:, :, :], aff[:, :, :], m4[:, :, None].broadcast_to((P, TT, E)), ALU.mult).then_inc(aff_ready, 1)
                j = J["affT", l]
                wait_full(j)
                row = [sel[0:E, n] for n in range(4)]
                V.tensor_copy(row[0], bank(j.lead)[0:E, :]).then_inc(free[j.lead], 1)
                dve.wait_ge(free[j.lead], j.count)
                top = small[0:E, 128:136]
                for r in range(CAP // 8):
                    step(V.max(top, row[min(r, 1)]))
                    step(V.match_replace(row[1], top, row[min(r, 1)], -1.0))
                step(V.tensor_scalar(row[2], row[1], 0.0, None, ALU.is_lt))
                step(V.tensor_tensor_scan(row[0], row[2], row[2], 0.0, ALU.add, ALU.max))
                step(V.tensor_tensor(row[0], row[0], row[2], ALU.mult))
                V.tensor_scalar(row[3], row[0], -1.0, None, ALU.add).then_inc(slot_ready, 1)
                j = J["slotT", l]
                wait_full(j)
                V.tensor_copy(slotc[:, :, :], bank(j.lead, TT * E).rearrange("p (t e) -> p t e", e=E)).then_inc(free[j.lead], 1)
                dve.wait_ge(free[j.lead], j.count)
                base = loop_base[l]
                with dve.Fori(0, E // 2) as i:
                    def wait_use(b, nth):
                        dve.wait_ge(full[b], i * LOOP_PER[b] + (base[b] + nth + 1))
                        return bank(b)

                    pair = (P, TT, 2, CAP)
                    slots = slotc[:, :, bass.ds(i * 2, 2)][:, :, :, None].broadcast_to(pair)
                    gates = aff[:, :, bass.ds(i * 2, 2)][:, :, :, None].broadcast_to(pair)
                    V.tensor_tensor(onehot, slots, iota[:, None, None, :].broadcast_to(pair), ALU.is_equal).then_inc(onehot_ready, 1)
                    dve.wait_ge(onehot_ready, i + (l * 8 + 1))
                    V.tensor_tensor(gated, onehot, gates, ALU.mult).then_inc(gated_ready, 1)
                    g = wait_use(5, 0)
                    for q in range(4):
                        k = 4 + q
                        ins = V.tensor_scalar(xe[:, k], g[:, q * P:(q + 1) * P], scaleA[:, 2 + l, k:k + 1],
                                              modc[:, l, 3, k:k + 1], ALU.mult, ALU.add)
                    ins.then_inc(free[5], 1)
                    wait_use(2, 0)
                    dve.wait_ge(free[0], i * 2 + (base[0] + 1))
                    V.tensor_tensor(actb, psf[:, 1024:2048], sil, ALU.mult).then_inc(free[2], 1)
                    V.tensor_copy(actT[:, 4:8].rearrange("p k n -> p (k n)"), wait_use(5, 1)).then_inc(free[5], 1)
                    wait_use(0, 1)
                    V.tensor_tensor(ye, psf[:, 0:1024], grow[:, :], ALU.mult).then_inc(free[0], 1)
                    for t in range(TT):
                        for half in range(2):
                            y = wait_use(6 + half, t + 1 - half)
                            hs = slice(512 * half, 512 * half + 512)
                            V.tensor_tensor(xs[:, t, hs], y, xs[:, t, hs], ALU.add).then_inc(free[6 + half], 1)

            add_out(0)
            if upto < 5:
                return
            moe(0)
            norm(2)
            for k in range(1, KT, 2):
                modulate(J["h3T", k], hT, k, scaleA[:, 1], modc[:, 1, 0], T)
            step(V.memset(uT[:, 0:1], 0.0))
            step(V.memset(uT[:, T + 1:T + 2], 0.0))
            for f in range(KT):
                j = J["conv", "c", f]
                dve.wait_ge(free[j.lead], j.count)
                j = J["conv", "b", f]
                dve.wait_ge(free[j.lead], j.count)
                j = J["conv", "v", f]
                wait_full(j)
                V.tensor_tensor(uT[:, 1:T + 1], bank(j.lead), cT[:, f], ALU.mult).then_inc(free[j.lead], 1)
                dve.wait_ge(free[j.lead], j.count)
                w = [colsA[:, 52 + 8 * n + f:53 + 8 * n + f] for n in range(3)]
                step(V.tensor_scalar(vT, uT[:, 0:T], w[0], None, ALU.mult))
                step(V.scalar_tensor_tensor(vT, uT[:, 1:T + 1], w[1], vT, ALU.mult, ALU.add))
                step(V.scalar_tensor_tensor(vT, uT[:, 2:T + 2], w[2], vT, ALU.mult, ALU.add))
                V.tensor_tensor(ycT[:, f], vT, bT[:, f], ALU.mult).then_inc(ycT_ready, 1)
                dve.wait_ge(ycT_ready, f + 1)
            add_out(1)
            moe(1)

        @block.scalar
        def _(act):
            S = nc.scalar
            step = Chain(act, act_step)

            def wait_full(j):
                act.wait_ge(full[j.lead], j.count)

            def copy(j, dst, n=512, func=ACT.Copy):
                wait_full(j)
                S.activation(dst, psf[:, 512 * j.lead:512 * j.lead + n], func).then_inc(free[j.lead], 1)

            def modulate(j, dst, k, gain, shift, n):
                wait_full(j)
                S.activation(dst[:, k], bank(j.lead, n), ACT.Identity, bias=shift[:, k:k + 1],
                             scale=gain[:, k:k + 1]).then_inc(free[j.lead], 1)

            act.wait_ge(cols_ready, 1)
            S.activation(silc[:, :, :], silc[:, :, :], ACT.Silu).then_inc(silc_ready, 1)

            def row_mod(m, half):
                j = J["modr", m, half]
                wait_full(j)
                S.activation(modrow[:, half * 512:(half + 1) * 512], ps[0:2, j.lead, :], ACT.Copy).then_inc(free[j.lead], 1)

            act.wait_ge(lam_dots, 1)
            S.activation(small[:, 2:4], small[:, 0:2], ACT.Exp).then_inc(lam_exps, 1)
            for n, t in enumerate([4, 5, 0, 1, 2, 3]):
                act.wait_ge(x_in, 16 * (TT + CT))
                if n:
                    act.wait_ge(squares_ready, n)
                S.activation(junk, x6[:, t], ACT.Square, accum_out=small[:, 8 + t:9 + t]).then_inc(squares_ready, 1)
            act.wait_ge(means_ready, 1)
            S.activation(rstd_(small, TT + CT), rstd_(small, TT + CT), ACT.Sqrt).then_inc(roots_ready, 1)
            for m in mods0:
                for half in range(2):
                    row_mod(m, half)
            act.wait_ge(scale_ready, 4)
            for k in range(0, KT, 2):
                modulate(J["hT", k], hT, k, scaleA[:, 0], modc[:, 0, 0], T)
            for k in range(0, KT, 2):
                modulate(J["hcT", k], hcT, k, scaleA[:, 4], modx[:, 0], TC)
            if upto < 1:
                return

            def take_qk(n, j, arr, t):
                copy(j, arr[:, t])
                act.wait_ge(free[j.lead], j.count)
                if n >= 2:
                    act.wait_ge(qk_means, n - 1)
                S.activation(tsq[:, n % 2], arr[:, t], ACT.Square).then_inc(qk_squares, 1)

            def roots_qk(n):
                act.wait_ge(qk_means, n + 1)
                r8 = small[:, 32 + 8 * (n % 2):40 + 8 * (n % 2)]
                S.activation(r8, r8, ACT.Sqrt).then_inc(qk_roots, 1)

            for t in range(TT + CT):
                take_qk(t, J["dk", t], ktok, t)
                roots_qk(t)
            for t in range(TT + CT):
                copy(J["dv", t], vtok[:, t])
            for h in range(HH):
                copy(J["gate", h], yT[:, h], func=ACT.Silu)
            for t in range(TT):
                take_qk(TT + CT + t, J["dq", t], qtok, t)
                roots_qk(TT + CT + t)
            for h in range(AH):
                copy(J["kT", h], kT[:, h], T + TC)

            def exps(n):
                h, t = att[n]
                if n >= 2:
                    act.wait_ge(wgt_ready, n - 1)
                for m in range(2):
                    j = J[f"s{m}", h, t]
                    act.wait_ge(max_ready, 2 * n + m + 1)
                    S.activation(prob[:, n % 2, m], psf[:, 512 * j.lead:512 * j.lead + T + TC], ACT.Exp,
                                 bias=small[:, 64 + 2 * (n % 2) + m:65 + 2 * (n % 2) + m], scale=AD ** -0.5,
                                 accum_out=small[:, 68 + 2 * (n % 2) + m:69 + 2 * (n % 2) + m]).then_inc(free[j.lead], 1)

            exps(0)
            for n, (h, t) in enumerate(att):
                if n + 1 < len(att):
                    exps(n + 1)
                copy(J["wT", h, t], wT.rearrange("p k n -> p (k n)"), T + TC)
                j = J["o", h, t]
                copy(j, oall[:, t, h * P:(h + 1) * P], P)
                act.wait_ge(free[j.lead], j.count)
                if n:
                    act.wait_ge(o_squares, n)
                S.activation(junk[:, 0:P], oall[:, t, h * P:(h + 1) * P], ACT.Square,
                             accum_out=small[:, 80 + 4 * t + h:81 + 4 * t + h]).then_inc(o_squares, 1)
            act.wait_ge(o_means, 1)
            S.activation(small[:, 80:96], small[:, 80:96], ACT.Sqrt).then_inc(o_roots, 1)
            for h in range(AH):
                copy(J["oT", h], yT[:, AH + h])
            if upto < 3:
                return
            for t in range(TT + CT):
                copy(J["hv", t], hv[:, t])
            n = 0
            last = None
            for d in (1, 0):
                for c, K, N in (("zc", ck[d], TC), ("z", hk[d], T)):
                    for h in range(HH):
                        j = J[c, d, h]
                        wait_full(j)
                        buf = spl[:, n % 2, 0:N]
                        if n >= 2:
                            act.wait_ge(free[last[0].lead], last[0].count)
                        step(S.activation(buf, bank(j.lead, N), ACT.Abs))
                        step(S.activation(buf, buf, ACT.Exp, scale=-1.0))
                        S.activation(buf, buf, ACT.Ln, bias=1.0).then_inc(log_ready, 1)
                        if last is not None:
                            pj, pk = last
                            act.wait_ge(free[pj.lead], pj.count)
                            S.activation(pk, pk, ACT.Exp, scale=-1.0).then_inc(hk_ready, 1)
                        last = (j, K[:, h])
                        n += 1
            pj, pk = last
            act.wait_ge(free[pj.lead], pj.count)
            S.activation(pk, pk, ACT.Exp, scale=-1.0).then_inc(hk_ready, 1)
            for h in range(HH):
                copy(J["hq", h], hq[:, h])
            act.wait_ge(b_ready, 4 * HH)
            n = 0
            for d in (1, 0):
                for h in range(HH):
                    ce = 0 if d else TC - 1
                    if n:
                        j = J["kcT", (1, 0)[(n - 1) // HH], (n - 1) % HH]
                        act.wait_ge(full[j.lead], j.count)
                    S.activation(kcdec, cb[d][:, h], ACT.Exp, scale=-1.0, bias=cb[d][:, h, ce:ce + 1]).then_inc(cdec_ready, 1)
                    j = J["kcT", d, h]
                    copy(j, kcdtok.rearrange("p t n -> p (t n)"), TC)
                    j = J["s0c", d, h]
                    copy(j, state[:, 0], P)
                    for L in range(LEVELS):
                        m = n * LEVELS + L
                        if (n, L) in fills:
                            row_mod(*fills[n, L])
                        act.wait_ge(diff_ready, m + 1)
                        step(S.activation(lvE[:, m % 2], lvE[:, m % 2], ACT.Abs))
                        S.activation(lvE[:, m % 2], lvE[:, m % 2], ACT.Exp, scale=-1.0).then_inc(decay_ready, 1)
                    if n:
                        j = J["ho", (1, 0)[(n - 1) // HH], (n - 1) % HH]
                        wait_full(j)
                    S.activation(qdec, hb[d][:, h], ACT.Exp)
                    for c in range(NC):
                        e = c * CH + (0 if d else CH - 1)
                        cc = slice(c * CH, (c + 1) * CH)
                        ins = S.activation(kdec[:, cc], hb[d][:, h, cc], ACT.Exp, scale=-1.0, bias=hb[d][:, h, e:e + 1])
                    ins.then_inc(ends_ready, 1)
                    copy(J["kdT", d, h], kdtok.rearrange("p c n -> p (c n)"))
                    if d == 1:
                        copy(J["ho", d, h], ho[:, h])
                    n += 1
            for h in range(HH):
                j = J["ho", 0, h]
                act.wait_ge(free[j.lead], j.count)
                S.activation(sq[:, h], ho[:, h], ACT.Square).then_inc(sq_ready, 1)
            for h in range(HH):
                j = J["ssq", h]
                act.wait_ge(free[j.lead], j.count)
                S.activation(root_h[:, h], root_h[:, h], ACT.Sqrt).then_inc(hroot_out, 1)

            def squares(nth, x_count):
                act.wait_ge(x_ready, x_count)
                if nth == 2:
                    for b in (6, 7):
                        act.wait_ge(free[b], loop_base[0][b] + LOOP_PER[b] * E // 2)
                for t in range(TT):
                    n = TT + CT + TT * (nth - 1) + t
                    act.wait_ge(squares_ready, n)
                    S.activation(junk_moe, xs[:, t], ACT.Square, accum_out=small[:, 8 + t:9 + t]).then_inc(squares_ready, 1)
                act.wait_ge(means_ready, nth + 1)
                S.activation(rstd_(small, TT), rstd_(small, TT), ACT.Sqrt).then_inc(roots_ready, 1)

            def moe(l):
                squares(1 + 2 * l, 8 + 8 * l)
                for k in range(0, KT, 2):
                    modulate(J["h2T", l, k], h2T, k, scaleA[:, 2 + l], modc[:, l, 3], T)
                j = J["logit", l]
                act.wait_ge(free[j.lead], j.count)
                S.activation(aff[:, :, :], aff[:, :, :], ACT.Exp).then_inc(logit_exp, 1)
                copy(J["grow2", l], grow[:, :], D)
                base = loop_base[l]
                with act.Fori(0, E // 2) as i:
                    def wait_use(b, nth):
                        act.wait_ge(full[b], i * LOOP_PER[b] + (base[b] + nth + 1))
                        return bank(b)

                    g = wait_use(4, 0)
                    for k in range(4):
                        ins = S.activation(xe[:, k], g[:, k * P:(k + 1) * P], ACT.Identity,
                                           bias=modc[:, l, 3, k:k + 1], scale=scaleA[:, 2 + l, k:k + 1])
                    ins.then_inc(free[4], 1)
                    S.activation(spread, wait_use(6, 0), ACT.Copy).then_inc(free[6], 1)
                    wait_use(0, 0)
                    S.activation(sil, psf[:, 0:1024], ACT.Silu).then_inc(free[0], 1)
                    S.activation(actT[:, 0:4].rearrange("p k n -> p (k n)"), wait_use(4, 1), ACT.Copy).then_inc(free[4], 1)

            copy(J["grow", 0], grow[:, :], D)
            if upto < 5:
                return
            moe(0)
            squares(2, 8)
            for k in range(0, KT, 2):
                modulate(J["h3T", k], hT, k, scaleA[:, 1], modc[:, 1, 0], T)
            for f in range(KT):
                copy(J["conv", "b", f], bT[:, f])
            for f in range(KT):
                copy(J["conv", "c", f], cT[:, f])
            copy(J["grow", 1], grow[:, :], D)
            moe(1)

        @block.gpsimd
        def _(pool):
            if upto < 3:
                return
            n = 0
            pool.wait_ge(b_ready, 4 * HH)
            for h in range(HH):
                j = J["hq", h]
                pool.wait_ge(full[j.lead], j.count)
            for d in (1, 0):
                for h in range(HH):
                    for L in range(LEVELS):
                        m = n * LEVELS + L
                        half = CH >> (L + 1)
                        if m >= 2:
                            pool.wait_ge(lv_ready, m - 1)
                        src = hb[d][:, h].rearrange("p (b w) -> p b w", w=2 * half)
                        mid = src[:, :, half - 1 + d:half + d].broadcast_to((P, T // (2 * half), 2 * half))
                        nc.gpsimd.tensor_tensor(lvE[:, m % 2].rearrange("p (b w) -> p b w", w=2 * half), src, mid,
                                                ALU.subtract).then_inc(diff_ready, 1)
                    n += 1


def rstd_(small, n):
    return small[:, 16:16 + n]


INPUTS = ["x", "c", "ctx", "c_ctx", "mod_w", "mod_b", "norm1_g", "norm2_g", "even_w_in", "even_w_out",
          "hgrn_norm_g", "diff_qnorm_g", "diff_knorm_g", "diff_lambda", "diff_subln_g", "conv_w_in",
          "conv_w", "conv_w_out", "router_w", "exp_w_gate", "exp_w_up", "exp_w_down"]


def shape_constants():
    n = AD // 2
    inv = (1.0 / (ROPE_THETA ** (np.arange(0, n, 2, dtype=np.float32) / np.float32(n)))).astype(np.float32)
    tok = np.arange(T)
    cos, sin = np.zeros((T, AD), np.float32), np.zeros((T, AD), np.float32)
    for axis, pos in enumerate((tok // GRID_W, tok % GRID_W)):
        ang = pos.astype(np.float32)[:, None] * inv[None, :]
        for w in range(2):
            at = slice(axis * n + w * (n // 2), axis * n + (w + 1) * (n // 2))
            cos[:, at] = np.cos(ang)
            sin[:, at] = np.sin(ang) * (-1.0, 1.0)[w]
    s = np.arange(CH)[:, None]
    t = np.arange(CH)[None, :]
    masks = np.zeros((P, 2, LEVELS + 1, CH), np.float32)
    for L in range(LEVELS):
        half = CH >> (L + 1)
        same = s // (2 * half) == t // (2 * half)
        masks[:, 0, L] = same & (s % (2 * half) < half) & (t % (2 * half) >= half)
        masks[:, 1, L] = same & (s % (2 * half) >= half) & (t % (2 * half) < half)
    masks[:, :, LEVELS] = (s == t)[:, None, :]

    def lay(v):
        return np.ascontiguousarray(v.reshape(TT, P, AD).transpose(1, 0, 2))

    return {"c_ident": np.eye(P, dtype=np.float32), "c_cos": lay(cos), "c_sin": lay(sin),
            "c_iota": np.tile(np.arange(CAP, dtype=np.float32), (P, 1)), "c_masks": masks.reshape(P, -1)}


def program(nc, arrays, stop=None, tap=None, extra_out=()):
    a = {}
    for name, v in arrays.items():
        a[name] = nc.dram_tensor(name, v.shape, mybir.dt.from_np(v.dtype), kind="ExternalInput").ap()
    out = nc.dram_tensor("out_x", (1, T, D), F32, kind="ExternalOutput").ap()
    extra = {n: nc.dram_tensor(n, s, F32, kind="ExternalOutput").ap() for n, s in extra_out}
    if tap is not None:
        build(nc, a, out, stop, lambda sp, loc: tap(sp, loc, extra))
    else:
        build(nc, a, out)


def kernel(**inputs):
    import concourse.bacc as bacc
    from concourse.bass_utils import run_bass_kernel_spmd as run

    arrays = {n: np.ascontiguousarray(inputs[n]) for n in INPUTS}
    arrays.update(shape_constants())
    nc = bacc.Bacc("TRN2", target_bir_lowering=False, num_devices=1)
    program(nc, arrays)
    r = run(nc, [arrays], core_ids=[0])
    return r.results[0]["out_x"]
```

```python
from contextlib import ExitStack
import math

import numpy as np

import concourse.bass as bass
from concourse import mybir

P = 128
D = 1024
T = 512
TC = 256
KT = D // P
TT = T // P
CT = TC // P
GRID_W = 64
HH = 4
HD = 128
AH = 4
AD = 64
CH = 128
NC = T // CH
LEVELS = 7
E = 16
CAP = 2 * T // E
EPS = 1e-6
LAM_INIT = 0.8 - 0.6 * math.exp(0.0)
ROPE_THETA = 10000.0
SLOTS = 3

F32 = mybir.dt.float32
U8 = mybir.dt.uint8
ALU = mybir.AluOpType
ACT = mybir.ActivationFunctionType
AX = mybir.AxisListType.X

KB = 256


class Job:

    def __init__(self, lead, banks, count, owners):
        self.lead, self.banks, self.count, self.owners = lead, banks, count, owners


class BankPlan:

    def __init__(self):
        self.used = [0] * 8
        self.owner = [None] * 8

    def job(self, *banks):
        lead = banks[0]
        self.used[lead] += 1
        owners = []
        for b in banks:
            if self.owner[b] is not None and self.owner[b] not in owners:
                owners.append(self.owner[b])
        j = Job(lead, banks, self.used[lead], owners)
        for b in banks:
            self.owner[b] = j
        return j

    def loop(self, per, leads, times):
        base = list(self.used)
        for b in range(8):
            self.used[b] += per[b] * times
        for b in range(8):
            self.owner[b] = Job(leads[b], (b,), self.used[leads[b]], [])
        return base


class Chain:

    def __init__(self, eng, sem):
        self.eng, self.sem, self.n, self.base, self.turn, self.per = eng, sem, 0, 0, None, 0

    def __call__(self, ins):
        self.n += 1
        ins.then_inc(self.sem, 1)
        if self.turn is None:
            self.eng.wait_ge(self.sem, self.n)
        else:
            self.eng.wait_ge(self.sem, self.turn * self.per + self.n)

    def enter(self, turn, per):
        self.base, self.turn, self.per = self.n, turn, per

    def leave(self, times):
        assert self.n - self.base == self.per, (self.n - self.base, self.per)
        self.n = self.base + self.per * times
        self.turn = None


def build(nc, a, out, stop=None, tap=None):
    bp = BankPlan()
    J = {}
    J["colsA"] = bp.job(0)
    J["colsB"] = bp.job(1)
    mods0 = [(0, 0), (0, 1)]
    mods1 = [(0, j) for j in range(2, 6)] + [(1, j) for j in range(6)]
    for m in mods0:
        for half in range(2):
            J["modr", m, half] = bp.job(2 + half)
            J["modc", m, half] = bp.job(2 + half)
    for kt in range(KT):
        J["hT", kt] = bp.job([4, 5, 6, 7][kt % 4])
    for kt in range(KT):
        J["hcT", kt] = bp.job([4, 5, 6, 7][kt % 4])
    n = 0
    for t in range(TT + CT):
        J["dk", t] = bp.job(n % 4); n += 1
    for t in range(TT + CT):
        J["dv", t] = bp.job(n % 4); n += 1
    for h in range(HH):
        J["gate", h] = bp.job(n % 4); n += 1
    for t in range(TT):
        J["dq", t] = bp.job(n % 4); n += 1
    J["hv", 0] = bp.job(7)
    for h in range(AH):
        J["qT", h] = bp.job(6)
        J["kT", h] = bp.job(4, 5)
    att = [(h, t) for h in range(AH) for t in range(TT)]
    hv_part = {3 * (t - 1) + i: (t, ks) for t in range(1, TT + CT)
               for i, ks in enumerate(((0, 1, 2), (3, 4, 5), (6, 7)))}
    assert len(hv_part) <= len(att)

    def score_jobs(h, t):
        J["s0", h, t] = bp.job(0, 1)
        J["s1", h, t] = bp.job(2, 3)

    score_jobs(0, 0)
    for n, (h, t) in enumerate(att):
        if n + 1 < len(att):
            score_jobs(*att[n + 1])
        if n in hv_part and hv_part[n][1][0] == 0:
            J["hv", hv_part[n][0]] = bp.job(7)
        J["wT", h, t] = bp.job(4, 5)
        J["o", h, t] = bp.job(6)
    for h in range(AH):
        J["oT", h] = bp.job(h)
    n = 0
    for d in (1, 0):
        for h in range(HH):
            J["zc", d, h] = bp.job(n % 4); n += 1
        for h in range(HH):
            J["z", d, h] = bp.job(n % 4); n += 1
        if d == 0:
            for h in range(HH):
                J["hq", h] = bp.job(n % 4); n += 1
    halves = [(m, half) for m in mods1 for half in range(2)]
    fills = {3 * f: mh for f, mh in enumerate(halves)}
    heads = [(d, h) for d in (1, 0) for h in range(HH)]
    SLOT = LEVELS + 1
    assert 3 * (len(halves) - 1) + 5 < SLOT * len(heads)

    def tail_jobs(d, h):
        J["ho", d, h] = bp.job(6)
        for c in range(NC - 1):
            J["kv", d, h, c] = bp.job(5)

    for n, (d, h) in enumerate(heads):
        for L in range(SLOT):
            p = n * SLOT + L
            if p - 4 in fills:
                J[("modc",) + fills[p - 4]] = bp.job(3)
            if p in fills:
                J[("modr",) + fills[p]] = bp.job(7)
            if L == 1:
                J["kcT", d, h] = bp.job(4)
            if L == 5:
                J["s0c", d, h] = bp.job(5)
            if L == 7:
                J["kdT", d, h] = bp.job(4)
            J["sc", d, h, L] = bp.job(p % 3)
            if L == 1 and n:
                tail_jobs(*heads[n - 1])
    tail_jobs(*heads[-1])
    for h in range(HH):
        J["ssq", h] = bp.job(h)

    def out_jobs(l):
        J["grow", l] = bp.job(4, 5)
        for t in range(TT):
            for half in range(2):
                J["y", l, t, half] = bp.job((2 * t + half) % 4)

    LOOP_PER = [2, 0, 1, 0, 2, 2, 5, 4]
    LOOP_LEAD = [0, 0, 2, 2, 4, 5, 6, 7]
    loop_base = {}

    def moe_jobs(l):
        for kt in range(KT):
            J["h2T", l, kt] = bp.job(kt)
        J["router", l] = bp.job(1)
        J["logit", l] = bp.job(0)
        J["affT", l] = bp.job(1)
        J["slotT", l] = bp.job(2)
        J["grow2", l] = bp.job(6, 7)
        loop_base[l] = bp.loop(LOOP_PER, LOOP_LEAD, E // 2)

    out_jobs(0)
    moe_jobs(0)
    for kt in range(KT):
        J["h3T", kt] = bp.job(kt)
    n = 0
    for part in "bcv":
        for f in range(KT):
            J["conv", part, f] = bp.job(n % 8); n += 1
    out_jobs(1)
    moe_jobs(1)

    def w_in(j):
        return a["even_w_in"][0][:, j * D:(j + 1) * D]

    chunks = {}
    stream = []
    slot_last = {}
    slot_used = [0] * SLOTS

    def chunk(name, slot, src, last_job):
        slot_used[slot] += 1
        chunks[name] = (slot, slot_used[slot])
        stream.append((slot, src, slot_last.get(slot), name))
        slot_last[slot] = last_job

    n = 0
    for m in mods0:
        chunk(("mod", m), (n + 1) % 2, a["mod_w"][m[0]][:, m[1] * D:(m[1] + 1) * D], J["modr", m, 1]); n += 1
    chunk("w3", (n + 1) % 2, w_in(3), J["dv", TT + CT - 1]); n += 1
    chunk("w2", (n + 1) % 2, w_in(2), J["dq", TT - 1]); n += 1
    chunk("w1", (n + 1) % 2, w_in(1), J["z", 1, HH - 1]); n += 1
    chunk("w0", (n + 1) % 2, w_in(0), J["hq", HH - 1]); n += 1
    for m in mods1:
        chunk(("mod", m), (n + 1) % 2, a["mod_w"][m[0]][:, m[1] * D:(m[1] + 1) * D], J["modr", m, 1]); n += 1
    chunk("wo", (n + 1) % 2, a["even_w_out"][0], J["y", 0, TT - 1, 1]); n += 1
    assert chunks["wo"][0] == 1
    head0 = list(stream)
    stream.clear()

    def experts(l):
        first = [slot_last.get(s) for s in range(3)]
        b = loop_base[l]
        slot_last[0] = slot_last[1] = slot_last[2] = Job(0, (0,), b[0] + LOOP_PER[0] * E // 2, [])
        return first

    first0 = experts(0)
    chunk("cb", 1, a["conv_w_in"][0][:, 0:D], J["conv", "b", KT - 1])
    chunk("cc", 2, a["conv_w_in"][0][:, D:2 * D], J["conv", "c", KT - 1])
    chunk("cv", 0, a["conv_w_in"][0][:, 2 * D:3 * D], J["conv", "v", KT - 1])
    chunk("co", 1, a["conv_w_out"][0], J["y", 1, TT - 1, 1])
    head1 = list(stream)
    first1 = experts(1)

    with ExitStack() as ctx:
        def sb(name, shape, dt=F32):
            return ctx.enter_context(nc.sbuf_tensor(name, shape, dt))

        def sem(name):
            return ctx.enter_context(nc.semaphore(name))

        ring = sb("ring", [P, SLOTS, KT, D])
        annex = ring[:, 2, :, :].rearrange("p k n -> p (k n)")
        room = sb("room", [P, 92 * KB])
        ident = sb("ident", [P, P])
        rope_sin = sb("rope_sin", [P, TT, AD])
        iota = sb("iota", [P, CAP])
        masks = sb("masks", [P, 2, LEVELS + 1, CH], U8)
        ones = sb("ones", [P, TC])
        reset = sb("reset", [P, 2, T])
        rowsA = room[:, 60 * KB:60 * KB + P]
        rowsB = room[:, 61 * KB:61 * KB + P]
        colsA = sb("colsA", [P, P])
        colsB = sb("colsB", [P, 96])
        silc = sb("silc", [P, KT, 32])
        fold = sb("fold", [P, E])
        astat = sb("astat", [P, 16, 8])
        modc = sb("modc", [P, 2, 6, KT])
        modx = sb("modx", [P, 2, KT])
        scaleA = sb("scaleA", [P, 5, KT])
        grow = sb("grow", [P, D])
        small = sb("small", [P, 256])
        gains = sb("gains", [P, AD + AD + 2 * AD])
        slotc = sb("slotc", [P, TT, E])
        aff = sb("aff", [P, TT, E])
        router = sb("router", [P, KT, 32])

        def view(at_kb, *shape, base=None):
            base = room if base is None else base
            size = 1
            for s in shape:
                size *= s
            v = base[:, int(at_kb * KB):int(at_kb * KB) + size]
            if len(shape) == 1:
                return v
            names = "abcd"[:len(shape)]
            spec = "p (" + " ".join(names) + ") -> p " + " ".join(names)
            return v.rearrange(spec, **{k: s for k, s in zip(names[:-1], shape[:-1])})

        xs = view(0, TT, D)
        xn = view(16, TT, D)
        x6 = view(16, TT + CT, D)
        hT = view(76, KT, T)
        hcT = view(68, KT, TC)
        yT = view(52, KT, T)
        qtok = view(0, TT, T)
        ktok = view(8, TT + CT, T)
        vtok = view(20, TT + CT, T)
        qT = view(32, AH, T)
        kT = view(40, AH, T + TC)
        prob = view(0, 2, 2, T + TC)
        wgt = view(12, T + TC)
        wT = view(15, CT + TT, P)
        oall = view(16, TT, T, base=annex)
        junk = view(0, D, base=annex)
        tsq = view(4, 2, T, base=annex)
        trot = view(8, 2, T, base=annex)
        ta = view(12, T, base=annex)
        hv = view(0, TT + CT, T, base=annex)
        hq = view(12, HH, T)
        hb = [view(20, HH, T), view(36, HH, T)]
        hk = [view(28, HH, T), view(44, HH, T)]
        ho = view(0, HH, T)
        cb = [view(12, HH, TC, base=annex), view(8, HH, TC)]
        ck = [view(16, HH, TC, base=annex), view(20, HH, TC, base=annex)]
        sqo = view(14, P, base=annex)
        spl = view(24, 2, T, base=annex)
        lvE = [view(68, T), reset[:, 0], reset[:, 1]]
        lvQ = [view(70, T), view(72, T), view(74, T)]
        lvK = [view(76, T), view(78, T), view(26, T, base=annex)]
        qdec = view(80, T)
        kdec = view(82, T)
        kdtok = view(84, NC, P)
        sc = view(86, T)
        state = view(88, 2, P)
        masks_in = view(16, 2 * (LEVELS + 1) * CH, base=annex)
        modrow = view(28, D, base=annex)
        lamv = view(24, 4 * AD, base=annex)
        rope_cos = view(25, TT, AD, base=annex)
        kcdec = view(24, TC, base=annex)
        kcdtok = view(25, CT, P, base=annex)
        sq = view(36, HH, T)
        root_h = view(44, HH, T)
        h2T = view(76, KT, T)
        sel = view(41, 4, T)
        onehot = view(49, TT, 2, CAP)
        gated = view(51, TT, 2, CAP)
        spread = view(53, T)
        xe = view(55, KT, P)
        sil = view(59, D)
        parts = view(59, T)
        actb = view(32, D)
        actT = view(63, KT, P)
        ye = view(67, D)
        junk_moe = view(36, D)
        xtmp = view(70, 2, T)
        bT = view(16, KT, T)
        cT = view(32, KT, T)
        uT = view(48, T + 2)
        vT = view(51, T)
        ycT = view(54, KT, T)

        ps = ctx.enter_context(nc.psum_tensor("ps", [P, 8, 512], F32))
        psf = ps[:, :, :].rearrange("p b n -> p (b n)")

        def bank(b, n=512):
            return ps[:, b, 0:n]

        def half_slot(q):
            return ring[:, q // 2, 4 * (q % 2):4 * (q % 2) + 4, :]

        full = [sem(f"bank_full{b}") for b in range(8)]
        free = [sem(f"bank_free{b}") for b in range(8)]
        ring_full = [sem(f"ring_full{s}") for s in range(SLOTS)]
        consts_in = sem("consts_in")
        rows_in = sem("rows_in")
        x_in = sem("x_in")
        x_again = sem("x_again")
        router_in = [sem("router_in0"), sem("router_in1")]
        cols_ready = sem("cols_ready")
        silc_ready = sem("silc_ready")
        squares_ready = sem("squares_ready")
        means_ready = sem("means_ready")
        roots_ready = sem("roots_ready")
        xn_ready = sem("xn_ready")
        scale_ready = sem("scale_ready")
        act_step = sem("act_step")
        dve_step = sem("dve_step")
        lam_dots = sem("lam_dots")
        lam_exps = sem("lam_exps")
        qk_squares = sem("qk_squares")
        qk_means = sem("qk_means")
        qk_roots = sem("qk_roots")
        qk_normed = sem("qk_normed")
        max_ready = sem("max_ready")
        wgt_ready = sem("wgt_ready")
        o_squares = sem("o_squares")
        o_means = sem("o_means")
        o_roots = sem("o_roots")
        o_normed = sem("o_normed")
        log_ready = sem("log_ready")
        hk_ready = sem("hk_ready")
        b_ready = sem("b_ready")
        cdec_ready = sem("cdec_ready")
        kcd_ready = sem("kcd_ready")
        diff_ready = sem("diff_ready")
        decay_ready = sem("decay_ready")
        lv_ready = sem("lv_ready")
        ends_ready = sem("ends_ready")
        qdec_ready = sem("qdec_ready")
        sq_ready = sem("sq_ready")
        y_hgrn = sem("y_hgrn")
        hroot_out = sem("hroot_out")
        x_ready = sem("x_ready")
        logit_exp = sem("logit_exp")
        aff_ready = sem("aff_ready")
        slot_ready = sem("slot_ready")
        onehot_ready = sem("onehot_ready")
        gated_ready = sem("gated_ready")
        gates_half = sem("gates_half")
        ups_half = sem("ups_half")
        downs_half = sem("downs_half")
        exp_full = [sem(f"exp_full{q}") for q in range(6)]
        ycT_ready = sem("ycT_ready")
        out_done = sem("out_done")

        stops = ["A", "B", "C", "D", "M0", "X"]
        upto = stops.index(stop) if stop else 99

        locals_of_build = locals()
        block = ctx.enter_context(nc.Block())

        @block.sync
        def _(sp):
            def load_chunk(slot, src, owner):
                if owner is not None:
                    sp.wait_ge(full[owner.lead], owner.count)
                sp.dma_start(ring[:, slot], src.rearrange("(k p) n -> p k n", p=P)).then_inc(ring_full[slot], 16)

            for dst, src in ((ident, "c_ident"), (rope_cos, "c_cos"), (rope_sin, "c_sin"),
                             (iota, "c_iota"), (masks_in, "c_masks")):
                sp.dma_start(dst if dst is masks_in or dst is rope_cos else dst[:], a[src]).then_inc(consts_in, 16)
            rows = [(0, a["c"].rearrange("b (k p) -> (b k) p", p=P)),
                    (8, a["c_ctx"].rearrange("(k p) -> k p", p=P)),
                    (16, a["norm1_g"].rearrange("l (k p) -> (l k) p", p=P)),
                    (32, a["norm2_g"].rearrange("l (k p) -> (l k) p", p=P)),
                    (48, a["hgrn_norm_g"][0]),
                    (52, a["conv_w"][0].rearrange("w (k p) -> (w k) p", p=P))]
            for at, src in rows:
                sp.dma_start(rowsA[at:at + src.shape[0], :], src).then_inc(rows_in, 16)
            sp.dma_start(rowsB[0:96, :], a["mod_b"].rearrange("l (k p) -> (l k) p", p=P)).then_inc(rows_in, 16)
            for t in range(CT):
                sp.dma_start(x6[:, TT + t], a["ctx"][0, t * P:(t + 1) * P, :]).then_inc(x_in, 16)
            for t in range(TT):
                sp.dma_start(x6[:, t], a["x"][0, t * P:(t + 1) * P, :]).then_inc(x_in, 16)
            for at, n, src in ((0, AD, a["diff_qnorm_g"]), (AD, AD, a["diff_knorm_g"]), (2 * AD, 2 * AD, a["diff_subln_g"])):
                sp.dma_start(gains[:, at:at + n], src.broadcast_to((P, n))).then_inc(rows_in, 16)
            sp.dma_start(lamv, a["diff_lambda"].rearrange("a r n -> a (r n)").broadcast_to((P, 4 * AD))).then_inc(rows_in, 16)
            for slot, src, owner, name in head0:
                if (upto < 1 and name == "w3") or (upto < 3 and name == "w0"):
                    break
                load_chunk(slot, src, owner)
            if upto >= 5:
                sp.wait_ge(full[first0[0].lead], first0[0].count)
                for e in range(2):
                    sp.dma_start(half_slot(e), a["exp_w_gate"][0, e, 0:512, :].rearrange("(k p) n -> p k n", p=P)).then_inc(exp_full[e], 16)
            if upto >= 4:
                sp.wait_ge(y_hgrn, HH)
                sp.dma_start(xs, a["x"][0].rearrange("(t p) d -> p t d", p=P)).then_inc(x_again, 16)

            def load_experts(l, first):
                tables = (a["exp_w_gate"][l], a["exp_w_up"][l], a["exp_w_down"][l])
                sp.dma_start(router[:, :, 0:E], a["router_w"][l].rearrange("(k p) e -> p k e", p=P)).then_inc(router_in[l], 16)
                base = loop_base[l]

                def load(j, i, turn=0):
                    halves = tables[j // 4].rearrange("e (h r) n -> (e h) r n", h=2)
                    at = i * 4 + (4 * turn + 2 * (j % 2) + (j // 2) % 2)
                    src = halves[bass.ds(at, 1)].rearrange("o (k p) n -> p (o k) n", p=P)
                    sp.dma_start(half_slot(j % 6), src).then_inc(exp_full[j % 6], 16)

                def second_half(i):
                    sp.wait_ge(gates_half, i + (l * 8 + 1))
                    load(6, i)
                    load(7, i)
                    sp.wait_ge(full[0], i * 2 + (base[0] + 1))
                    load(8, i)
                    load(9, i)
                    sp.wait_ge(ups_half, i + (l * 8 + 1))
                    load(10, i)
                    load(11, i)

                for j in range(2 * (1 - l), 6):
                    if first[j // 2] is not None:
                        sp.wait_ge(full[first[j // 2].lead], first[j // 2].count)
                    load(j, 0)
                with sp.Fori(0, E // 2 - 1) as i:
                    second_half(i)
                    sp.wait_ge(full[2], i + (base[2] + 1))
                    load(0, i, 1)
                    load(1, i, 1)
                    sp.wait_ge(downs_half, i + (l * 8 + 1))
                    load(2, i, 1)
                    load(3, i, 1)
                    sp.wait_ge(full[0], i * 2 + (base[0] + 2))
                    load(4, i, 1)
                    load(5, i, 1)
                second_half(E // 2 - 1)

            if upto >= 5:
                load_experts(0, first0)
                for slot, src, owner, name in head1:
                    load_chunk(slot, src, owner)
                sp.wait_ge(full[1], J["router", 0].count)
                load_experts(1, first1)
                for b in (6, 7):
                    sp.wait_ge(free[b], loop_base[1][b] + LOOP_PER[b] * E // 2)
                sp.dma_start(out[0].rearrange("(t p) d -> p t d", p=P), xs).then_inc(out_done, 16)
                sp.wait_ge(out_done, 16)
            if tap is not None:
                tap(sp, dict(locals_of_build))

        @block.tensor
        def _(pe):
            def open_(j):
                for o in j.owners:
                    pe.wait_ge(free[o.lead], o.count)
                return j

            def taken(j):
                pe.wait_ge(free[j.lead], j.count)

            def arrived(name):
                slot, n = chunks[name]
                pe.wait_ge(ring_full[slot], 16 * n)
                return ring[:, slot]

            def mod(m, half):
                j = open_(J["modr", m, half])
                w = arrived(("mod", m))
                for k in range(KT):
                    q = k % 4
                    mm = nc.tensor.matmul(ps[32 * q:32 * q + 32, j.lead, :], silc[:, k, :],
                                          w[:, k, half * 512:(half + 1) * 512], start=(k < 4), stop=(k >= 4))
                mm.then_inc(full[j.lead], 1)

            def mod_turn(m, half):
                taken(J["modr", m, half])
                j = open_(J["modc", m, half])
                for q in range(4):
                    mm = nc.tensor.matmul(bank(j.lead)[:, 2 * q:2 * q + 2], modrow[:, (4 * half + q) * P:(4 * half + q + 1) * P],
                                          fold[:, 0:2], start=True, stop=True)
                mm.then_inc(full[j.lead], 1)

            def tok_product(j, h, tile, w, n0):
                open_(j)
                for k in range(KT):
                    mm = nc.tensor.matmul(bank(j.lead), h[:, k, tile * P:(tile + 1) * P], w[:, k, n0:n0 + 512],
                                          start=(k == 0), stop=(k == KT - 1))
                mm.then_inc(full[j.lead], 1)

            def feat_product(j, h, n, w, n0):
                open_(j)
                for k in range(KT):
                    mm = nc.tensor.matmul(bank(j.lead, n), w[:, k, n0:n0 + P], h[:, k, 0:n],
                                          start=(k == 0), stop=(k == KT - 1))
                mm.then_inc(full[j.lead], 1)

            def turn(j, pieces):
                open_(j)
                at = 512 * j.lead
                for piece in pieces:
                    rows = piece.shape[0]
                    cols = piece.shape[1]
                    mm = nc.tensor.transpose(psf[0:cols, at:at + rows], piece, ident[0:rows, 0:rows])
                    at += rows
                mm.then_inc(full[j.lead], 1)

            pe.wait_ge(consts_in, 16 * 5)
            pe.wait_ge(rows_in, 16 * 11)
            turn(J["colsA"], [rowsA[0:76, :]])
            turn(J["colsB"], [rowsB[0:96, :]])
            pe.wait_ge(silc_ready, 1)
            for m in mods0:
                for half in range(2):
                    mod(m, half)
                    mod_turn(m, half)
            pe.wait_ge(xn_ready, TT + CT)
            for k in range(KT):
                turn(J["hT", k], [x6[:, t, k * P:(k + 1) * P] for t in range(TT)])
            for k in range(KT):
                turn(J["hcT", k], [x6[:, TT + t, k * P:(k + 1) * P] for t in range(CT)])
            if upto < 1:
                return
            for k in range(KT):
                taken(J["hT", k])
                taken(J["hcT", k])
            w = arrived("w3")
            for name, n0 in (("dk", 0), ("dv", 512)):
                for t in range(TT):
                    tok_product(J[name, t], hT, t, w, n0)
                for t in range(CT):
                    tok_product(J[name, TT + t], hcT, t, w, n0)
            w = arrived("w2")
            for h in range(HH):
                feat_product(J["gate", h], hT, T, w, h * P)
            for t in range(TT):
                tok_product(J["dq", t], hT, t, w, 512)
            w_hv = arrived("w1")
            tok_product(J["hv", 0], hT, 0, w_hv, 512)
            pe.wait_ge(qk_normed, 2 * TT + CT)
            for h in range(AH):
                turn(J["qT", h], [qtok[:, t, h * P:(h + 1) * P] for t in range(TT)])
                turn(J["kT", h], [ktok[:, t, h * P:(h + 1) * P] for t in range(TT + CT)])
            for h in range(AH):
                taken(J["qT", h])
                taken(J["kT", h])
            for t in range(TT + CT):
                taken(J["dv", t])

            def scores(h, t):
                for m in range(2):
                    j = open_(J[f"s{m}", h, t])
                    f = slice(m * AD, (m + 1) * AD)
                    for k0, kn in ((0, T), (T, TC)):
                        mm = nc.tensor.matmul(psf[:, 512 * j.lead + k0:512 * j.lead + k0 + kn],
                                              qT[f, h, t * P:(t + 1) * P], kT[f, h, k0:k0 + kn],
                                              start=True, stop=True)
                    mm.then_inc(full[j.lead], 1)

            scores(0, 0)
            for n, (h, t) in enumerate(att):
                if n + 1 < len(att):
                    scores(*att[n + 1])
                pe.wait_ge(wgt_ready, n + 1)
                turn(J["wT", h, t], [wgt[:, k * P:(k + 1) * P] for k in range(TT + CT)])
                if n in hv_part:
                    tile, ks = hv_part[n]
                    j = J["hv", tile]
                    if ks[0] == 0:
                        open_(j)
                    left, at = (hT, tile) if tile < TT else (hcT, tile - TT)
                    for k in ks:
                        mm = nc.tensor.matmul(bank(j.lead), left[:, k, at * P:(at + 1) * P], w_hv[:, k, 512:1024],
                                              start=(k == 0), stop=(k == KT - 1))
                    if k == KT - 1:
                        mm.then_inc(full[j.lead], 1)
                taken(J["wT", h, t])
                j = open_(J["o", h, t])
                for k in range(TT + CT):
                    mm = nc.tensor.matmul(bank(j.lead, P), wT[:, k, :], vtok[:, k, h * P:(h + 1) * P],
                                          start=(k == 0), stop=(k == TT + CT - 1))
                mm.then_inc(full[j.lead], 1)
            pe.wait_ge(o_normed, TT)
            for h in range(AH):
                turn(J["oT", h], [oall[:, t, h * P:(h + 1) * P] for t in range(TT)])
            if upto < 3:
                return
            for d, name, n0 in ((1, "w1", 0), (0, "w0", 512)):
                w = arrived(name)
                for h in range(HH):
                    feat_product(J["zc", d, h], hcT, TC, w, n0 + h * P)
                for h in range(HH):
                    feat_product(J["z", d, h], hT, T, w, n0 + h * P)
            for h in range(HH):
                feat_product(J["hq", h], hT, T, w, h * P)
            for t in range(TT + CT):
                taken(J["hv", t])
            for h in range(HH):
                taken(J["hq", h])
            pe.wait_ge(hk_ready, 4 * HH)
            def tail(d, h):
                taken(J["kdT", d, h])
                taken(J["sc", d, h, LEVELS])
                jo = open_(J["ho", d, h])
                order = range(NC) if d == 0 else range(NC - 1, -1, -1)
                for s, c in enumerate(order):
                    cc = slice(c * CH, (c + 1) * CH)
                    if s < NC - 1:
                        j = open_(J["kv", d, h, s])
                        nc.tensor.matmul(bank(j.lead, P), kdtok[:, c, :], hv[:, c, h * P:(h + 1) * P],
                                         start=True, stop=True).then_inc(full[j.lead], 1)
                    nc.tensor.matmul(bank(jo.lead)[:, cc], hv[:, c, h * P:(h + 1) * P], sc[:, cc],
                                     start=True, stop=False)
                    taken(J["kv", d, h, s - 1] if s else J["s0c", d, h])
                    mm = nc.tensor.matmul(bank(jo.lead)[:, cc], state[:, s % 2], qdec[:, cc],
                                          start=False, stop=True)
                mm.then_inc(full[jo.lead], 1)

            for n, (d, h) in enumerate(heads):
                for L in range(SLOT):
                    p = n * SLOT + L
                    if p - 4 in fills:
                        mod_turn(*fills[p - 4])
                    if p in fills:
                        mod(*fills[p])
                    if L == 1:
                        pe.wait_ge(kcd_ready, n + 1)
                        turn(J["kcT", d, h], [kcdec[:, t * P:(t + 1) * P] for t in range(CT)])
                    if L == 5:
                        taken(J["kcT", d, h])
                        j = open_(J["s0c", d, h])
                        for t in range(CT):
                            mm = nc.tensor.matmul(bank(j.lead, P), kcdtok[:, t, :], hv[:, TT + t, h * P:(h + 1) * P],
                                                  start=(t == 0), stop=(t == CT - 1))
                        mm.then_inc(full[j.lead], 1)
                    if L == 7:
                        pe.wait_ge(qdec_ready, n + 1)
                        turn(J["kdT", d, h], [kdec[:, c * CH:(c + 1) * CH] for c in range(NC)])
                    if L < LEVELS:
                        m = n * LEVELS + L
                        pe.wait_ge(lv_ready, m + 1)
                        kk, qq = lvK[m % 3], lvQ[m % 3]
                    else:
                        kk, qq = hk[d][:, h], hq[:, h]
                    j = open_(J["sc", d, h, L])
                    for c in range(NC):
                        cc = slice(c * CH, (c + 1) * CH)
                        mm = nc.tensor.matmul(bank(j.lead)[:, cc], kk[:, cc], qq[:, cc], start=True, stop=True)
                    mm.then_inc(full[j.lead], 1)
                    if L == 1 and n:
                        tail(*heads[n - 1])
            tail(*heads[-1])
            for h in range(HH):
                pe.wait_ge(sq_ready, h + 1)
                j = open_(J["ssq", h])
                nc.tensor.matmul(bank(j.lead), ones[:, 0:P], sq[:, h], start=True, stop=True).then_inc(full[j.lead], 1)

            def grow_row(j, l, which):
                open_(j)
                for k in range(KT):
                    mm = nc.tensor.matmul(psf[:, 512 * j.lead + k * P:512 * j.lead + (k + 1) * P],
                                          modc[:, l, which, k:k + 1].broadcast_to((P, P)), ident[:, :],
                                          start=True, stop=True)
                mm.then_inc(full[j.lead], 1)

            def project_out(l, y, w):
                grow_row(J["grow", l], l, 2)
                w = arrived(w)
                for t in range(TT):
                    for half in range(2):
                        tok_product(J["y", l, t, half], y, t, w, 512 * half)

            pe.wait_ge(y_hgrn, HH)
            for h in range(AH):
                taken(J["oT", h])
            project_out(0, yT, "wo")
            if upto < 5:
                return

            def moe(l):
                pe.wait_ge(xn_ready, TT + CT + TT * (1 + 2 * l))
                for k in range(KT):
                    turn(J["h2T", l, k], [xn[:, t, k * P:(k + 1) * P] for t in range(TT)])
                pe.wait_ge(router_in[l], 16)
                for k in range(KT):
                    taken(J["h2T", l, k])
                j = open_(J["router", l])
                for k in range(KT):
                    q = k % 4
                    mm = nc.tensor.matmul(ps[32 * q:32 * q + 32, j.lead, :], router[:, k, :], h2T[:, k, :],
                                          start=(k < 4), stop=(k >= 4))
                mm.then_inc(full[j.lead], 1)
                taken(j)
                j = open_(J["logit", l])
                for t in range(TT):
                    mm = nc.tensor.matmul(bank(j.lead)[:, t * E:(t + 1) * E], parts[:, t * P:(t + 1) * P], fold[:, :],
                                          start=True, stop=True)
                mm.then_inc(full[j.lead], 1)
                pe.wait_ge(x_ready, 8 * (l + 1))
                grow_row(J["grow2", l], l, 5)
                pe.wait_ge(aff_ready, l + 1)
                turn(J["affT", l], [aff[:, t, :] for t in range(TT)])
                pe.wait_ge(slot_ready, l + 1)
                turn(J["slotT", l], [sel[0:E, 3, t * P:(t + 1) * P] for t in range(TT)])
                taken(J["grow2", l])
                for b in range(8):
                    pe.wait_ge(free[b], loop_base[l][b])
                base = loop_base[l]
                with pe.Fori(0, E // 2) as i:
                    def use(b, nth):
                        pe.wait_ge(free[b], i * LOOP_PER[b] + (base[b] + nth))

                    def made(b, nth):
                        pe.wait_ge(free[b], i * LOOP_PER[b] + (base[b] + nth + 1))

                    def product(b, j, left, nth, half_done):
                        for top in range(2):
                            for e in range(2):
                                q = (j + 2 * top + e) % 6
                                pe.wait_ge(exp_full[q], i * 32 + (l * 256 + 16 * nth[top]))
                            for k in range(4 * top, 4 * top + 4):
                                for half in range(2):
                                    for e in range(2):
                                        w = half_slot((j + 2 * top + e) % 6)
                                        mm = nc.tensor.matmul(ps[e * CAP:(e + 1) * CAP, b + half, :],
                                                              left[:, k, e * CAP:(e + 1) * CAP],
                                                              w[:, k % 4, half * 512:(half + 1) * 512],
                                                              start=(k == 0), stop=(k == KT - 1))
                            mm.then_inc(full[b] if top else half_done, 1)

                    pe.wait_ge(onehot_ready, i + (l * 8 + 1))
                    for half in range(2):
                        use(4 + half, 0)
                        for q in range(4):
                            k = 4 * half + q
                            for t in range(TT):
                                mm = nc.tensor.matmul(bank(4 + half)[:, q * P:(q + 1) * P], xn[:, t, k * P:(k + 1) * P],
                                                      onehot[:, t].rearrange("p e s -> p (e s)"),
                                                      start=(t == 0), stop=(t == TT - 1))
                        mm.then_inc(full[4 + half], 1)
                    use(6, 0)
                    pe.wait_ge(gated_ready, i + (l * 8 + 1))
                    for t in range(TT):
                        mm = nc.tensor.transpose(bank(6)[:, t * P:(t + 1) * P],
                                                 gated[:, t].rearrange("p e s -> p (e s)"), ident[:, :])
                    mm.then_inc(full[6], 1)
                    made(4, 0)
                    made(5, 0)
                    use(0, 0)
                    product(0, 0, xe, (1, 1), gates_half)
                    use(2, 0)
                    product(2, 4, xe, (1, 2), ups_half)
                    made(2, 0)
                    for half in range(2):
                        use(4 + half, 1)
                        for q in range(4):
                            mm = nc.tensor.transpose(bank(4 + half)[:, q * P:(q + 1) * P],
                                                     actb[:, (4 * half + q) * P:(4 * half + q + 1) * P], ident[:, :])
                        mm.then_inc(full[4 + half], 1)
                    use(0, 1)
                    made(4, 1)
                    made(5, 1)
                    product(0, 8, actT, (2, 2), downs_half)
                    made(6, 0)
                    made(0, 1)
                    for t in range(TT):
                        for half in range(2):
                            b = 6 + half
                            use(b, t + 1 - half)
                            nc.tensor.matmul(bank(b), spread[:, t * P:(t + 1) * P], ye[:, half * 512:(half + 1) * 512],
                                             start=True, stop=True).then_inc(full[b], 1)

            moe(0)
            pe.wait_ge(xn_ready, TT + CT + 2 * TT)
            for k in range(KT):
                turn(J["h3T", k], [xn[:, t, k * P:(k + 1) * P] for t in range(TT)])
            for k in range(KT):
                taken(J["h3T", k])
            for part, name in (("b", "cb"), ("c", "cc"), ("v", "cv")):
                w = arrived(name)
                for f in range(KT):
                    feat_product(J["conv", part, f], hT, T, w, f * P)
            pe.wait_ge(ycT_ready, KT)
            project_out(1, ycT, "co")
            moe(1)

        @block.vector
        def _(dve):
            step = Chain(dve, dve_step)
            V = nc.vector

            def wait_full(j):
                dve.wait_ge(full[j.lead], j.count)

            step(V.memset(ones[:, :], 1.0))
            step(V.memset(reset[:, :, :], 1.0))
            step(V.memset(reset[:, 0, 0:T:CH], 0.0))
            step(V.memset(reset[:, 1, CH - 1:T:CH], 0.0))
            dve.wait_ge(consts_in, 16 * 5)
            step(V.tensor_copy(masks[:, :, :, :].rearrange("p d l n -> p (d l n)"), masks_in))
            wait_full(J["colsA"])
            V.tensor_copy(colsA[:, 0:76], bank(0, 76)).then_inc(free[0], 1)
            dve.wait_ge(free[0], 1)
            step(V.memset(silc[:, :, :], 0.0))
            step(V.memset(router[:, :, :], 0.0))
            step(V.tensor_reduce(fold[:, :], ident[:, :].rearrange("p (q w) -> p w q", w=32)[:, 0:E], AX, ALU.add))
            V.tensor_copy(silc[:, :, 0:2].rearrange("p k w -> p w k"), colsA[:, 0:16].rearrange("p (w k) -> p w k", w=2)).then_inc(cols_ready, 1)
            wait_full(J["colsB"])
            V.tensor_copy(colsB[:, :], bank(1, 96)).then_inc(free[1], 1)
            dve.wait_ge(free[1], 1)
            dve.wait_ge(rows_in, 16 * 11)
            lv = lamv.rearrange("p (r n) -> p r n", r=4)
            step(V.tensor_tensor(ta[:, 0:2 * AD].rearrange("p (r n) -> p r n", r=2), lv[:, 0::2], lv[:, 1::2], ALU.mult))
            V.tensor_reduce(small[:, 0:2], ta[:, 0:2 * AD].rearrange("p (r n) -> p r n", r=2), AX, ALU.add).then_inc(lam_dots, 1)
            dve.wait_ge(lam_exps, 1)
            step(V.tensor_tensor(small[:, 4:5], small[:, 2:3], small[:, 3:4], ALU.subtract))
            step(V.tensor_scalar(small[:, 5:6], small[:, 4:5], LAM_INIT, -1.0, ALU.add, ALU.mult))
            step(V.tensor_scalar(gains[:, 2 * AD:4 * AD], gains[:, 2 * AD:4 * AD], 1.0 - LAM_INIT, None, ALU.mult))

            def root(src, dst, n, scale, which):
                sem_in, sem_out, count = which
                V.tensor_scalar(dst, src, scale, EPS, ALU.mult, ALU.add).then_inc(sem_in, 1)
                dve.wait_ge(sem_out, count)
                step(V.reciprocal(dst, dst))

            dve.wait_ge(squares_ready, TT + CT)
            rstd = small[:, 16:16 + TT + CT]
            root(small[:, 8:8 + TT + CT], rstd, TT + CT, 1.0 / D, (means_ready, roots_ready, 1))
            for t in range(TT + CT):
                V.tensor_scalar(x6[:, t], x6[:, t], rstd[:, t:t + 1], None, ALU.mult).then_inc(xn_ready, 1)

            def take_mod(m, half):
                l, jj = m
                j = J["modc", m, half]
                wait_full(j)
                pv = bank(j.lead, KT).rearrange("p (k w) -> p k w", w=2)
                kk = slice(4 * half, 4 * half + 4)
                b0 = (6 * l + jj) * KT + 4 * half
                if l == 0 and jj < 2:
                    step(V.tensor_tensor(modx[:, jj, kk], pv[:, :, 1], colsB[:, b0:b0 + 4], ALU.add))
                V.tensor_tensor(modc[:, l, jj, kk], pv[:, :, 0], colsB[:, b0:b0 + 4], ALU.add).then_inc(free[j.lead], 1)
                dve.wait_ge(free[j.lead], j.count)
                if jj in (1, 4):
                    n = (0 if jj == 1 else 2) + l
                    g0 = (16 if jj == 1 else 32) + l * KT + 4 * half
                    V.scalar_tensor_tensor(scaleA[:, n, kk], modc[:, l, jj, kk], 1.0, colsA[:, g0:g0 + 4],
                                           ALU.add, ALU.mult).then_inc(scale_ready, 1)
                    if m == (0, 1):
                        V.scalar_tensor_tensor(scaleA[:, 4, kk], modx[:, 1, kk], 1.0, colsA[:, g0:g0 + 4],
                                               ALU.add, ALU.mult).then_inc(scale_ready, 1)

            for m in mods0:
                for half in range(2):
                    take_mod(m, half)
            dve.wait_ge(scale_ready, 4)

            def modulate(j, dst, k, gain, shift, n):
                wait_full(j)
                V.tensor_scalar(dst[:, k], bank(j.lead, n), gain[:, k:k + 1], shift[:, k:k + 1],
                                ALU.mult, ALU.add).then_inc(free[j.lead], 1)

            for k in range(1, KT, 2):
                modulate(J["hT", k], hT, k, scaleA[:, 0], modc[:, 0, 0], T)
            for k in range(1, KT, 2):
                modulate(J["hcT", k], hcT, k, scaleA[:, 4], modx[:, 0], TC)
            if upto < 1:
                return
            for n, (arr, t, g0, rot) in enumerate([(ktok, t, AD, t < TT) for t in range(TT + CT)]
                                                  + [(qtok, t, 0, True) for t in range(TT)]):
                x8 = arr[:, t].rearrange("p (g n) -> p g n", n=AD)
                r8 = small[:, 32 + 8 * (n % 2):40 + 8 * (n % 2)]
                dve.wait_ge(qk_squares, n + 1)
                step(V.tensor_reduce(r8, tsq[:, n % 2].rearrange("p (g n) -> p g n", n=AD), AX, ALU.add))
                root(r8, r8, 8, 1.0 / AD, (qk_means, qk_roots, n + 1))
                step(V.tensor_tensor(x8, x8, r8[:, :, None].broadcast_to((P, 8, AD)), ALU.mult))
                gain = gains[:, g0:g0 + AD][:, None, :].broadcast_to((P, 8, AD))
                last = V.tensor_tensor(x8, x8, gain, ALU.mult)
                if rot:
                    step(last)
                    cos8 = rope_cos[:, t][:, None, :].broadcast_to((P, 8, AD))
                    halves = arr[:, t].rearrange("p (g a w n) -> p (g a) w n", a=2, w=2, n=AD // 4)
                    sw = trot[:, 1].rearrange("p (g a w n) -> p (g a) w n", a=2, w=2, n=AD // 4)
                    step(V.tensor_tensor(trot[:, 0].rearrange("p (g n) -> p g n", n=AD), x8, cos8, ALU.mult))
                    for w in range(2):
                        sin8 = rope_sin[:, t].rearrange("p (a w n) -> p a w n", a=2, w=2)[:, :, w]
                        sin8 = sin8[:, None].broadcast_to((P, 8, 2, AD // 4))
                        o4 = sw[:, :, w].rearrange("p (g a) n -> p g a n", a=2)
                        i4 = halves[:, :, 1 - w].rearrange("p (g a) n -> p g a n", a=2)
                        step(V.tensor_tensor(o4, i4, sin8, ALU.mult))
                    last = V.tensor_tensor(arr[:, t], trot[:, 0], trot[:, 1], ALU.add)
                last.then_inc(qk_normed, 1)
            for h in range(AH):
                j = J["qT", h]
                wait_full(j)
                V.tensor_copy(qT[:, h], bank(j.lead)).then_inc(free[j.lead], 1)

            def maxima(n):
                h, t = att[n]
                for m in range(2):
                    j = J[f"s{m}", h, t]
                    wait_full(j)
                    mx = astat[:, n, m:m + 1]
                    step(V.tensor_reduce(mx, psf[:, 512 * j.lead:512 * j.lead + T + TC], AX, ALU.max))
                    V.tensor_scalar(mx, mx, -AD ** -0.5, None, ALU.mult).then_inc(max_ready, 1)

            maxima(0)
            for n, (h, t) in enumerate(att):
                j = J["s1", h, t]
                dve.wait_ge(free[j.lead], j.count)
                j = J["s0", h, t]
                dve.wait_ge(free[j.lead], j.count)
                step(V.reciprocal(astat[:, n, 4:6], astat[:, n, 2:4]))
                step(V.scalar_tensor_tensor(astat[:, n, 6:7], astat[:, n, 5:6], small[:, 5:6], astat[:, n, 2:3],
                                            ALU.mult, ALU.mult))
                if n:
                    jw = J["wT", *att[n - 1]]
                    dve.wait_ge(full[jw.lead], jw.count)
                V.scalar_tensor_tensor(wgt, prob[:, n % 2, 1], astat[:, n, 6:7], prob[:, n % 2, 0],
                                       ALU.mult, ALU.add).then_inc(wgt_ready, 1)
                if n + 1 < len(att):
                    maxima(n + 1)
            dve.wait_ge(o_squares, len(att))
            root(small[:, 80:96], small[:, 80:96], 16, 1.0 / (2 * AD), (o_means, o_roots, 1))
            for t in range(TT):
                o4 = oall[:, t].rearrange("p (h n) -> p h n", h=AH)
                step(V.tensor_tensor(o4, o4, small[:, 80 + 4 * t:84 + 4 * t][:, :, None].broadcast_to((P, AH, P)), ALU.mult))
                V.tensor_tensor(o4, o4, gains[:, 2 * AD:4 * AD][:, None, :].broadcast_to((P, AH, P)),
                                ALU.mult).then_inc(o_normed, 1)
            if upto < 3:
                return
            n = 0
            for d in (1, 0):
                for c, B, K, N in (("zc", cb[d], ck[d], TC), ("z", hb[d], hk[d], T)):
                    for h in range(HH):
                        j = J[c, d, h]
                        dve.wait_ge(log_ready, n + 1)
                        l1 = spl[:, n % 2, 0:N]
                        step(V.scalar_tensor_tensor(B[:, h], bank(j.lead, N), 0.0, l1, ALU.min, ALU.subtract))
                        V.scalar_tensor_tensor(K[:, h], bank(j.lead, N), 0.0, l1, ALU.max, ALU.add).then_inc(free[j.lead], 1)
                        rev = slice(None, None, -1) if d else slice(None)
                        keep = ones[:, 0:N] if c == "zc" else reset[:, d]
                        V.tensor_tensor_scan(B[:, h][:, rev], keep[:, rev], B[:, h][:, rev], 0.0,
                                             ALU.mult, ALU.add).then_inc(b_ready, 1)
                        n += 1
            dve.wait_ge(hk_ready, 4 * HH)
            for h in range(HH):
                j = J["hq", h]
                dve.wait_ge(free[j.lead], j.count)
            def take_scores(p):
                d, h = heads[p // SLOT]
                L = p % SLOT
                if L == 0:
                    if p:
                        j = J[("ho",) + heads[p // SLOT - 1]]
                        dve.wait_ge(full[j.lead], j.count)
                    if h == 0:
                        step(V.memset(sc, 0.0))
                j = J["sc", d, h, L]
                wait_full(j)
                mk = masks[:, d, L][:, None, :].broadcast_to((P, NC, CH))
                V.copy_predicated(sc.rearrange("p (c n) -> p c n", c=NC), mk,
                                  bank(j.lead).rearrange("p (c n) -> p c n", c=NC)).then_inc(free[j.lead], 1)
                dve.wait_ge(free[j.lead], j.count)

            def states(d, h):
                order = range(NC) if d == 0 else range(NC - 1, -1, -1)
                j = J["s0c", d, h]
                dve.wait_ge(free[j.lead], j.count)
                for s, c in enumerate(order):
                    if s < NC - 1:
                        j = J["kv", d, h, s]
                        wait_full(j)
                        V.scalar_tensor_tensor(state[:, (s + 1) % 2], state[:, s % 2], small[:, 100 + c:101 + c],
                                               bank(j.lead, P), ALU.mult, ALU.add).then_inc(free[j.lead], 1)
                        dve.wait_ge(free[j.lead], j.count)

            def sum_directions(d, h):
                if d == 0:
                    j = J["ho", 0, h]
                    wait_full(j)
                    V.tensor_tensor(ho[:, h], bank(j.lead), ho[:, h], ALU.add).then_inc(free[j.lead], 1)

            for n, (d, h) in enumerate(heads):
                for L in range(SLOT):
                    p = n * SLOT + L
                    if p - 5 in fills:
                        take_mod(*fills[p - 5])
                    if L < LEVELS:
                        m = n * LEVELS + L
                        dve.wait_ge(decay_ready, m + 1)
                        step(V.tensor_tensor(lvQ[m % 3], lvE[m % 3], hq[:, h], ALU.mult))
                        V.tensor_tensor(lvK[m % 3], lvE[m % 3], hk[d][:, h], ALU.mult).then_inc(lv_ready, 1)
                    if L == 0:
                        dve.wait_ge(cdec_ready, n + 1)
                        V.tensor_tensor(kcdec, kcdec, ck[d][:, h], ALU.mult).then_inc(kcd_ready, 1)
                    if L == 2 and n:
                        states(*heads[n - 1])
                    if L == 4 and n:
                        sum_directions(*heads[n - 1])
                    if L == 5:
                        dve.wait_ge(ends_ready, n + 1)
                        end = 0 if d else CH - 1
                        step(V.tensor_copy(small[:, 100:100 + NC], qdec[:, end::CH]))
                        step(V.tensor_tensor(qdec, qdec, hq[:, h], ALU.mult))
                        V.tensor_tensor(kdec, kdec, hk[d][:, h], ALU.mult).then_inc(qdec_ready, 1)
                    if p >= 2:
                        take_scores(p - 2)
            take_scores(p - 1)
            take_scores(p)
            states(*heads[-1])
            sum_directions(*heads[-1])
            for h in range(HH):
                j = J["ssq", h]
                wait_full(j)
                V.tensor_scalar(root_h[:, h], bank(j.lead), 1.0 / HD, EPS, ALU.mult, ALU.add).then_inc(free[j.lead], 1)
            for h in range(HH):
                dve.wait_ge(hroot_out, h + 1)
                step(V.reciprocal(root_h[:, h], root_h[:, h]))
                step(V.tensor_tensor(root_h[:, h], root_h[:, h], ho[:, h], ALU.mult))
                V.scalar_tensor_tensor(yT[:, h], root_h[:, h], colsA[:, 48 + h:49 + h], yT[:, h],
                                       ALU.mult, ALU.mult).then_inc(y_hgrn, 1)

            def add_out(l):
                j = J["grow", l]
                dve.wait_ge(free[j.lead], j.count)
                if l == 0:
                    dve.wait_ge(x_again, 16)
                for t in range(TT):
                    for half in range(2):
                        hs = slice(512 * half, 512 * half + 512)
                        j = J["y", l, t, half]
                        wait_full(j)
                        V.tensor_tensor(xtmp[:, half], bank(j.lead), grow[:, hs], ALU.mult).then_inc(free[j.lead], 1)
                        dve.wait_ge(free[j.lead], j.count)
                        V.tensor_tensor(xs[:, t, hs], xs[:, t, hs], xtmp[:, half], ALU.add).then_inc(x_ready, 1)

            def norm(nth):
                dve.wait_ge(squares_ready, TT + CT + TT * nth)
                root(small[:, 8:8 + TT], rstd[:, 0:TT], TT, 1.0 / D, (means_ready, roots_ready, nth + 1))
                for t in range(TT):
                    V.tensor_scalar(xn[:, t], xs[:, t], rstd[:, t:t + 1], None, ALU.mult).then_inc(xn_ready, 1)

            def moe(l):
                norm(1 + 2 * l)
                for k in range(1, KT, 2):
                    modulate(J["h2T", l, k], h2T, k, scaleA[:, 2 + l], modc[:, l, 3], T)
                j = J["logit", l]
                wait_full(j)
                lg = bank(j.lead, TT * E).rearrange("p (t e) -> p t e", e=E)
                m4 = small[:, 120:124]
                step(V.tensor_reduce(m4, lg, AX, ALU.max))
                V.tensor_tensor(aff[:, :, :], lg, m4[:, :, None].broadcast_to((P, TT, E)), ALU.subtract).then_inc(free[j.lead], 1)
                dve.wait_ge(logit_exp, l + 1)
                step(V.tensor_reduce(m4, aff[:, :, :], AX, ALU.add))
                step(V.reciprocal(m4, m4))
                V.tensor_tensor(aff[:, :, :], aff[:, :, :], m4[:, :, None].broadcast_to((P, TT, E)), ALU.mult).then_inc(aff_ready, 1)
                j = J["affT", l]
                wait_full(j)
                row = [sel[0:E, n] for n in range(4)]
                V.tensor_copy(row[0], bank(j.lead)[0:E, :]).then_inc(free[j.lead], 1)
                dve.wait_ge(free[j.lead], j.count)
                top = small[0:E, 128:136]
                for r in range(CAP // 8):
                    step(V.max(top, row[min(r, 1)]))
                    step(V.match_replace(row[1], top, row[min(r, 1)], -1.0))
                step(V.tensor_scalar(row[2], row[1], 0.0, None, ALU.is_lt))
                step(V.tensor_tensor_scan(row[0], row[2], row[2], 0.0, ALU.add, ALU.max))
                step(V.tensor_tensor(row[0], row[0], row[2], ALU.mult))
                V.tensor_scalar(row[3], row[0], -1.0, None, ALU.add).then_inc(slot_ready, 1)
                j = J["slotT", l]
                wait_full(j)
                V.tensor_copy(slotc[:, :, :], bank(j.lead, TT * E).rearrange("p (t e) -> p t e", e=E)).then_inc(free[j.lead], 1)
                dve.wait_ge(free[j.lead], j.count)
                base = loop_base[l]
                with dve.Fori(0, E // 2) as i:
                    def wait_use(b, nth):
                        dve.wait_ge(full[b], i * LOOP_PER[b] + (base[b] + nth + 1))
                        return bank(b)

                    pair = (P, TT, 2, CAP)
                    slots = slotc[:, :, bass.ds(i * 2, 2)][:, :, :, None].broadcast_to(pair)
                    gates = aff[:, :, bass.ds(i * 2, 2)][:, :, :, None].broadcast_to(pair)
                    V.tensor_tensor(onehot, slots, iota[:, None, None, :].broadcast_to(pair), ALU.is_equal).then_inc(onehot_ready, 1)
                    dve.wait_ge(onehot_ready, i + (l * 8 + 1))
                    V.tensor_tensor(gated, onehot, gates, ALU.mult).then_inc(gated_ready, 1)
                    g = wait_use(5, 0)
                    for q in range(4):
                        k = 4 + q
                        ins = V.tensor_scalar(xe[:, k], g[:, q * P:(q + 1) * P], scaleA[:, 2 + l, k:k + 1],
                                              modc[:, l, 3, k:k + 1], ALU.mult, ALU.add)
                    ins.then_inc(free[5], 1)
                    wait_use(2, 0)
                    dve.wait_ge(free[0], i * 2 + (base[0] + 1))
                    V.tensor_tensor(actb, psf[:, 1024:2048], sil, ALU.mult).then_inc(free[2], 1)
                    V.tensor_copy(actT[:, 4:8].rearrange("p k n -> p (k n)"), wait_use(5, 1)).then_inc(free[5], 1)
                    wait_use(0, 1)
                    V.tensor_tensor(ye, psf[:, 0:1024], grow[:, :], ALU.mult).then_inc(free[0], 1)
                    for t in range(TT):
                        for half in range(2):
                            y = wait_use(6 + half, t + 1 - half)
                            hs = slice(512 * half, 512 * half + 512)
                            V.tensor_tensor(xs[:, t, hs], y, xs[:, t, hs], ALU.add).then_inc(free[6 + half], 1)

            add_out(0)
            if upto < 5:
                return
            moe(0)
            norm(2)
            for k in range(1, KT, 2):
                modulate(J["h3T", k], hT, k, scaleA[:, 1], modc[:, 1, 0], T)
            step(V.memset(uT[:, 0:1], 0.0))
            step(V.memset(uT[:, T + 1:T + 2], 0.0))
            for f in range(KT):
                j = J["conv", "c", f]
                dve.wait_ge(free[j.lead], j.count)
                j = J["conv", "b", f]
                dve.wait_ge(free[j.lead], j.count)
                j = J["conv", "v", f]
                wait_full(j)
                V.tensor_tensor(uT[:, 1:T + 1], bank(j.lead), cT[:, f], ALU.mult).then_inc(free[j.lead], 1)
                dve.wait_ge(free[j.lead], j.count)
                w = [colsA[:, 52 + 8 * n + f:53 + 8 * n + f] for n in range(3)]
                step(V.tensor_scalar(vT, uT[:, 0:T], w[0], None, ALU.mult))
                step(V.scalar_tensor_tensor(vT, uT[:, 1:T + 1], w[1], vT, ALU.mult, ALU.add))
                step(V.scalar_tensor_tensor(vT, uT[:, 2:T + 2], w[2], vT, ALU.mult, ALU.add))
                V.tensor_tensor(ycT[:, f], vT, bT[:, f], ALU.mult).then_inc(ycT_ready, 1)
                dve.wait_ge(ycT_ready, f + 1)
            add_out(1)
            moe(1)

        @block.scalar
        def _(act):
            S = nc.scalar
            step = Chain(act, act_step)

            def wait_full(j):
                act.wait_ge(full[j.lead], j.count)

            def copy(j, dst, n=512, func=ACT.Copy):
                wait_full(j)
                S.activation(dst, psf[:, 512 * j.lead:512 * j.lead + n], func).then_inc(free[j.lead], 1)

            def modulate(j, dst, k, gain, shift, n):
                wait_full(j)
                S.activation(dst[:, k], bank(j.lead, n), ACT.Identity, bias=shift[:, k:k + 1],
                             scale=gain[:, k:k + 1]).then_inc(free[j.lead], 1)

            act.wait_ge(cols_ready, 1)
            S.activation(silc[:, :, 0:2], silc[:, :, 0:2], ACT.Silu).then_inc(silc_ready, 1)

            def row_mod(m, half):
                j = J["modr", m, half]
                wait_full(j)
                S.activation(modrow[:, half * 512:(half + 1) * 512], bank(j.lead), ACT.Copy).then_inc(free[j.lead], 1)

            act.wait_ge(lam_dots, 1)
            S.activation(small[:, 2:4], small[:, 0:2], ACT.Exp).then_inc(lam_exps, 1)
            for n, t in enumerate([4, 5, 0, 1, 2, 3]):
                act.wait_ge(x_in, 16 * (TT + CT))
                if n:
                    act.wait_ge(squares_ready, n)
                S.activation(junk, x6[:, t], ACT.Square, accum_out=small[:, 8 + t:9 + t]).then_inc(squares_ready, 1)
            act.wait_ge(means_ready, 1)
            S.activation(rstd_(small, TT + CT), rstd_(small, TT + CT), ACT.Sqrt).then_inc(roots_ready, 1)
            for m in mods0:
                for half in range(2):
                    row_mod(m, half)
            act.wait_ge(scale_ready, 4)
            for k in range(0, KT, 2):
                modulate(J["hT", k], hT, k, scaleA[:, 0], modc[:, 0, 0], T)
            for k in range(0, KT, 2):
                modulate(J["hcT", k], hcT, k, scaleA[:, 4], modx[:, 0], TC)
            if upto < 1:
                return

            def take_qk(n, j, arr, t):
                copy(j, arr[:, t])
                act.wait_ge(free[j.lead], j.count)
                if n >= 2:
                    act.wait_ge(qk_means, n - 1)
                S.activation(tsq[:, n % 2], arr[:, t], ACT.Square).then_inc(qk_squares, 1)

            def roots_qk(n):
                act.wait_ge(qk_means, n + 1)
                r8 = small[:, 32 + 8 * (n % 2):40 + 8 * (n % 2)]
                S.activation(r8, r8, ACT.Sqrt).then_inc(qk_roots, 1)

            for t in range(TT + CT):
                take_qk(t, J["dk", t], ktok, t)
                roots_qk(t)
            for t in range(TT + CT):
                copy(J["dv", t], vtok[:, t])
            for h in range(HH):
                copy(J["gate", h], yT[:, h], func=ACT.Silu)
            for t in range(TT):
                take_qk(TT + CT + t, J["dq", t], qtok, t)
                roots_qk(TT + CT + t)
            copy(J["hv", 0], hv[:, 0])
            for h in range(AH):
                copy(J["kT", h], kT[:, h], T + TC)

            def exps(n):
                h, t = att[n]
                if n >= 2:
                    act.wait_ge(wgt_ready, n - 1)
                for m in range(2):
                    j = J[f"s{m}", h, t]
                    act.wait_ge(max_ready, 2 * n + m + 1)
                    S.activation(prob[:, n % 2, m], psf[:, 512 * j.lead:512 * j.lead + T + TC], ACT.Exp,
                                 bias=astat[:, n, m:m + 1], scale=AD ** -0.5,
                                 accum_out=astat[:, n, 2 + m:3 + m]).then_inc(free[j.lead], 1)

            exps(0)
            for n, (h, t) in enumerate(att):
                copy(J["wT", h, t], wT.rearrange("p k n -> p (k n)"), T + TC)
                if n + 1 < len(att):
                    exps(n + 1)
                j = J["o", h, t]
                wait_full(j)
                S.activation(oall[:, t, h * P:(h + 1) * P], bank(j.lead, P), ACT.Copy,
                             scale=astat[:, n, 4:5]).then_inc(free[j.lead], 1)
                act.wait_ge(free[j.lead], j.count)
                if n:
                    act.wait_ge(o_squares, n)
                S.activation(sqo, oall[:, t, h * P:(h + 1) * P], ACT.Square,
                             accum_out=small[:, 80 + 4 * t + h:81 + 4 * t + h]).then_inc(o_squares, 1)
                if n in hv_part and hv_part[n][1][-1] == KT - 1:
                    tile = hv_part[n][0]
                    copy(J["hv", tile], hv[:, tile])
            act.wait_ge(o_means, 1)
            S.activation(small[:, 80:96], small[:, 80:96], ACT.Sqrt).then_inc(o_roots, 1)
            for h in range(AH):
                copy(J["oT", h], yT[:, AH + h])
            if upto < 3:
                return
            n = 0
            last = None
            for d in (1, 0):
                for c, K, N in (("zc", ck[d], TC), ("z", hk[d], T)):
                    for h in range(HH):
                        j = J[c, d, h]
                        wait_full(j)
                        buf = spl[:, n % 2, 0:N]
                        if n >= 2:
                            act.wait_ge(free[last[0].lead], last[0].count)
                        step(S.activation(buf, bank(j.lead, N), ACT.Abs))
                        step(S.activation(buf, buf, ACT.Exp, scale=-1.0))
                        S.activation(buf, buf, ACT.Ln, bias=1.0).then_inc(log_ready, 1)
                        if last is not None:
                            pj, pk = last
                            act.wait_ge(free[pj.lead], pj.count)
                            S.activation(pk, pk, ACT.Exp, scale=-1.0).then_inc(hk_ready, 1)
                        last = (j, K[:, h])
                        n += 1
            pj, pk = last
            act.wait_ge(free[pj.lead], pj.count)
            S.activation(pk, pk, ACT.Exp, scale=-1.0).then_inc(hk_ready, 1)
            for h in range(HH):
                copy(J["hq", h], hq[:, h])
            act.wait_ge(b_ready, 4 * HH)
            def take_turned(d, h):
                copy(J["kdT", d, h], kdtok.rearrange("p c n -> p (c n)"))

            def take_out(d, h):
                if d == 1:
                    copy(J["ho", d, h], ho[:, h])

            for n, (d, h) in enumerate(heads):
                before = heads[n - 1] if n else None
                for L in range(SLOT):
                    p = n * SLOT + L
                    if p - 3 in fills:
                        row_mod(*fills[p - 3])
                    if L == 0:
                        ce = 0 if d else TC - 1
                        if n:
                            copy(J[("s0c",) + before], state[:, 0], P)
                            j = J[("kcT",) + before]
                            act.wait_ge(full[j.lead], j.count)
                        S.activation(kcdec, cb[d][:, h], ACT.Exp, scale=-1.0,
                                     bias=cb[d][:, h, ce:ce + 1]).then_inc(cdec_ready, 1)
                    if L == 1 and n:
                        take_turned(*before)
                    if L == 4:
                        copy(J["kcT", d, h], kcdtok.rearrange("p t n -> p (t n)"), TC)
                    if L == 5:
                        if n:
                            j = J[("ho",) + before]
                            wait_full(j)
                            take_out(*before)
                        S.activation(qdec, hb[d][:, h], ACT.Exp)
                        for c in range(NC):
                            e = c * CH + (0 if d else CH - 1)
                            cc = slice(c * CH, (c + 1) * CH)
                            ins = S.activation(kdec[:, cc], hb[d][:, h, cc], ACT.Exp, scale=-1.0, bias=hb[d][:, h, e:e + 1])
                        ins.then_inc(ends_ready, 1)
                    if L < LEVELS:
                        m = n * LEVELS + L
                        act.wait_ge(diff_ready, m + 1)
                        step(S.activation(lvE[m % 3], lvE[m % 3], ACT.Abs))
                        S.activation(lvE[m % 3], lvE[m % 3], ACT.Exp, scale=-1.0).then_inc(decay_ready, 1)
            copy(J[("s0c",) + heads[-1]], state[:, 0], P)
            take_turned(*heads[-1])
            take_out(*heads[-1])
            for h in range(HH):
                j = J["ho", 0, h]
                act.wait_ge(free[j.lead], j.count)
                S.activation(sq[:, h], ho[:, h], ACT.Square).then_inc(sq_ready, 1)
            for h in range(HH):
                j = J["ssq", h]
                act.wait_ge(free[j.lead], j.count)
                S.activation(root_h[:, h], root_h[:, h], ACT.Sqrt).then_inc(hroot_out, 1)

            def squares(nth, x_count):
                if nth == 2:
                    for b in (6, 7):
                        act.wait_ge(free[b], loop_base[0][b] + LOOP_PER[b] * E // 2)
                for t in range(TT):
                    n = TT + CT + TT * (nth - 1) + t
                    act.wait_ge(x_ready, x_count - 2 * (TT - 1 - t))
                    act.wait_ge(squares_ready, n)
                    S.activation(junk_moe, xs[:, t], ACT.Square, accum_out=small[:, 8 + t:9 + t]).then_inc(squares_ready, 1)
                act.wait_ge(means_ready, nth + 1)
                S.activation(rstd_(small, TT), rstd_(small, TT), ACT.Sqrt).then_inc(roots_ready, 1)

            def moe(l):
                squares(1 + 2 * l, 8 + 8 * l)
                for k in range(0, KT, 2):
                    modulate(J["h2T", l, k], h2T, k, scaleA[:, 2 + l], modc[:, l, 3], T)
                copy(J["router", l], parts)
                j = J["logit", l]
                act.wait_ge(free[j.lead], j.count)
                S.activation(aff[:, :, :], aff[:, :, :], ACT.Exp).then_inc(logit_exp, 1)
                copy(J["grow2", l], grow[:, :], D)
                base = loop_base[l]
                with act.Fori(0, E // 2) as i:
                    def wait_use(b, nth):
                        act.wait_ge(full[b], i * LOOP_PER[b] + (base[b] + nth + 1))
                        return bank(b)

                    g = wait_use(4, 0)
                    for k in range(4):
                        ins = S.activation(xe[:, k], g[:, k * P:(k + 1) * P], ACT.Identity,
                                           bias=modc[:, l, 3, k:k + 1], scale=scaleA[:, 2 + l, k:k + 1])
                    ins.then_inc(free[4], 1)
                    S.activation(spread, wait_use(6, 0), ACT.Copy).then_inc(free[6], 1)
                    wait_use(0, 0)
                    S.activation(sil, psf[:, 0:1024], ACT.Silu).then_inc(free[0], 1)
                    S.activation(actT[:, 0:4].rearrange("p k n -> p (k n)"), wait_use(4, 1), ACT.Copy).then_inc(free[4], 1)

            copy(J["grow", 0], grow[:, :], D)
            if upto < 5:
                return
            moe(0)
            squares(2, 8)
            for k in range(0, KT, 2):
                modulate(J["h3T", k], hT, k, scaleA[:, 1], modc[:, 1, 0], T)
            for f in range(KT):
                copy(J["conv", "b", f], bT[:, f])
            for f in range(KT):
                copy(J["conv", "c", f], cT[:, f])
            copy(J["grow", 1], grow[:, :], D)
            moe(1)

        @block.gpsimd
        def _(pool):
            if upto < 3:
                return
            n = 0
            pool.wait_ge(b_ready, 4 * HH)
            for h in range(HH):
                j = J["hq", h]
                pool.wait_ge(full[j.lead], j.count)
            for d in (1, 0):
                for h in range(HH):
                    for L in range(LEVELS):
                        m = n * LEVELS + L
                        half = CH >> (L + 1)
                        if m >= 3:
                            pool.wait_ge(lv_ready, m - 2)
                        src = hb[d][:, h].rearrange("p (b w) -> p b w", w=2 * half)
                        mid = src[:, :, half - 1 + d:half + d].broadcast_to((P, T // (2 * half), 2 * half))
                        nc.gpsimd.tensor_tensor(lvE[m % 3].rearrange("p (b w) -> p b w", w=2 * half), src, mid,
                                                ALU.subtract).then_inc(diff_ready, 1)
                    n += 1


def rstd_(small, n):
    return small[:, 16:16 + n]


INPUTS = ["x", "c", "ctx", "c_ctx", "mod_w", "mod_b", "norm1_g", "norm2_g", "even_w_in", "even_w_out",
          "hgrn_norm_g", "diff_qnorm_g", "diff_knorm_g", "diff_lambda", "diff_subln_g", "conv_w_in",
          "conv_w", "conv_w_out", "router_w", "exp_w_gate", "exp_w_up", "exp_w_down"]


def shape_constants():
    n = AD // 2
    inv = (1.0 / (ROPE_THETA ** (np.arange(0, n, 2, dtype=np.float32) / np.float32(n)))).astype(np.float32)
    tok = np.arange(T)
    cos, sin = np.zeros((T, AD), np.float32), np.zeros((T, AD), np.float32)
    for axis, pos in enumerate((tok // GRID_W, tok % GRID_W)):
        ang = pos.astype(np.float32)[:, None] * inv[None, :]
        for w in range(2):
            at = slice(axis * n + w * (n // 2), axis * n + (w + 1) * (n // 2))
            cos[:, at] = np.cos(ang)
            sin[:, at] = np.sin(ang) * (-1.0, 1.0)[w]
    s = np.arange(CH)[:, None]
    t = np.arange(CH)[None, :]
    masks = np.zeros((P, 2, LEVELS + 1, CH), np.float32)
    for L in range(LEVELS):
        half = CH >> (L + 1)
        same = s // (2 * half) == t // (2 * half)
        masks[:, 0, L] = same & (s % (2 * half) < half) & (t % (2 * half) >= half)
        masks[:, 1, L] = same & (s % (2 * half) >= half) & (t % (2 * half) < half)
    masks[:, :, LEVELS] = (s == t)[:, None, :]

    def lay(v):
        return np.ascontiguousarray(v.reshape(TT, P, AD).transpose(1, 0, 2))

    return {"c_ident": np.eye(P, dtype=np.float32), "c_cos": lay(cos), "c_sin": lay(sin),
            "c_iota": np.tile(np.arange(CAP, dtype=np.float32), (P, 1)), "c_masks": masks.reshape(P, -1)}


def program(nc, arrays, stop=None, tap=None, extra_out=()):
    a = {}
    for name, v in arrays.items():
        a[name] = nc.dram_tensor(name, v.shape, mybir.dt.from_np(v.dtype), kind="ExternalInput").ap()
    out = nc.dram_tensor("out_x", (1, T, D), F32, kind="ExternalOutput").ap()
    extra = {n: nc.dram_tensor(n, s, F32, kind="ExternalOutput").ap() for n, s in extra_out}
    if tap is not None:
        build(nc, a, out, stop, lambda sp, loc: tap(sp, loc, extra))
    else:
        build(nc, a, out)


def kernel(**inputs):
    import concourse.bacc as bacc
    from concourse.bass_utils import run_bass_kernel_spmd as run

    arrays = {n: np.ascontiguousarray(inputs[n]) for n in INPUTS}
    arrays.update(shape_constants())
    nc = bacc.Bacc("TRN2", target_bir_lowering=False, num_devices=1)
    program(nc, arrays)
    r = run(nc, [arrays], core_ids=[0])
    return r.results[0]["out_x"]
```

```python
from contextlib import ExitStack
import math

import numpy as np

import concourse.bass as bass
from concourse import mybir

P = 128
D = 1024
T = 512
TC = 256
KT = D // P
TT = T // P
CT = TC // P
GRID_W = 64
HH = 4
HD = 128
AH = 4
AD = 64
CH = 128
NC = T // CH
LEVELS = 7
E = 16
CAP = 2 * T // E
EPS = 1e-6
LAM_INIT = 0.8 - 0.6 * math.exp(0.0)
ROPE_THETA = 10000.0
SLOTS = 3

F32 = mybir.dt.float32
F32R = mybir.dt.float32r
U8 = mybir.dt.uint8
ALU = mybir.AluOpType
ACT = mybir.ActivationFunctionType
AX = mybir.AxisListType.X

KB = 256


class Job:

    def __init__(self, lead, banks, count, owners):
        self.lead, self.banks, self.count, self.owners = lead, banks, count, owners


class BankPlan:

    def __init__(self):
        self.used = [0] * 8
        self.owner = [None] * 8

    def job(self, *banks):
        lead = banks[0]
        self.used[lead] += 1
        owners = []
        for b in banks:
            if self.owner[b] is not None and self.owner[b] not in owners:
                owners.append(self.owner[b])
        j = Job(lead, banks, self.used[lead], owners)
        for b in banks:
            self.owner[b] = j
        return j

    def loop(self, per, leads, times):
        base = list(self.used)
        for b in range(8):
            self.used[b] += per[b] * times
        for b in range(8):
            self.owner[b] = Job(leads[b], (b,), self.used[leads[b]], [])
        return base


class Chain:

    def __init__(self, eng, sem):
        self.eng, self.sem, self.n, self.base, self.turn, self.per = eng, sem, 0, 0, None, 0

    def __call__(self, ins):
        self.n += 1
        ins.then_inc(self.sem, 1)
        if self.turn is None:
            self.eng.wait_ge(self.sem, self.n)
        else:
            self.eng.wait_ge(self.sem, self.turn * self.per + self.n)

    def enter(self, turn, per):
        self.base, self.turn, self.per = self.n, turn, per

    def leave(self, times):
        assert self.n - self.base == self.per, (self.n - self.base, self.per)
        self.n = self.base + self.per * times
        self.turn = None


def build(nc, a, out):
    bp = BankPlan()
    J = {}
    J["colsA"] = bp.job(0)
    J["colsB"] = bp.job(1)
    mods0 = [(0, 0), (0, 1)]
    mods1 = [(0, j) for j in range(2, 6)] + [(1, j) for j in range(6)]
    for m in mods0:
        for half in range(2):
            J["modr", m, half] = bp.job(2 + half)
            J["modc", m, half] = bp.job(2 + half)
    for kt in range(KT):
        J["hT", kt] = bp.job([4, 5, 6, 7][kt % 4])
    for kt in range(KT):
        J["hcT", kt] = bp.job([4, 5, 6, 7][kt % 4])
    n = 0
    for t in range(TT + CT):
        J["dk", t] = bp.job(n % 4); n += 1
    for t in range(TT + CT):
        J["dv", t] = bp.job(n % 4); n += 1
    for h in range(HH):
        J["gate", h] = bp.job(n % 4); n += 1
    for t in range(TT):
        J["dq", t] = bp.job(n % 4); n += 1
    J["hv", 0] = bp.job(7)
    for h in range(AH):
        J["qT", h] = bp.job(6)
        J["kT", h] = bp.job(4, 5)
    att = [(h, t) for h in range(AH) for t in range(TT)]
    hv_part = {3 * (t - 1) + i: (t, ks) for t in range(1, TT + CT)
               for i, ks in enumerate(((0, 1, 2), (3, 4, 5), (6, 7)))}
    assert len(hv_part) <= len(att)

    def score_jobs(h, t):
        J["s0", h, t] = bp.job(0, 1)
        J["s1", h, t] = bp.job(2, 3)

    score_jobs(0, 0)
    for n, (h, t) in enumerate(att):
        if n + 1 < len(att):
            score_jobs(*att[n + 1])
        if n in hv_part and hv_part[n][1][0] == 0:
            J["hv", hv_part[n][0]] = bp.job(7)
        J["wT", h, t] = bp.job(4, 5)
        J["o", h, t] = bp.job(6)
    n = 0
    for d in (1, 0):
        for h in range(HH):
            J["zc", d, h] = bp.job(n % 4); n += 1
        if d == 1:
            for h in range(AH):
                J["oT", h] = bp.job(4 + h)
        for h in range(HH):
            J["z", d, h] = bp.job(n % 4); n += 1
        if d == 0:
            for h in range(HH):
                J["hq", h] = bp.job(n % 4); n += 1
    halves = [(m, half) for m in mods1 for half in range(2)]
    fills = {3 * f: mh for f, mh in enumerate(halves)}
    heads = [(d, h) for d in (1, 0) for h in range(HH)]
    SLOT = LEVELS + 1
    assert 3 * (len(halves) - 1) + 5 < SLOT * len(heads)

    def tail_jobs(d, h):
        J["ho", d, h] = bp.job(6)
        for c in range(NC - 1):
            J["kv", d, h, c] = bp.job(5)

    for n, (d, h) in enumerate(heads):
        for L in range(SLOT):
            p = n * SLOT + L
            if p - 4 in fills:
                J[("modc",) + fills[p - 4]] = bp.job(3)
            if p in fills:
                J[("modr",) + fills[p]] = bp.job(7)
            if L == 1:
                J["kcT", d, h] = bp.job(4)
            if L == 5:
                J["s0c", d, h] = bp.job(5)
            if L == 7:
                J["kdT", d, h] = bp.job(4)
            J["sc", d, h, L] = bp.job(p % 3)
            if L == 1 and n:
                tail_jobs(*heads[n - 1])
    tail_jobs(*heads[-1])
    J["ssq"] = bp.job(0)
    for h in range(HH):
        J["rrow", h] = bp.job(1 + h)

    def out_jobs(l):
        J["grow", l] = bp.job(4, 5)
        for t in range(TT):
            for half in range(2):
                J["y", l, t, half] = bp.job((2 * t + half) % 4)

    LOOP_PER = [2, 0, 1, 0, 2, 2, 5, 4]
    LOOP_LEAD = [0, 0, 2, 2, 4, 5, 6, 7]
    loop_base = {}

    def moe_jobs(l):
        for kt in range(KT):
            J["h2T", l, kt] = bp.job(kt)
        J["router", l] = bp.job(1)
        J["logit", l] = bp.job(0)
        J["affT", l] = bp.job(1)
        J["slotT", l] = bp.job(2)
        J["grow2", l] = bp.job(6, 7)
        loop_base[l] = bp.loop(LOOP_PER, LOOP_LEAD, E // 2)

    out_jobs(0)
    moe_jobs(0)
    for kt in range(KT):
        J["h3T", kt] = bp.job(kt)
    n = 0
    for part in "bcv":
        for f in range(KT):
            J["conv", part, f] = bp.job(n % 8); n += 1
    out_jobs(1)
    moe_jobs(1)

    def w_in(j):
        return a["even_w_in"][0][:, j * D:(j + 1) * D]

    chunks = {}
    stream = []
    slot_last = {}
    slot_used = [0] * SLOTS

    def chunk(name, slot, src, last_job):
        slot_used[slot] += 1
        chunks[name] = (slot, slot_used[slot])
        stream.append((slot, src, slot_last.get(slot), name))
        slot_last[slot] = last_job

    n = 0
    for m in mods0:
        chunk(("mod", m), (n + 1) % 2, a["mod_w"][m[0]][:, m[1] * D:(m[1] + 1) * D], J["modr", m, 1]); n += 1
    chunk("w3", (n + 1) % 2, w_in(3), J["dv", TT + CT - 1]); n += 1
    chunk("w2", (n + 1) % 2, w_in(2), J["dq", TT - 1]); n += 1
    chunk("w1", (n + 1) % 2, w_in(1), J["z", 1, HH - 1]); n += 1
    chunk("w0", (n + 1) % 2, w_in(0), J["hq", HH - 1]); n += 1
    for m in mods1:
        chunk(("mod", m), (n + 1) % 2, a["mod_w"][m[0]][:, m[1] * D:(m[1] + 1) * D], J["modr", m, 1]); n += 1
    chunk("wo", (n + 1) % 2, a["even_w_out"][0], J["y", 0, TT - 1, 1]); n += 1
    assert chunks["wo"][0] == 1
    head0 = list(stream)
    stream.clear()

    def experts(l):
        first = [slot_last.get(s) for s in range(3)]
        b = loop_base[l]
        slot_last[0] = slot_last[1] = slot_last[2] = Job(0, (0,), b[0] + LOOP_PER[0] * E // 2, [])
        return first

    first0 = experts(0)
    units = [(part, f) for part in "bcv" for f in range(KT)]
    chunk("cb", 1, a["conv_w_in"][0][:, 0:D], J["conv", "b", KT - 1])
    chunk("cc", 2, a["conv_w_in"][0][:, D:2 * D], J["conv", "c", KT - 1])
    chunk("cv", 0, a["conv_w_in"][0][:, 2 * D:3 * D], J["conv", "v", KT - 1])
    chunk("co", 1, a["conv_w_out"][0], J["y", 1, TT - 1, 1])
    head1 = list(stream)
    first1 = experts(1)

    with ExitStack() as ctx:
        def sb(name, shape, dt=F32):
            return ctx.enter_context(nc.sbuf_tensor(name, shape, dt))

        def sem(name):
            return ctx.enter_context(nc.semaphore(name))

        with ExitStack() as typed:
            def piece(name, *shape):
                return typed.enter_context(nc.sbuf_tensor(name, [P, *shape], F32R))

            ring_r = [piece(f"ring_r{s}", KT, D) for s in range(SLOTS)]
            piece("room_0_16", 16 * KB)
            bT_r = piece("bT_r", KT, T)
            y_hi_r = piece("y_hi_r", KT, T)
            piece("room_48_54", 6 * KB)
            h3lo_r = piece("h3lo_r", KT, T)
            unit_hi0_r = piece("unit_hi0_r", KT, P)
            piece("room_74_76", 2 * KB)
            hT_r = piece("hT_r", KT, T)
            unit_hi_r = [unit_hi0_r, piece("grow_r", KT, P)]
            wo_hi_r = [h3lo_r, hT_r]
        ring = sb("ring", [P, SLOTS, KT, D])
        annex = ring[:, 2, :, :].rearrange("p k n -> p (k n)")
        room = sb("room", [P, 92 * KB])
        grow = sb("grow", [P, D])
        ident = sb("ident", [P, P])
        rope_sin = sb("rope_sin", [P, TT, AD])
        iota = sb("iota", [P, CAP])
        masks = sb("masks", [P, 2, LEVELS + 1, CH], U8)
        ones = sb("ones", [P, TC])
        reset = sb("reset", [P, 2, T])
        rowsA = room[:, 60 * KB:60 * KB + P]
        rowsB = room[:, 61 * KB:61 * KB + P]
        colsA = sb("colsA", [P, P])
        colsB = sb("colsB", [P, 96])
        silc = sb("silc", [P, KT, 32])
        fold = sb("fold", [P, E])
        astat = sb("astat", [P, 16, 8])
        modc = sb("modc", [P, 2, 6, KT])
        modx = sb("modx", [P, 2, KT])
        scaleA = sb("scaleA", [P, 5, KT])
        small = sb("small", [P, 256])
        gains = sb("gains", [P, AD + AD + 2 * AD])
        slotc = sb("slotc", [P, TT, E])
        aff = sb("aff", [P, TT, E])
        router = sb("router", [P, KT, 32])

        def view(at_kb, *shape, base=None):
            base = room if base is None else base
            size = 1
            for s in shape:
                size *= s
            v = base[:, int(at_kb * KB):int(at_kb * KB) + size]
            if len(shape) == 1:
                return v
            names = "abcd"[:len(shape)]
            spec = "p (" + " ".join(names) + ") -> p " + " ".join(names)
            return v.rearrange(spec, **{k: s for k, s in zip(names[:-1], shape[:-1])})

        xs = view(0, TT, D)
        xn = view(16, TT, D)
        x6 = view(16, TT + CT, D)
        hT = view(76, KT, T)
        hcT = view(68, KT, TC)
        yT = view(52, KT, T)
        qtok = view(0, TT, T)
        ktok = view(8, TT + CT, T)
        vtok = view(20, TT + CT, T)
        qT = view(32, AH, T)
        kT = view(40, AH, T + TC)
        prob = view(0, 2, 2, T + TC)
        wgt = view(12, T + TC)
        wT = view(15, CT + TT, P)
        oall = view(16, TT, T, base=annex)
        junk = view(0, D, base=annex)
        tsq = view(4, 2, T, base=annex)
        trot = view(8, 2, T, base=annex)
        ta = view(12, T, base=annex)
        hv = view(0, TT + CT, T, base=annex)
        hq = view(12, HH, T)
        hb = [view(20, HH, T), view(36, HH, T)]
        hk = [view(28, HH, T), view(44, HH, T)]
        ho = view(0, HH, T)
        cb = [view(12, HH, TC, base=annex), view(8, HH, TC)]
        ck = [view(16, HH, TC, base=annex), view(20, HH, TC, base=annex)]
        sqo = view(14, P, base=annex)
        spl = view(24, 2, T, base=annex)
        lvE = [view(68, T), reset[:, 0], reset[:, 1]]
        lvQ = [view(70, T), view(72, T), view(74, T)]
        lvK = [view(76, T), view(78, T), view(26, T, base=annex)]
        qdec = view(80, T)
        kdec = view(82, T)
        kdtok = view(84, NC, P)
        sc = view(86, T)
        state = view(88, 2, P)
        masks_in = view(16, 2 * (LEVELS + 1) * CH, base=annex)
        modrow = view(28, D, base=annex)
        lamv = view(24, 4 * AD, base=annex)
        rope_cos = view(25, TT, AD, base=annex)
        kcdec = view(24, TC, base=annex)
        kcdtok = view(25, CT, P, base=annex)
        sq = view(36, HH, T)
        hstat = astat[:, :, :].rearrange("p a b -> p (a b)")[:, 0:HH * TT]
        h2T = view(76, KT, T)
        sel = view(41, 4, T)
        onehot = view(49, TT, 2, CAP)
        gated = view(51, TT, 2, CAP)
        spread = view(53, T)
        xe = view(55, KT, P)
        sil = view(59, D)
        parts = view(59, T)
        actb = view(32, D)
        actT = view(63, KT, P)
        ye = view(67, D)
        junk_moe = view(48, D)
        xtmp = view(70, 2, T)
        bT = view(16, KT, T)
        cT = view(32, KT, T)
        uT = view(48, T + 2)
        vT = view(51, T)
        h3lo = view(54, KT, T)

        ps = ctx.enter_context(nc.psum_tensor("ps", [P, 8, 512], F32))
        psf = ps[:, :, :].rearrange("p b n -> p (b n)")

        def bank(b, n=512):
            return ps[:, b, 0:n]

        def half_slot(q):
            return ring[:, q // 2, 4 * (q % 2):4 * (q % 2) + 4, :]

        full = [sem(f"bank_full{b}") for b in range(8)]
        free = [sem(f"bank_free{b}") for b in range(8)]
        ring_full = [sem(f"ring_full{s}") for s in range(SLOTS)]
        consts_in = sem("consts_in")
        level_masks_in = sem("level_masks_in")
        rows_in = sem("rows_in")
        x_in = sem("x_in")
        x_again = sem("x_again")
        router_in = [sem("router_in0"), sem("router_in1")]
        cols_ready = sem("cols_ready")
        silc_ready = sem("silc_ready")
        squares_ready = sem("squares_ready")
        means_ready = sem("means_ready")
        roots_ready = sem("roots_ready")
        xn_ready = sem("xn_ready")
        scale_ready = sem("scale_ready")
        act_step = sem("act_step")
        dve_step = sem("dve_step")
        lam_dots = sem("lam_dots")
        lam_exps = sem("lam_exps")
        qk_squares = sem("qk_squares")
        qk_means = sem("qk_means")
        qk_roots = sem("qk_roots")
        qk_normed = sem("qk_normed")
        max_ready = sem("max_ready")
        wgt_ready = sem("wgt_ready")
        o_squares = sem("o_squares")
        o_means = sem("o_means")
        o_roots = sem("o_roots")
        o_normed = sem("o_normed")
        log_ready = sem("log_ready")
        hk_ready = sem("hk_ready")
        b_ready = sem("b_ready")
        cdec_ready = sem("cdec_ready")
        kcd_ready = sem("kcd_ready")
        diff_ready = sem("diff_ready")
        decay_ready = sem("decay_ready")
        lv_ready = sem("lv_ready")
        lvq_ready = sem("lvq_ready")
        ends_ready = sem("ends_ready")
        qdec_ready = sem("qdec_ready")
        sq_ready = sem("sq_ready")
        hroot_out = sem("hroot_out")
        hrec_ready = sem("hrec_ready")
        x_ready = sem("x_ready")
        logit_exp = sem("logit_exp")
        aff_ready = sem("aff_ready")
        slot_ready = sem("slot_ready")
        onehot_ready = sem("onehot_ready")
        gated_ready = sem("gated_ready")
        gates_half = sem("gates_half")
        ups_half = sem("ups_half")
        downs_half = sem("downs_half")
        exp_full = [sem(f"exp_full{q}") for q in range(6)]
        ycT_ready = sem("ycT_ready")
        h3_hi = sem("h3_hi")
        h3_lo = sem("h3_lo")
        unit_hi_ready = sem("unit_hi_ready")
        unit_lo_ready = sem("unit_lo_ready")
        y_hi_ready = sem("y_hi_ready")
        y_lo_ready = sem("y_lo_ready")
        wo_hi_ready = sem("wo_hi_ready")
        wo_lo_ready = sem("wo_lo_ready")
        out_done = sem("out_done")


        block = ctx.enter_context(nc.Block())

        @block.sync
        def _(sp):
            def load_chunk(slot, src, owner):
                if owner is not None:
                    sp.wait_ge(full[owner.lead], owner.count)
                sp.dma_start(ring[:, slot], src.rearrange("(k p) n -> p k n", p=P)).then_inc(ring_full[slot], 16)

            for dst, src in ((ident, "c_ident"), (rope_cos, "c_cos"), (rope_sin, "c_sin"),
                             (iota, "c_iota")):
                sp.dma_start(dst if dst is rope_cos else dst[:], a[src]).then_inc(consts_in, 16)
            rows = [(0, a["c"].rearrange("b (k p) -> (b k) p", p=P)),
                    (8, a["c_ctx"].rearrange("(k p) -> k p", p=P)),
                    (16, a["norm1_g"].rearrange("l (k p) -> (l k) p", p=P)),
                    (32, a["norm2_g"].rearrange("l (k p) -> (l k) p", p=P)),
                    (48, a["hgrn_norm_g"][0]),
                    (52, a["conv_w"][0].rearrange("w (k p) -> (w k) p", p=P))]
            for at, src in rows:
                sp.dma_start(rowsA[at:at + src.shape[0], :], src).then_inc(rows_in, 16)
            sp.dma_start(rowsB[0:96, :], a["mod_b"].rearrange("l (k p) -> (l k) p", p=P)).then_inc(rows_in, 16)
            for at, n, src in ((0, AD, a["diff_qnorm_g"]), (AD, AD, a["diff_knorm_g"]), (2 * AD, 2 * AD, a["diff_subln_g"])):
                sp.dma_start(gains[:, at:at + n], src.broadcast_to((P, n))).then_inc(rows_in, 16)
            sp.dma_start(lamv, a["diff_lambda"].rearrange("a r n -> a (r n)").broadcast_to((P, 4 * AD))).then_inc(rows_in, 16)
            for t in range(CT):
                sp.dma_start(x6[:, TT + t], a["ctx"][0, t * P:(t + 1) * P, :]).then_inc(x_in, 16)
            for t in range(TT):
                sp.dma_start(x6[:, t], a["x"][0, t * P:(t + 1) * P, :]).then_inc(x_in, 16)
            for slot, src, owner, name in head0:
                load_chunk(slot, src, owner)
                if name == ("mod", mods0[-1]):
                    sp.dma_start(masks_in, a["c_masks"]).then_inc(level_masks_in, 16)
            sp.wait_ge(full[first0[0].lead], first0[0].count)
            for e in range(2):
                sp.dma_start(half_slot(e), a["exp_w_gate"][0, e, 0:512, :].rearrange("(k p) n -> p k n", p=P)).then_inc(exp_full[e], 16)
            for h in range(HH):
                j = J["rrow", h]
                sp.wait_ge(free[j.lead], j.count)
            sp.dma_start(xs, a["x"][0].rearrange("(t p) d -> p t d", p=P)).then_inc(x_again, 16)

            def load_experts(l, first):
                tables = (a["exp_w_gate"][l], a["exp_w_up"][l], a["exp_w_down"][l])
                sp.dma_start(router[:, :, 0:E], a["router_w"][l].rearrange("(k p) e -> p k e", p=P)).then_inc(router_in[l], 16)
                base = loop_base[l]

                def load(j, i, turn=0):
                    halves = tables[j // 4].rearrange("e (h r) n -> (e h) r n", h=2)
                    at = i * 4 + (4 * turn + 2 * (j % 2) + (j // 2) % 2)
                    src = halves[bass.ds(at, 1)].rearrange("o (k p) n -> p (o k) n", p=P)
                    sp.dma_start(half_slot(j % 6), src).then_inc(exp_full[j % 6], 16)

                def second_half(i):
                    sp.wait_ge(gates_half, i + (l * 8 + 1))
                    load(6, i)
                    load(7, i)
                    sp.wait_ge(full[0], i * 2 + (base[0] + 1))
                    load(8, i)
                    load(9, i)
                    sp.wait_ge(ups_half, i + (l * 8 + 1))
                    load(10, i)
                    load(11, i)

                for j in range(2 * (1 - l), 6):
                    if first[j // 2] is not None:
                        sp.wait_ge(full[first[j // 2].lead], first[j // 2].count)
                    load(j, 0)
                with sp.Fori(0, E // 2 - 1) as i:
                    second_half(i)
                    sp.wait_ge(full[2], i + (base[2] + 1))
                    load(0, i, 1)
                    load(1, i, 1)
                    sp.wait_ge(downs_half, i + (l * 8 + 1))
                    load(2, i, 1)
                    load(3, i, 1)
                    sp.wait_ge(full[0], i * 2 + (base[0] + 2))
                    load(4, i, 1)
                    load(5, i, 1)
                second_half(E // 2 - 1)

            load_experts(0, first0)
            for slot, src, owner, name in head1:
                load_chunk(slot, src, owner)
            sp.wait_ge(full[1], J["router", 0].count)
            load_experts(1, first1)
            for b in (6, 7):
                sp.wait_ge(free[b], loop_base[1][b] + LOOP_PER[b] * E // 2)
            sp.dma_start(out[0].rearrange("(t p) d -> p t d", p=P), xs).then_inc(out_done, 16)
            sp.wait_ge(out_done, 16)

        @block.tensor
        def _(pe):
            def open_(j):
                for o in j.owners:
                    pe.wait_ge(free[o.lead], o.count)
                return j

            def taken(j):
                pe.wait_ge(free[j.lead], j.count)

            def arrived(name):
                slot, n = chunks[name]
                pe.wait_ge(ring_full[slot], 16 * n)
                return ring[:, slot]

            def mod(m, half):
                j = open_(J["modr", m, half])
                w = arrived(("mod", m))
                for k in range(KT):
                    q = k % 4
                    mm = nc.tensor.matmul(ps[32 * q:32 * q + 32, j.lead, :], silc[:, k, :],
                                          w[:, k, half * 512:(half + 1) * 512], start=(k < 4), stop=(k >= 4))
                mm.then_inc(full[j.lead], 1)

            def mod_turn(m, half):
                taken(J["modr", m, half])
                j = open_(J["modc", m, half])
                for q in range(4):
                    mm = nc.tensor.matmul(bank(j.lead)[:, 2 * q:2 * q + 2], modrow[:, (4 * half + q) * P:(4 * half + q + 1) * P],
                                          fold[:, 0:2], start=True, stop=True)
                mm.then_inc(full[j.lead], 1)

            def tok_product(j, h, tile, w, n0):
                open_(j)
                for k in range(KT):
                    mm = nc.tensor.matmul(bank(j.lead), h[:, k, tile * P:(tile + 1) * P], w[:, k, n0:n0 + 512],
                                          start=(k == 0), stop=(k == KT - 1))
                mm.then_inc(full[j.lead], 1)

            def feat_product(j, h, n, w, n0):
                open_(j)
                for k in range(KT):
                    mm = nc.tensor.matmul(bank(j.lead, n), w[:, k, n0:n0 + P], h[:, k, 0:n],
                                          start=(k == 0), stop=(k == KT - 1))
                mm.then_inc(full[j.lead], 1)

            def turn(j, pieces):
                open_(j)
                at = 512 * j.lead
                for piece in pieces:
                    rows = piece.shape[0]
                    cols = piece.shape[1]
                    mm = nc.tensor.transpose(psf[0:cols, at:at + rows], piece, ident[0:rows, 0:rows])
                    at += rows
                mm.then_inc(full[j.lead], 1)

            pe.wait_ge(consts_in, 16 * 4)
            pe.wait_ge(rows_in, 16 * 11)
            turn(J["colsA"], [rowsA[0:76, :]])
            turn(J["colsB"], [rowsB[0:96, :]])
            pe.wait_ge(silc_ready, 1)
            for m in mods0:
                for half in range(2):
                    mod(m, half)
                for half in range(2):
                    mod_turn(m, half)
            pe.wait_ge(xn_ready, TT + CT)
            for k in range(KT):
                turn(J["hT", k], [x6[:, t, k * P:(k + 1) * P] for t in range(TT)])
            for k in range(KT):
                turn(J["hcT", k], [x6[:, TT + t, k * P:(k + 1) * P] for t in range(CT)])
            for k in range(KT):
                taken(J["hT", k])
                taken(J["hcT", k])
            w = arrived("w3")
            for name, n0 in (("dk", 0), ("dv", 512)):
                for t in range(TT):
                    tok_product(J[name, t], hT, t, w, n0)
                for t in range(CT):
                    tok_product(J[name, TT + t], hcT, t, w, n0)
            w = arrived("w2")
            for h in range(HH):
                feat_product(J["gate", h], hT, T, w, h * P)
            for t in range(TT):
                tok_product(J["dq", t], hT, t, w, 512)
            w_hv = arrived("w1")
            tok_product(J["hv", 0], hT, 0, w_hv, 512)
            pe.wait_ge(qk_normed, 2 * TT + CT)
            for h in range(AH):
                turn(J["qT", h], [qtok[:, t, h * P:(h + 1) * P] for t in range(TT)])
                turn(J["kT", h], [ktok[:, t, h * P:(h + 1) * P] for t in range(TT + CT)])
            for h in range(AH):
                taken(J["qT", h])
                taken(J["kT", h])
            for t in range(TT + CT):
                taken(J["dv", t])

            def scores(h, t):
                for m in range(2):
                    j = open_(J[f"s{m}", h, t])
                    f = slice(m * AD, (m + 1) * AD)
                    for k0, kn in ((0, T), (T, TC)):
                        mm = nc.tensor.matmul(psf[:, 512 * j.lead + k0:512 * j.lead + k0 + kn],
                                              qT[f, h, t * P:(t + 1) * P], kT[f, h, k0:k0 + kn],
                                              start=True, stop=True)
                    mm.then_inc(full[j.lead], 1)

            scores(0, 0)
            for n, (h, t) in enumerate(att):
                if n + 1 < len(att):
                    scores(*att[n + 1])
                pe.wait_ge(wgt_ready, n + 1)
                turn(J["wT", h, t], [wgt[:, k * P:(k + 1) * P] for k in range(TT + CT)])
                if n in hv_part:
                    tile, ks = hv_part[n]
                    j = J["hv", tile]
                    if ks[0] == 0:
                        open_(j)
                    left, at = (hT, tile) if tile < TT else (hcT, tile - TT)
                    for k in ks:
                        mm = nc.tensor.matmul(bank(j.lead), left[:, k, at * P:(at + 1) * P], w_hv[:, k, 512:1024],
                                              start=(k == 0), stop=(k == KT - 1))
                    if k == KT - 1:
                        mm.then_inc(full[j.lead], 1)
                taken(J["wT", h, t])
                j = open_(J["o", h, t])
                for k in range(TT + CT):
                    mm = nc.tensor.matmul(bank(j.lead, P), wT[:, k, :], vtok[:, k, h * P:(h + 1) * P],
                                          start=(k == 0), stop=(k == TT + CT - 1))
                mm.then_inc(full[j.lead], 1)
            for d, name, n0 in ((1, "w1", 0), (0, "w0", 512)):
                w = arrived(name)
                for h in range(HH):
                    feat_product(J["zc", d, h], hcT, TC, w, n0 + h * P)
                if d == 1:
                    pe.wait_ge(o_normed, TT)
                    for h in range(AH):
                        turn(J["oT", h], [oall[:, t, h * P:(h + 1) * P] for t in range(TT)])
                for h in range(HH):
                    feat_product(J["z", d, h], hT, T, w, n0 + h * P)
            for h in range(HH):
                feat_product(J["hq", h], hT, T, w, h * P)
            for t in range(TT + CT):
                taken(J["hv", t])
            for h in range(HH):
                taken(J["hq", h])
            pe.wait_ge(hk_ready, 4 * HH)
            def tail(d, h):
                taken(J["kdT", d, h])
                taken(J["sc", d, h, LEVELS])
                jo = open_(J["ho", d, h])
                order = range(NC) if d == 0 else range(NC - 1, -1, -1)
                for s, c in enumerate(order):
                    cc = slice(c * CH, (c + 1) * CH)
                    if s < NC - 1:
                        j = open_(J["kv", d, h, s])
                        nc.tensor.matmul(bank(j.lead, P), kdtok[:, c, :], hv[:, c, h * P:(h + 1) * P],
                                         start=True, stop=True).then_inc(full[j.lead], 1)
                    nc.tensor.matmul(bank(jo.lead)[:, cc], hv[:, c, h * P:(h + 1) * P], sc[:, cc],
                                     start=True, stop=False)
                    taken(J["kv", d, h, s - 1] if s else J["s0c", d, h])
                    mm = nc.tensor.matmul(bank(jo.lead)[:, cc], state[:, s % 2], qdec[:, cc],
                                          start=False, stop=True)
                mm.then_inc(full[jo.lead], 1)

            for n, (d, h) in enumerate(heads):
                for L in range(SLOT):
                    p = n * SLOT + L
                    if p - 4 in fills:
                        mod_turn(*fills[p - 4])
                    if p in fills:
                        mod(*fills[p])
                    if L == 1:
                        pe.wait_ge(kcd_ready, n + 1)
                        turn(J["kcT", d, h], [kcdec[:, t * P:(t + 1) * P] for t in range(CT)])
                    if L == 5:
                        taken(J["kcT", d, h])
                        j = open_(J["s0c", d, h])
                        for t in range(CT):
                            mm = nc.tensor.matmul(bank(j.lead, P), kcdtok[:, t, :], hv[:, TT + t, h * P:(h + 1) * P],
                                                  start=(t == 0), stop=(t == CT - 1))
                        mm.then_inc(full[j.lead], 1)
                    if L == 7:
                        pe.wait_ge(qdec_ready, n + 1)
                        turn(J["kdT", d, h], [kdec[:, c * CH:(c + 1) * CH] for c in range(NC)])
                    if L < LEVELS:
                        m = n * LEVELS + L
                        pe.wait_ge(lv_ready, m + 1)
                        pe.wait_ge(lvq_ready, m + 1)
                        kk, qq = lvK[m % 3], lvQ[m % 3]
                    else:
                        kk, qq = hk[d][:, h], hq[:, h]
                    j = open_(J["sc", d, h, L])
                    for c in range(NC):
                        cc = slice(c * CH, (c + 1) * CH)
                        mm = nc.tensor.matmul(bank(j.lead)[:, cc], kk[:, cc], qq[:, cc], start=True, stop=True)
                    mm.then_inc(full[j.lead], 1)
                    if L == 1 and n:
                        tail(*heads[n - 1])
            tail(*heads[-1])
            for h in range(HH):
                pe.wait_ge(sq_ready, h + 1)
                j = open_(J["ssq"]) if h == 0 else J["ssq"]
                for t in range(TT):
                    mm = nc.tensor.matmul(bank(j.lead)[:, h * TT + t:h * TT + t + 1], sq[:, h, t * P:(t + 1) * P],
                                          ones[:, 0:1], start=True, stop=True)
            mm.then_inc(full[j.lead], 1)
            pe.wait_ge(hrec_ready, 1)
            for h in range(HH):
                j = open_(J["rrow", h])
                for t in range(TT):
                    mm = nc.tensor.matmul(bank(j.lead)[:, t * P:(t + 1) * P],
                                          hstat[:, h * TT + t:h * TT + t + 1].broadcast_to((P, P)), ident[:, :],
                                          start=True, stop=True)
                mm.then_inc(full[j.lead], 1)

            def grow_row(j, l, which):
                open_(j)
                for k in range(KT):
                    mm = nc.tensor.matmul(psf[:, 512 * j.lead + k * P:512 * j.lead + (k + 1) * P],
                                          modc[:, l, which, k:k + 1].broadcast_to((P, P)), ident[:, :],
                                          start=True, stop=True)
                mm.then_inc(full[j.lead], 1)

            def exact(out_, left, right, first, last):
                (lh, ll), (rh, rl) = left, right
                nc.tensor.matmul(out_, ll, rh, start=first, stop=False)
                nc.tensor.matmul(out_, lh, rl, start=False, stop=False)
                return nc.tensor.matmul(out_, lh, rh, start=False, stop=last)

            def project_out(y):
                grow_row(J["grow", 0], 0, 2)
                w = arrived("wo")
                for t in range(TT):
                    for half in range(2):
                        tok_product(J["y", 0, t, half], y, t, w, 512 * half)

            def project_out_split():
                grow_row(J["grow", 1], 1, 2)
                arrived("co")
                w = ring_r[chunks["co"][0]]
                pe.wait_ge(y_lo_ready, KT)
                for t in range(TT):
                    ts = slice(t * P, (t + 1) * P)
                    for half in range(2):
                        j = open_(J["y", 1, t, half])
                        for k in range(KT):
                            if t == 0:
                                pe.wait_ge(wo_lo_ready, half * KT + k + 1)
                            mm = exact(bank(j.lead), (y_hi_r[:, k, ts], bT_r[:, k, ts]),
                                       (wo_hi_r[half][:, k], w[:, k, 512 * half:512 * half + 512]),
                                       k == 0, k == KT - 1)
                        mm.then_inc(full[j.lead], 1)

            for h in range(HH):
                taken(J["rrow", h])
            for h in range(AH):
                taken(J["oT", h])
            project_out(yT)

            def moe(l):
                pe.wait_ge(xn_ready, TT + CT + TT * (1 + 2 * l))
                for k in range(KT):
                    turn(J["h2T", l, k], [xn[:, t, k * P:(k + 1) * P] for t in range(TT)])
                pe.wait_ge(router_in[l], 16)
                for k in range(KT):
                    taken(J["h2T", l, k])
                j = open_(J["router", l])
                for k in range(KT):
                    q = k % 4
                    mm = nc.tensor.matmul(ps[32 * q:32 * q + 32, j.lead, :], router[:, k, :], h2T[:, k, :],
                                          start=(k < 4), stop=(k >= 4))
                mm.then_inc(full[j.lead], 1)
                taken(j)
                j = open_(J["logit", l])
                for t in range(TT):
                    mm = nc.tensor.matmul(bank(j.lead)[:, t * E:(t + 1) * E], parts[:, t * P:(t + 1) * P], fold[:, :],
                                          start=True, stop=True)
                mm.then_inc(full[j.lead], 1)
                pe.wait_ge(x_ready, 8 * (l + 1))
                grow_row(J["grow2", l], l, 5)
                pe.wait_ge(aff_ready, l + 1)
                turn(J["affT", l], [aff[:, t, :] for t in range(TT)])
                pe.wait_ge(slot_ready, l + 1)
                turn(J["slotT", l], [sel[0:E, 3, t * P:(t + 1) * P] for t in range(TT)])
                taken(J["grow2", l])
                for b in range(8):
                    pe.wait_ge(free[b], loop_base[l][b])
                base = loop_base[l]
                with pe.Fori(0, E // 2) as i:
                    def use(b, nth):
                        pe.wait_ge(free[b], i * LOOP_PER[b] + (base[b] + nth))

                    def made(b, nth):
                        pe.wait_ge(free[b], i * LOOP_PER[b] + (base[b] + nth + 1))

                    def product(b, j, left, nth, half_done):
                        for top in range(2):
                            for e in range(2):
                                q = (j + 2 * top + e) % 6
                                pe.wait_ge(exp_full[q], i * 32 + (l * 256 + 16 * nth[top]))
                            for k in range(4 * top, 4 * top + 4):
                                for half in range(2):
                                    for e in range(2):
                                        w = half_slot((j + 2 * top + e) % 6)
                                        mm = nc.tensor.matmul(ps[e * CAP:(e + 1) * CAP, b + half, :],
                                                              left[:, k, e * CAP:(e + 1) * CAP],
                                                              w[:, k % 4, half * 512:(half + 1) * 512],
                                                              start=(k == 0), stop=(k == KT - 1))
                            mm.then_inc(full[b] if top else half_done, 1)

                    pe.wait_ge(onehot_ready, i + (l * 8 + 1))
                    for half in range(2):
                        use(4 + half, 0)
                        for q in range(4):
                            k = 4 * half + q
                            for t in range(TT):
                                mm = nc.tensor.matmul(bank(4 + half)[:, q * P:(q + 1) * P], xn[:, t, k * P:(k + 1) * P],
                                                      onehot[:, t].rearrange("p e s -> p (e s)"),
                                                      start=(t == 0), stop=(t == TT - 1))
                        mm.then_inc(full[4 + half], 1)
                    use(6, 0)
                    pe.wait_ge(gated_ready, i + (l * 8 + 1))
                    for t in range(TT):
                        mm = nc.tensor.transpose(bank(6)[:, t * P:(t + 1) * P],
                                                 gated[:, t].rearrange("p e s -> p (e s)"), ident[:, :])
                    mm.then_inc(full[6], 1)
                    made(4, 0)
                    made(5, 0)
                    use(0, 0)
                    product(0, 0, xe, (1, 1), gates_half)
                    use(2, 0)
                    product(2, 4, xe, (1, 2), ups_half)
                    made(2, 0)
                    for half in range(2):
                        use(4 + half, 1)
                        for q in range(4):
                            mm = nc.tensor.transpose(bank(4 + half)[:, q * P:(q + 1) * P],
                                                     actb[:, (4 * half + q) * P:(4 * half + q + 1) * P], ident[:, :])
                        mm.then_inc(full[4 + half], 1)
                    use(0, 1)
                    made(4, 1)
                    made(5, 1)
                    product(0, 8, actT, (2, 2), downs_half)
                    made(6, 0)
                    made(0, 1)
                    for t in range(TT):
                        for half in range(2):
                            b = 6 + half
                            use(b, t + 1 - half)
                            nc.tensor.matmul(bank(b), spread[:, t * P:(t + 1) * P], ye[:, half * 512:(half + 1) * 512],
                                             start=True, stop=True).then_inc(full[b], 1)

            moe(0)
            pe.wait_ge(xn_ready, TT + CT + 2 * TT)
            for k in range(KT):
                turn(J["h3T", k], [xn[:, t, k * P:(k + 1) * P] for t in range(TT)])
            pe.wait_ge(h3_lo, KT)
            for u, (part, f) in enumerate(units):
                arrived("c" + part)
                w = ring_r[chunks["c" + part][0]]
                fs = slice(f * P, (f + 1) * P)
                pe.wait_ge(unit_lo_ready, u + 1)
                j = open_(J["conv", part, f])
                for k in range(KT):
                    mm = exact(bank(j.lead), (unit_hi_r[u % 2][:, k], w[:, k, fs]),
                               (hT_r[:, k], h3lo_r[:, k]),
                               k == 0, k == KT - 1)
                mm.then_inc(full[j.lead], 1)
            project_out_split()
            moe(1)

        @block.vector
        def _(dve):
            step = Chain(dve, dve_step)
            V = nc.vector

            def wait_full(j):
                dve.wait_ge(full[j.lead], j.count)

            step(V.memset(ones[:, :], 1.0))
            step(V.memset(reset[:, :, :], 1.0))
            step(V.memset(reset[:, 0, 0:T:CH], 0.0))
            step(V.memset(reset[:, 1, CH - 1:T:CH], 0.0))
            dve.wait_ge(consts_in, 16 * 4)
            wait_full(J["colsA"])
            V.tensor_copy(colsA[:, 0:76], bank(0, 76)).then_inc(free[0], 1)
            dve.wait_ge(free[0], 1)
            step(V.memset(silc[:, :, :], 0.0))
            step(V.memset(router[:, :, :], 0.0))
            step(V.tensor_reduce(fold[:, :], ident[:, :].rearrange("p (q w) -> p w q", w=32)[:, 0:E], AX, ALU.add))
            V.tensor_copy(silc[:, :, 0:2].rearrange("p k w -> p w k"), colsA[:, 0:16].rearrange("p (w k) -> p w k", w=2)).then_inc(cols_ready, 1)
            wait_full(J["colsB"])
            V.tensor_copy(colsB[:, :], bank(1, 96)).then_inc(free[1], 1)
            dve.wait_ge(free[1], 1)
            dve.wait_ge(rows_in, 16 * 11)
            lv = lamv.rearrange("p (r n) -> p r n", r=4)
            step(V.tensor_tensor(ta[:, 0:2 * AD].rearrange("p (r n) -> p r n", r=2), lv[:, 0::2], lv[:, 1::2], ALU.mult))
            V.tensor_reduce(small[:, 0:2], ta[:, 0:2 * AD].rearrange("p (r n) -> p r n", r=2), AX, ALU.add).then_inc(lam_dots, 1)
            dve.wait_ge(lam_exps, 1)
            step(V.tensor_tensor(small[:, 4:5], small[:, 2:3], small[:, 3:4], ALU.subtract))
            step(V.tensor_scalar(small[:, 5:6], small[:, 4:5], LAM_INIT, -1.0, ALU.add, ALU.mult))
            step(V.tensor_scalar(gains[:, 2 * AD:4 * AD], gains[:, 2 * AD:4 * AD], 1.0 - LAM_INIT, None, ALU.mult))

            def root(src, dst, n, scale, which):
                sem_in, sem_out, count = which
                V.tensor_scalar(dst, src, scale, EPS, ALU.mult, ALU.add).then_inc(sem_in, 1)
                dve.wait_ge(sem_out, count)
                step(V.reciprocal(dst, dst))

            dve.wait_ge(squares_ready, TT + CT)
            rstd = small[:, 16:16 + TT + CT]
            root(small[:, 8:8 + TT + CT], rstd, TT + CT, 1.0 / D, (means_ready, roots_ready, 1))
            for t in range(TT + CT):
                V.tensor_scalar(x6[:, t], x6[:, t], rstd[:, t:t + 1], None, ALU.mult).then_inc(xn_ready, 1)

            def take_mod(m, half):
                l, jj = m
                j = J["modc", m, half]
                wait_full(j)
                pv = bank(j.lead, KT).rearrange("p (k w) -> p k w", w=2)
                kk = slice(4 * half, 4 * half + 4)
                b0 = (6 * l + jj) * KT + 4 * half
                if l == 0 and jj < 2:
                    step(V.tensor_tensor(modx[:, jj, kk], pv[:, :, 1], colsB[:, b0:b0 + 4], ALU.add))
                V.tensor_tensor(modc[:, l, jj, kk], pv[:, :, 0], colsB[:, b0:b0 + 4], ALU.add).then_inc(free[j.lead], 1)
                dve.wait_ge(free[j.lead], j.count)
                if jj in (1, 4):
                    n = (0 if jj == 1 else 2) + l
                    g0 = (16 if jj == 1 else 32) + l * KT + 4 * half
                    V.scalar_tensor_tensor(scaleA[:, n, kk], modc[:, l, jj, kk], 1.0, colsA[:, g0:g0 + 4],
                                           ALU.add, ALU.mult).then_inc(scale_ready, 1)
                    if m == (0, 1):
                        V.scalar_tensor_tensor(scaleA[:, 4, kk], modx[:, 1, kk], 1.0, colsA[:, g0:g0 + 4],
                                               ALU.add, ALU.mult).then_inc(scale_ready, 1)

            for m in mods0:
                for half in range(2):
                    take_mod(m, half)
            dve.wait_ge(scale_ready, 4)

            def modulate(j, dst, k, gain, shift, n):
                wait_full(j)
                V.tensor_scalar(dst[:, k], bank(j.lead, n), gain[:, k:k + 1], shift[:, k:k + 1],
                                ALU.mult, ALU.add).then_inc(free[j.lead], 1)

            for k in range(1, KT, 2):
                modulate(J["hT", k], hT, k, scaleA[:, 0], modc[:, 0, 0], T)
            for k in range(1, KT, 2):
                modulate(J["hcT", k], hcT, k, scaleA[:, 4], modx[:, 0], TC)
            for n, (arr, t, g0, rot) in enumerate([(ktok, t, AD, t < TT) for t in range(TT + CT)]
                                                  + [(qtok, t, 0, True) for t in range(TT)]):
                x8 = arr[:, t].rearrange("p (g n) -> p g n", n=AD)
                r8 = small[:, 32 + 8 * (n % 2):40 + 8 * (n % 2)]
                dve.wait_ge(qk_squares, n + 1)
                step(V.tensor_reduce(r8, tsq[:, n % 2].rearrange("p (g n) -> p g n", n=AD), AX, ALU.add))
                root(r8, r8, 8, 1.0 / AD, (qk_means, qk_roots, n + 1))
                step(V.tensor_tensor(x8, x8, r8[:, :, None].broadcast_to((P, 8, AD)), ALU.mult))
                gain = gains[:, g0:g0 + AD][:, None, :].broadcast_to((P, 8, AD))
                last = V.tensor_tensor(x8, x8, gain, ALU.mult)
                if rot:
                    step(last)
                    cos8 = rope_cos[:, t][:, None, :].broadcast_to((P, 8, AD))
                    halves = arr[:, t].rearrange("p (g a w n) -> p (g a) w n", a=2, w=2, n=AD // 4)
                    sw = trot[:, 1].rearrange("p (g a w n) -> p (g a) w n", a=2, w=2, n=AD // 4)
                    step(V.tensor_tensor(trot[:, 0].rearrange("p (g n) -> p g n", n=AD), x8, cos8, ALU.mult))
                    for w in range(2):
                        sin8 = rope_sin[:, t].rearrange("p (a w n) -> p a w n", a=2, w=2)[:, :, w]
                        sin8 = sin8[:, None].broadcast_to((P, 8, 2, AD // 4))
                        o4 = sw[:, :, w].rearrange("p (g a) n -> p g a n", a=2)
                        i4 = halves[:, :, 1 - w].rearrange("p (g a) n -> p g a n", a=2)
                        step(V.tensor_tensor(o4, i4, sin8, ALU.mult))
                    last = V.tensor_tensor(arr[:, t], trot[:, 0], trot[:, 1], ALU.add)
                last.then_inc(qk_normed, 1)
            dve.wait_ge(level_masks_in, 16)
            step(V.tensor_copy(masks[:, :, :, :].rearrange("p d l n -> p (d l n)"), masks_in))
            for h in range(AH):
                j = J["qT", h]
                wait_full(j)
                V.tensor_copy(qT[:, h], bank(j.lead)).then_inc(free[j.lead], 1)

            def maxima(n):
                h, t = att[n]
                for m in range(2):
                    j = J[f"s{m}", h, t]
                    wait_full(j)
                    mx = astat[:, n, m:m + 1]
                    step(V.tensor_reduce(mx, psf[:, 512 * j.lead:512 * j.lead + T + TC], AX, ALU.max))
                    V.tensor_scalar(mx, mx, -AD ** -0.5, None, ALU.mult).then_inc(max_ready, 1)

            maxima(0)
            for n, (h, t) in enumerate(att):
                j = J["s1", h, t]
                dve.wait_ge(free[j.lead], j.count)
                j = J["s0", h, t]
                dve.wait_ge(free[j.lead], j.count)
                step(V.reciprocal(astat[:, n, 4:6], astat[:, n, 2:4]))
                step(V.scalar_tensor_tensor(astat[:, n, 6:7], astat[:, n, 5:6], small[:, 5:6], astat[:, n, 2:3],
                                            ALU.mult, ALU.mult))
                if n:
                    jw = J["wT", *att[n - 1]]
                    dve.wait_ge(full[jw.lead], jw.count)
                V.scalar_tensor_tensor(wgt, prob[:, n % 2, 1], astat[:, n, 6:7], prob[:, n % 2, 0],
                                       ALU.mult, ALU.add).then_inc(wgt_ready, 1)
                if n + 1 < len(att):
                    maxima(n + 1)
            dve.wait_ge(o_squares, len(att))
            root(small[:, 80:96], small[:, 80:96], 16, 1.0 / (2 * AD), (o_means, o_roots, 1))
            for t in range(TT):
                o4 = oall[:, t].rearrange("p (h n) -> p h n", h=AH)
                step(V.tensor_tensor(o4, o4, small[:, 80 + 4 * t:84 + 4 * t][:, :, None].broadcast_to((P, AH, P)), ALU.mult))
                V.tensor_tensor(o4, o4, gains[:, 2 * AD:4 * AD][:, None, :].broadcast_to((P, AH, P)),
                                ALU.mult).then_inc(o_normed, 1)
            n = 0
            for d in (1, 0):
                for c, B, K, N in (("zc", cb[d], ck[d], TC), ("z", hb[d], hk[d], T)):
                    for h in range(HH):
                        j = J[c, d, h]
                        dve.wait_ge(log_ready, n + 1)
                        l1 = spl[:, n % 2, 0:N]
                        step(V.scalar_tensor_tensor(B[:, h], bank(j.lead, N), 0.0, l1, ALU.min, ALU.subtract))
                        V.scalar_tensor_tensor(K[:, h], bank(j.lead, N), 0.0, l1, ALU.max, ALU.add).then_inc(free[j.lead], 1)
                        rev = slice(None, None, -1) if d else slice(None)
                        keep = ones[:, 0:N] if c == "zc" else reset[:, d]
                        V.tensor_tensor_scan(B[:, h][:, rev], keep[:, rev], B[:, h][:, rev], 0.0,
                                             ALU.mult, ALU.add).then_inc(b_ready, 1)
                        n += 1
            dve.wait_ge(hk_ready, 4 * HH)
            for h in range(HH):
                j = J["hq", h]
                dve.wait_ge(free[j.lead], j.count)
            def take_scores(p):
                d, h = heads[p // SLOT]
                L = p % SLOT
                if L == 0:
                    if p:
                        j = J[("ho",) + heads[p // SLOT - 1]]
                        dve.wait_ge(full[j.lead], j.count)
                    if h == 0:
                        step(V.memset(sc, 0.0))
                j = J["sc", d, h, L]
                wait_full(j)
                mk = masks[:, d, L][:, None, :].broadcast_to((P, NC, CH))
                V.copy_predicated(sc.rearrange("p (c n) -> p c n", c=NC), mk,
                                  bank(j.lead).rearrange("p (c n) -> p c n", c=NC)).then_inc(free[j.lead], 1)
                dve.wait_ge(free[j.lead], j.count)

            def states(d, h):
                order = range(NC) if d == 0 else range(NC - 1, -1, -1)
                j = J["s0c", d, h]
                dve.wait_ge(free[j.lead], j.count)
                for s, c in enumerate(order):
                    if s < NC - 1:
                        j = J["kv", d, h, s]
                        wait_full(j)
                        V.scalar_tensor_tensor(state[:, (s + 1) % 2], state[:, s % 2], small[:, 100 + c:101 + c],
                                               bank(j.lead, P), ALU.mult, ALU.add).then_inc(free[j.lead], 1)
                        dve.wait_ge(free[j.lead], j.count)

            def sum_directions(d, h):
                if d == 0:
                    j = J["ho", 0, h]
                    wait_full(j)
                    V.tensor_tensor(ho[:, h], bank(j.lead), ho[:, h], ALU.add).then_inc(free[j.lead], 1)

            for n, (d, h) in enumerate(heads):
                for L in range(SLOT):
                    p = n * SLOT + L
                    if p - 5 in fills:
                        take_mod(*fills[p - 5])
                    if L < LEVELS:
                        m = n * LEVELS + L
                        dve.wait_ge(decay_ready, m + 1)
                        V.tensor_tensor(lvK[m % 3], lvE[m % 3], hk[d][:, h], ALU.mult).then_inc(lv_ready, 1)
                    if L == 0:
                        dve.wait_ge(cdec_ready, n + 1)
                        V.tensor_tensor(kcdec, kcdec, ck[d][:, h], ALU.mult).then_inc(kcd_ready, 1)
                    if L == 2 and n:
                        states(*heads[n - 1])
                    if L == 4 and n:
                        sum_directions(*heads[n - 1])
                    if L == 5:
                        dve.wait_ge(ends_ready, n + 1)
                        end = 0 if d else CH - 1
                        step(V.tensor_copy(small[:, 100:100 + NC], qdec[:, end::CH]))
                        step(V.tensor_tensor(qdec, qdec, hq[:, h], ALU.mult))
                        V.tensor_tensor(kdec, kdec, hk[d][:, h], ALU.mult).then_inc(qdec_ready, 1)
                    if p >= 2:
                        take_scores(p - 2)
            take_scores(p - 1)
            take_scores(p)
            states(*heads[-1])
            sum_directions(*heads[-1])
            for h in range(HH):
                step(V.scalar_tensor_tensor(yT[:, h], ho[:, h], colsA[:, 48 + h:49 + h], yT[:, h], ALU.mult, ALU.mult))
            j = J["ssq"]
            wait_full(j)
            V.tensor_scalar(hstat, bank(j.lead, HH * TT), 1.0 / HD, EPS, ALU.mult, ALU.add).then_inc(free[j.lead], 1)
            dve.wait_ge(hroot_out, 1)
            V.reciprocal(hstat, hstat).then_inc(hrec_ready, 1)
            for h in range(HH):
                j = J["rrow", h]
                wait_full(j)
                V.tensor_tensor(yT[:, h], bank(j.lead), yT[:, h], ALU.mult).then_inc(free[j.lead], 1)

            def add_out(l):
                j = J["grow", l]
                dve.wait_ge(free[j.lead], j.count)
                if l == 0:
                    dve.wait_ge(x_again, 16)
                for t in range(TT):
                    for half in range(2):
                        hs = slice(512 * half, 512 * half + 512)
                        j = J["y", l, t, half]
                        wait_full(j)
                        V.tensor_tensor(xtmp[:, half], bank(j.lead), grow[:, hs], ALU.mult).then_inc(free[j.lead], 1)
                        dve.wait_ge(free[j.lead], j.count)
                        V.tensor_tensor(xs[:, t, hs], xs[:, t, hs], xtmp[:, half], ALU.add).then_inc(x_ready, 1)

            def norm(nth):
                dve.wait_ge(squares_ready, TT + CT + TT * nth)
                root(small[:, 8:8 + TT], rstd[:, 0:TT], TT, 1.0 / D, (means_ready, roots_ready, nth + 1))
                for t in range(TT):
                    V.tensor_scalar(xn[:, t], xs[:, t], rstd[:, t:t + 1], None, ALU.mult).then_inc(xn_ready, 1)

            def moe(l):
                norm(1 + 2 * l)
                for k in range(1, KT, 2):
                    modulate(J["h2T", l, k], h2T, k, scaleA[:, 2 + l], modc[:, l, 3], T)
                j = J["logit", l]
                wait_full(j)
                lg = bank(j.lead, TT * E).rearrange("p (t e) -> p t e", e=E)
                m4 = small[:, 120:124]
                step(V.tensor_reduce(m4, lg, AX, ALU.max))
                V.tensor_tensor(aff[:, :, :], lg, m4[:, :, None].broadcast_to((P, TT, E)), ALU.subtract).then_inc(free[j.lead], 1)
                dve.wait_ge(logit_exp, l + 1)
                step(V.tensor_reduce(m4, aff[:, :, :], AX, ALU.add))
                step(V.reciprocal(m4, m4))
                V.tensor_tensor(aff[:, :, :], aff[:, :, :], m4[:, :, None].broadcast_to((P, TT, E)), ALU.mult).then_inc(aff_ready, 1)
                j = J["affT", l]
                wait_full(j)
                row = [sel[0:E, n] for n in range(4)]
                V.tensor_copy(row[0], bank(j.lead)[0:E, :]).then_inc(free[j.lead], 1)
                dve.wait_ge(free[j.lead], j.count)
                top = small[0:E, 128:136]
                for r in range(CAP // 8):
                    step(V.max(top, row[min(r, 1)]))
                    step(V.match_replace(row[1], top, row[min(r, 1)], -1.0))
                step(V.tensor_scalar(row[2], row[1], 0.0, None, ALU.is_lt))
                step(V.tensor_tensor_scan(row[0], row[2], row[2], 0.0, ALU.add, ALU.max))
                step(V.tensor_tensor(row[0], row[0], row[2], ALU.mult))
                V.tensor_scalar(row[3], row[0], -1.0, None, ALU.add).then_inc(slot_ready, 1)
                j = J["slotT", l]
                wait_full(j)
                V.tensor_copy(slotc[:, :, :], bank(j.lead, TT * E).rearrange("p (t e) -> p t e", e=E)).then_inc(free[j.lead], 1)
                dve.wait_ge(free[j.lead], j.count)
                base = loop_base[l]
                with dve.Fori(0, E // 2) as i:
                    def wait_use(b, nth):
                        dve.wait_ge(full[b], i * LOOP_PER[b] + (base[b] + nth + 1))
                        return bank(b)

                    pair = (P, TT, 2, CAP)
                    slots = slotc[:, :, bass.ds(i * 2, 2)][:, :, :, None].broadcast_to(pair)
                    gates = aff[:, :, bass.ds(i * 2, 2)][:, :, :, None].broadcast_to(pair)
                    V.tensor_tensor(onehot, slots, iota[:, None, None, :].broadcast_to(pair), ALU.is_equal).then_inc(onehot_ready, 1)
                    dve.wait_ge(onehot_ready, i + (l * 8 + 1))
                    V.tensor_tensor(gated, onehot, gates, ALU.mult).then_inc(gated_ready, 1)
                    g = wait_use(5, 0)
                    for q in range(4):
                        k = 4 + q
                        ins = V.tensor_scalar(xe[:, k], g[:, q * P:(q + 1) * P], scaleA[:, 2 + l, k:k + 1],
                                              modc[:, l, 3, k:k + 1], ALU.mult, ALU.add)
                    ins.then_inc(free[5], 1)
                    wait_use(2, 0)
                    dve.wait_ge(free[0], i * 2 + (base[0] + 1))
                    V.tensor_tensor(actb, psf[:, 1024:2048], sil, ALU.mult).then_inc(free[2], 1)
                    V.tensor_copy(actT[:, 4:8].rearrange("p k n -> p (k n)"), wait_use(5, 1)).then_inc(free[5], 1)
                    wait_use(0, 1)
                    V.tensor_tensor(ye, psf[:, 0:1024], grow[:, :], ALU.mult).then_inc(free[0], 1)
                    for t in range(TT):
                        for half in range(2):
                            y = wait_use(6 + half, t + 1 - half)
                            hs = slice(512 * half, 512 * half + 512)
                            V.tensor_tensor(xs[:, t, hs], y, xs[:, t, hs], ALU.add).then_inc(free[6 + half], 1)

            add_out(0)
            moe(0)
            norm(2)
            def split_h3(k):
                dve.wait_ge(h3_hi, k + 1)
                V.tensor_tensor(h3lo_r[:, k], h3lo[:, k], hT_r[:, k].bitcast(F32), ALU.subtract).then_inc(h3_lo, 1)

            for k in range(0, KT, 2):
                modulate(J["h3T", k + 1], h3lo, k + 1, scaleA[:, 1], modc[:, 1, 0], T)
                if k:
                    split_h3(k - 2)
                    split_h3(k - 1)
            split_h3(KT - 2)
            split_h3(KT - 1)
            step(V.memset(uT[:, 0:1], 0.0))
            step(V.memset(uT[:, T + 1:T + 2], 0.0))

            def split_unit(u):
                part, f = units[u]
                dve.wait_ge(unit_hi_ready, u + 1)
                slot, fs = chunks["c" + part][0], slice(f * P, (f + 1) * P)
                V.tensor_tensor(ring_r[slot][:, :, fs], ring[:, slot, :, fs], unit_hi_r[u % 2][:].bitcast(F32), ALU.subtract).then_inc(unit_lo_ready, 1)

            def split_y(k):
                dve.wait_ge(y_hi_ready, k + 1)
                V.tensor_tensor(bT_r[:, k], bT[:, k], y_hi_r[:, k].bitcast(F32), ALU.subtract).then_inc(y_lo_ready, 1)

            split_unit(0)
            split_unit(1)
            for u, (part, f) in enumerate(units):
                if u + 2 < len(units):
                    split_unit(u + 2)
                if part != "v":
                    continue
                j = J["conv", "c", f]
                dve.wait_ge(free[j.lead], j.count)
                j = J["conv", "b", f]
                dve.wait_ge(free[j.lead], j.count)
                j = J["conv", "v", f]
                wait_full(j)
                V.tensor_tensor(uT[:, 1:T + 1], bank(j.lead), cT[:, f], ALU.mult).then_inc(free[j.lead], 1)
                dve.wait_ge(free[j.lead], j.count)
                w = [colsA[:, 52 + 8 * n + f:53 + 8 * n + f] for n in range(3)]
                step(V.tensor_scalar(vT, uT[:, 0:T], w[0], None, ALU.mult))
                step(V.scalar_tensor_tensor(vT, uT[:, 1:T + 1], w[1], vT, ALU.mult, ALU.add))
                step(V.scalar_tensor_tensor(vT, uT[:, 2:T + 2], w[2], vT, ALU.mult, ALU.add))
                V.tensor_tensor(bT[:, f], vT, bT[:, f], ALU.mult).then_inc(ycT_ready, 1)
                dve.wait_ge(ycT_ready, f + 1)
                if f:
                    split_y(f - 1)
            split_y(KT - 1)
            slot = chunks["co"][0]
            for half in range(2):
                hs = slice(512 * half, 512 * half + 512)
                for k in range(KT):
                    dve.wait_ge(wo_hi_ready, half * KT + k + 1)
                    V.tensor_tensor(ring_r[slot][:, k, hs], ring[:, slot, k, hs], wo_hi_r[half][:, k].bitcast(F32), ALU.subtract).then_inc(wo_lo_ready, 1)
            add_out(1)
            moe(1)

        @block.scalar
        def _(act):
            S = nc.scalar
            step = Chain(act, act_step)

            def wait_full(j):
                act.wait_ge(full[j.lead], j.count)

            def copy(j, dst, n=512, func=ACT.Copy):
                wait_full(j)
                S.activation(dst, psf[:, 512 * j.lead:512 * j.lead + n], func).then_inc(free[j.lead], 1)

            def modulate(j, dst, k, gain, shift, n):
                wait_full(j)
                S.activation(dst[:, k], bank(j.lead, n), ACT.Identity, bias=shift[:, k:k + 1],
                             scale=gain[:, k:k + 1]).then_inc(free[j.lead], 1)

            act.wait_ge(cols_ready, 1)
            S.activation(silc[:, :, 0:2], silc[:, :, 0:2], ACT.Silu).then_inc(silc_ready, 1)

            def row_mod(m, half):
                j = J["modr", m, half]
                wait_full(j)
                S.activation(modrow[:, half * 512:(half + 1) * 512], bank(j.lead), ACT.Copy).then_inc(free[j.lead], 1)

            act.wait_ge(lam_dots, 1)
            S.activation(small[:, 2:4], small[:, 0:2], ACT.Exp).then_inc(lam_exps, 1)
            for n, t in enumerate([4, 5, 0, 1, 2, 3]):
                act.wait_ge(x_in, 16 * (TT + CT))
                if n:
                    act.wait_ge(squares_ready, n)
                S.activation(junk, x6[:, t], ACT.Square, accum_out=small[:, 8 + t:9 + t]).then_inc(squares_ready, 1)
            act.wait_ge(means_ready, 1)
            S.activation(rstd_(small, TT + CT), rstd_(small, TT + CT), ACT.Sqrt).then_inc(roots_ready, 1)
            for m in mods0:
                for half in range(2):
                    row_mod(m, half)
            act.wait_ge(scale_ready, 4)
            for k in range(0, KT, 2):
                modulate(J["hT", k], hT, k, scaleA[:, 0], modc[:, 0, 0], T)
            for k in range(0, KT, 2):
                modulate(J["hcT", k], hcT, k, scaleA[:, 4], modx[:, 0], TC)

            def take_qk(n, j, arr, t):
                copy(j, arr[:, t])
                act.wait_ge(free[j.lead], j.count)
                if n >= 2:
                    act.wait_ge(qk_means, n - 1)
                S.activation(tsq[:, n % 2], arr[:, t], ACT.Square).then_inc(qk_squares, 1)

            def roots_qk(n):
                act.wait_ge(qk_means, n + 1)
                r8 = small[:, 32 + 8 * (n % 2):40 + 8 * (n % 2)]
                S.activation(r8, r8, ACT.Sqrt).then_inc(qk_roots, 1)

            for t in range(TT + CT):
                take_qk(t, J["dk", t], ktok, t)
                roots_qk(t)
            for t in range(TT + CT):
                copy(J["dv", t], vtok[:, t])
            for h in range(HH):
                copy(J["gate", h], yT[:, h], func=ACT.Silu)
            for t in range(TT):
                take_qk(TT + CT + t, J["dq", t], qtok, t)
                roots_qk(TT + CT + t)
            copy(J["hv", 0], hv[:, 0])
            for h in range(AH):
                copy(J["kT", h], kT[:, h], T + TC)

            def exps(n):
                h, t = att[n]
                if n >= 2:
                    act.wait_ge(wgt_ready, n - 1)
                for m in range(2):
                    j = J[f"s{m}", h, t]
                    act.wait_ge(max_ready, 2 * n + m + 1)
                    S.activation(prob[:, n % 2, m], psf[:, 512 * j.lead:512 * j.lead + T + TC], ACT.Exp,
                                 bias=astat[:, n, m:m + 1], scale=AD ** -0.5,
                                 accum_out=astat[:, n, 2 + m:3 + m]).then_inc(free[j.lead], 1)

            exps(0)
            for n, (h, t) in enumerate(att):
                copy(J["wT", h, t], wT.rearrange("p k n -> p (k n)"), T + TC)
                if n + 1 < len(att):
                    exps(n + 1)
                j = J["o", h, t]
                wait_full(j)
                S.activation(oall[:, t, h * P:(h + 1) * P], bank(j.lead, P), ACT.Copy,
                             scale=astat[:, n, 4:5]).then_inc(free[j.lead], 1)
                act.wait_ge(free[j.lead], j.count)
                if n:
                    act.wait_ge(o_squares, n)
                S.activation(sqo, oall[:, t, h * P:(h + 1) * P], ACT.Square,
                             accum_out=small[:, 80 + 4 * t + h:81 + 4 * t + h]).then_inc(o_squares, 1)
                if n in hv_part and hv_part[n][1][-1] == KT - 1:
                    tile = hv_part[n][0]
                    copy(J["hv", tile], hv[:, tile])
            act.wait_ge(o_means, 1)
            S.activation(small[:, 80:96], small[:, 80:96], ACT.Sqrt).then_inc(o_roots, 1)
            for h in range(AH):
                copy(J["oT", h], yT[:, AH + h])
            gates = [(J[c, d, h], K[:, h], N) for d in (1, 0)
                     for c, K, N in (("zc", ck[d], TC), ("z", hk[d], T)) for h in range(HH)]

            def keys(n):
                for j, key, _ in gates[n:n + 2]:
                    act.wait_ge(free[j.lead], j.count)
                    S.activation(key, key, ACT.Exp, scale=-1.0).then_inc(hk_ready, 1)

            for n in range(0, len(gates), 2):
                for m in (n, n + 1):
                    j, _, N = gates[m]
                    buf = spl[:, m % 2, 0:N]
                    wait_full(j)
                    if m >= 2:
                        act.wait_ge(free[gates[m - 2][0].lead], gates[m - 2][0].count)
                    step(S.activation(buf, bank(j.lead, N), ACT.Abs))
                    step(S.activation(buf, buf, ACT.Exp, scale=-1.0))
                if n:
                    keys(n - 2)
                for m in (n, n + 1):
                    buf = spl[:, m % 2, 0:gates[m][2]]
                    S.activation(buf, buf, ACT.Ln, bias=1.0).then_inc(log_ready, 1)
            keys(len(gates) - 2)
            for h in range(HH):
                copy(J["hq", h], hq[:, h])
            act.wait_ge(b_ready, 4 * HH)
            def take_turned(d, h):
                copy(J["kdT", d, h], kdtok.rearrange("p c n -> p (c n)"))

            def take_out(d, h):
                if d == 1:
                    copy(J["ho", d, h], ho[:, h])

            for n, (d, h) in enumerate(heads):
                before = heads[n - 1] if n else None
                for L in range(SLOT):
                    p = n * SLOT + L
                    if p - 3 in fills:
                        row_mod(*fills[p - 3])
                    if L == 0:
                        ce = 0 if d else TC - 1
                        if n:
                            copy(J[("s0c",) + before], state[:, 0], P)
                            j = J[("kcT",) + before]
                            act.wait_ge(full[j.lead], j.count)
                        S.activation(kcdec, cb[d][:, h], ACT.Exp, scale=-1.0,
                                     bias=cb[d][:, h, ce:ce + 1]).then_inc(cdec_ready, 1)
                    if L == 1 and n:
                        take_turned(*before)
                    if L == 4:
                        copy(J["kcT", d, h], kcdtok.rearrange("p t n -> p (t n)"), TC)
                    if L == 5:
                        if n:
                            j = J[("ho",) + before]
                            wait_full(j)
                            take_out(*before)
                        S.activation(qdec, hb[d][:, h], ACT.Exp)
                        for c in range(NC):
                            e = c * CH + (0 if d else CH - 1)
                            cc = slice(c * CH, (c + 1) * CH)
                            ins = S.activation(kdec[:, cc], hb[d][:, h, cc], ACT.Exp, scale=-1.0, bias=hb[d][:, h, e:e + 1])
                        ins.then_inc(ends_ready, 1)
                    if L < LEVELS:
                        m = n * LEVELS + L
                        act.wait_ge(diff_ready, m + 1)
                        step(S.activation(lvE[m % 3], lvE[m % 3], ACT.Abs))
                        S.activation(lvE[m % 3], lvE[m % 3], ACT.Exp, scale=-1.0).then_inc(decay_ready, 1)
            copy(J[("s0c",) + heads[-1]], state[:, 0], P)
            take_turned(*heads[-1])
            take_out(*heads[-1])
            for h in range(HH):
                j = J["ho", 0, h]
                act.wait_ge(free[j.lead], j.count)
                S.activation(sq[:, h], ho[:, h], ACT.Square).then_inc(sq_ready, 1)

            j = J["ssq"]
            act.wait_ge(free[j.lead], j.count)
            S.activation(hstat, hstat, ACT.Sqrt).then_inc(hroot_out, 1)

            def squares(nth, x_count):
                if nth == 2:
                    for b in (6, 7):
                        act.wait_ge(free[b], loop_base[0][b] + LOOP_PER[b] * E // 2)
                for t in range(TT):
                    n = TT + CT + TT * (nth - 1) + t
                    act.wait_ge(x_ready, x_count - 2 * (TT - 1 - t))
                    act.wait_ge(squares_ready, n)
                    S.activation(junk_moe, xs[:, t], ACT.Square, accum_out=small[:, 8 + t:9 + t]).then_inc(squares_ready, 1)
                act.wait_ge(means_ready, nth + 1)
                S.activation(rstd_(small, TT), rstd_(small, TT), ACT.Sqrt).then_inc(roots_ready, 1)

            def moe(l):
                squares(1 + 2 * l, 8 + 8 * l)
                for k in range(0, KT, 2):
                    modulate(J["h2T", l, k], h2T, k, scaleA[:, 2 + l], modc[:, l, 3], T)
                copy(J["router", l], parts)
                j = J["logit", l]
                act.wait_ge(free[j.lead], j.count)
                S.activation(aff[:, :, :], aff[:, :, :], ACT.Exp).then_inc(logit_exp, 1)
                copy(J["grow2", l], grow[:, :], D)
                base = loop_base[l]
                with act.Fori(0, E // 2) as i:
                    def wait_use(b, nth):
                        act.wait_ge(full[b], i * LOOP_PER[b] + (base[b] + nth + 1))
                        return bank(b)

                    g = wait_use(4, 0)
                    for k in range(4):
                        ins = S.activation(xe[:, k], g[:, k * P:(k + 1) * P], ACT.Identity,
                                           bias=modc[:, l, 3, k:k + 1], scale=scaleA[:, 2 + l, k:k + 1])
                    ins.then_inc(free[4], 1)
                    S.activation(spread, wait_use(6, 0), ACT.Copy).then_inc(free[6], 1)
                    wait_use(0, 0)
                    S.activation(sil, psf[:, 0:1024], ACT.Silu).then_inc(free[0], 1)
                    S.activation(actT[:, 0:4].rearrange("p k n -> p (k n)"), wait_use(4, 1), ACT.Copy).then_inc(free[4], 1)

            copy(J["grow", 0], grow[:, :], D)
            moe(0)
            squares(2, 8)
            for k in range(KT):
                j = J["h3T", k]
                if k % 2 == 0:
                    modulate(j, h3lo, k, scaleA[:, 1], modc[:, 1, 0], T)
                act.wait_ge(free[j.lead], j.count)
                S.activation(hT_r[:, k], h3lo[:, k], ACT.Copy).then_inc(h3_hi, 1)

            def high_unit(u):
                part, f = units[u]
                slot, n = chunks["c" + part]
                act.wait_ge(ring_full[slot], 16 * n)
                if u >= 2:
                    j = J[("conv",) + units[u - 2]]
                    act.wait_ge(full[j.lead], j.count)
                S.activation(unit_hi_r[u % 2][:], ring[:, slot, :, f * P:(f + 1) * P],
                             ACT.Copy).then_inc(unit_hi_ready, 1)

            def high_y(k):
                act.wait_ge(ycT_ready, k + 1)
                S.activation(y_hi_r[:, k], bT[:, k], ACT.Copy).then_inc(y_hi_ready, 1)

            def high_wo(half):
                slot, n = chunks["co"]
                act.wait_ge(ring_full[slot], 16 * n)
                for k in range(KT):
                    S.activation(wo_hi_r[half][:, k], ring[:, slot, k, 512 * half:512 * half + 512],
                                 ACT.Copy).then_inc(wo_hi_ready, 1)

            high_unit(0)
            high_unit(1)
            for u, (part, f) in enumerate(units):
                if u + 2 < len(units):
                    high_unit(u + 2)
                if part == "b":
                    copy(J["conv", "b", f], bT[:, f])
                elif part == "c":
                    copy(J["conv", "c", f], cT[:, f])
                elif f:
                    high_y(f - 1)
            j = J["conv", "v", KT - 1]
            act.wait_ge(full[j.lead], j.count)
            high_y(KT - 1)
            high_wo(0)
            high_wo(1)
            copy(J["grow", 1], grow[:, :], D)
            moe(1)

        @block.gpsimd
        def _(pool):
            n = 0
            pool.wait_ge(b_ready, 4 * HH)
            for h in range(HH):
                j = J["hq", h]
                pool.wait_ge(full[j.lead], j.count)
            def difference(m):
                n, L = m // LEVELS, m % LEVELS
                d, h = heads[n]
                half = CH >> (L + 1)
                if m >= 3:
                    pool.wait_ge(lv_ready, m - 2)
                src = hb[d][:, h].rearrange("p (b w) -> p b w", w=2 * half)
                mid = src[:, :, half - 1 + d:half + d].broadcast_to((P, T // (2 * half), 2 * half))
                nc.gpsimd.tensor_tensor(lvE[m % 3].rearrange("p (b w) -> p b w", w=2 * half), src, mid,
                                        ALU.subtract).then_inc(diff_ready, 1)

            levels = LEVELS * len(heads)
            difference(0)
            difference(1)
            for m in range(levels):
                d, h = heads[m // LEVELS]
                pool.wait_ge(decay_ready, m + 1)
                if m >= 3:
                    j = J["sc", *heads[(m - 3) // LEVELS], (m - 3) % LEVELS]
                    pool.wait_ge(full[j.lead], j.count)
                nc.gpsimd.tensor_tensor(lvQ[m % 3], lvE[m % 3], hq[:, h], ALU.mult).then_inc(lvq_ready, 1)
                pool.wait_ge(lvq_ready, m + 1)
                if m + 2 < levels:
                    difference(m + 2)


def rstd_(small, n):
    return small[:, 16:16 + n]


INPUTS = ["x", "c", "ctx", "c_ctx", "mod_w", "mod_b", "norm1_g", "norm2_g", "even_w_in", "even_w_out",
          "hgrn_norm_g", "diff_qnorm_g", "diff_knorm_g", "diff_lambda", "diff_subln_g", "conv_w_in",
          "conv_w", "conv_w_out", "router_w", "exp_w_gate", "exp_w_up", "exp_w_down"]


def shape_constants():
    n = AD // 2
    inv = (1.0 / (ROPE_THETA ** (np.arange(0, n, 2, dtype=np.float32) / np.float32(n)))).astype(np.float32)
    tok = np.arange(T)
    cos, sin = np.zeros((T, AD), np.float32), np.zeros((T, AD), np.float32)
    for axis, pos in enumerate((tok // GRID_W, tok % GRID_W)):
        ang = pos.astype(np.float32)[:, None] * inv[None, :]
        for w in range(2):
            at = slice(axis * n + w * (n // 2), axis * n + (w + 1) * (n // 2))
            cos[:, at] = np.cos(ang)
            sin[:, at] = np.sin(ang) * (-1.0, 1.0)[w]
    s = np.arange(CH)[:, None]
    t = np.arange(CH)[None, :]
    masks = np.zeros((P, 2, LEVELS + 1, CH), np.float32)
    for L in range(LEVELS):
        half = CH >> (L + 1)
        same = s // (2 * half) == t // (2 * half)
        masks[:, 0, L] = same & (s % (2 * half) < half) & (t % (2 * half) >= half)
        masks[:, 1, L] = same & (s % (2 * half) >= half) & (t % (2 * half) < half)
    masks[:, :, LEVELS] = (s == t)[:, None, :]

    def lay(v):
        return np.ascontiguousarray(v.reshape(TT, P, AD).transpose(1, 0, 2))

    return {"c_ident": np.eye(P, dtype=np.float32), "c_cos": lay(cos), "c_sin": lay(sin),
            "c_iota": np.tile(np.arange(CAP, dtype=np.float32), (P, 1)), "c_masks": masks.reshape(P, -1)}


def program(nc, arrays):
    a = {}
    for name, v in arrays.items():
        a[name] = nc.dram_tensor(name, v.shape, mybir.dt.from_np(v.dtype), kind="ExternalInput").ap()
    out = nc.dram_tensor("out_x", (1, T, D), F32, kind="ExternalOutput").ap()
    build(nc, a, out)


def kernel(**inputs):
    import concourse.bacc as bacc
    from concourse.bass_utils import run_bass_kernel_spmd as run

    arrays = {n: np.ascontiguousarray(inputs[n]) for n in INPUTS}
    arrays.update(shape_constants())
    nc = bacc.Bacc("TRN2", target_bir_lowering=False, num_devices=1)
    program(nc, arrays)
    r = run(nc, [arrays], core_ids=[0])
    return r.results[0]["out_x"]
```
